# Optimizing a Trainium2 kernel written in Bass

```python
import jax, jax.numpy as jnp
from jax import lax
import numpy as np

D_MODEL = 1024
BATCH = 1
SEQ = 512
DEPTH = 1

GRID_W = 64
CTX_LEN = 256

F_GROUP_DIM = 64
F_DIM = D_MODEL // 2
F_GROUPS = F_DIM // F_GROUP_DIM
SSM_HEAD_DIM = 64
D_SSM = 3 * D_MODEL // 2
SSM_HEADS = D_SSM // SSM_HEAD_DIM
SSM_GROUPS = 4
D_STATE = 128
CONV_K = 5
CHUNK = 128
D_MIX = F_DIM + D_SSM
CONV_DIM = D_SSM + 2 * SSM_GROUPS * D_STATE
D_IN_PROJ = F_DIM + D_SSM + CONV_DIM + 2 * SSM_HEADS

N_EXPERTS = 16
CAPACITY_FACTOR = 2
D_EXPERT = 2048
N_MOD = 6
EPS = 1e-6

kernel_name = 'hybrid_fnet_ssd_ecmoe_diffusion'

def rms_norm(x, w):
    xf = x.astype(jnp.float32)
    y = xf * lax.rsqrt(jnp.mean(xf * xf, axis=-1, keepdims=True) + EPS)
    return (y * w.astype(jnp.float32)).astype(x.dtype)

def modulate(h, shift, scale):
    return h * (1 + scale) + shift

def centred_dwconv(u, w, b):
    out = lax.conv_general_dilated(
        u, w[:, None, :].astype(u.dtype), window_strides=(1,),
        padding=[(CONV_K // 2, CONV_K // 2)],
        dimension_numbers=('NWC', 'WIO', 'NWC'),
        feature_group_count=u.shape[-1])
    return out + b

def mixer_inputs(h, w_in, conv_w, conv_b, dt_bias):
    bsz, L, _ = h.shape
    proj = h @ w_in
    u_f, z, xbc, dt_raw = jnp.split(proj, [F_DIM, F_DIM + D_SSM, F_DIM + D_SSM + CONV_DIM], axis=-1)
    xbc = jax.nn.silu(centred_dwconv(xbc, conv_w, conv_b))
    xs, bm, cm = jnp.split(xbc, [D_SSM, D_SSM + SSM_GROUPS * D_STATE], axis=-1)
    xs = xs.reshape(bsz, L, SSM_HEADS, SSM_HEAD_DIM)
    bm = bm.reshape(bsz, L, SSM_GROUPS, D_STATE)
    cm = cm.reshape(bsz, L, SSM_GROUPS, D_STATE)
    dt = jax.nn.softplus(dt_raw.astype(jnp.float32).reshape(bsz, L, 2, SSM_HEADS)
                         + dt_bias.astype(jnp.float32))
    return u_f, z, xs, bm, cm, dt[:, :, 0], dt[:, :, 1]

def ssd_chunked(xs, dt, a, bm, cm, h0, with_output):
    bsz, L, H, P = xs.shape
    G, N = bm.shape[2], bm.shape[3]
    HG = H // G
    nc = L // CHUNK
    xs = xs.astype(jnp.float32)
    bm = bm.astype(jnp.float32).reshape(bsz, nc, CHUNK, G, N)
    cm = cm.astype(jnp.float32).reshape(bsz, nc, CHUNK, G, N)
    xdt = (xs * dt[..., None]).reshape(bsz, nc, CHUNK, G, HG, P)
    a_cs = jnp.cumsum((dt * a).reshape(bsz, nc, CHUNK, G, HG), axis=2)
    to_end = jnp.exp(a_cs[:, :, -1:] - a_cs)
    states = jnp.einsum('bclgn,bclgh,bclghp->bcghpn', bm, to_end, xdt)
    chunk_decay = jnp.exp(a_cs[:, :, -1])

    def step(h, inp):
        st, dec = inp
        return dec[..., None, None] * h + st, h

    h_last, h_prev = lax.scan(step, h0.astype(jnp.float32).reshape(bsz, G, HG, P, N),
                              (jnp.moveaxis(states, 1, 0), jnp.moveaxis(chunk_decay, 1, 0)))
    h_last = h_last.reshape(bsz, H, P, N)
    if not with_output:
        return None, h_last
    h_prev = jnp.moveaxis(h_prev, 0, 1)
    lower = jnp.tril(jnp.ones((CHUNK, CHUNK), dtype=bool))
    seg = a_cs[:, :, :, None] - a_cs[:, :, None, :]
    decay = jnp.exp(jnp.where(lower[:, :, None, None], seg, -jnp.inf))
    cb = jnp.einsum('bclgn,bcsgn->bclsg', cm, bm)
    y_diag = jnp.einsum('bclsg,bclsgh,bcsghp->bclghp', cb, decay, xdt)
    y_off = jnp.einsum('bclgn,bcghpn,bclgh->bclghp', cm, h_prev, jnp.exp(a_cs))
    return (y_diag + y_off).reshape(bsz, L, H, P), h_last

def ssd_bidir(xs, bm, cm, dt_f, dt_b, a_log, h0_f, h0_b, with_output):
    a = -jnp.exp(a_log.astype(jnp.float32))
    flip = lambda t: jnp.flip(t, axis=1)
    y_f, h_f = ssd_chunked(xs, dt_f, a[0], bm, cm, h0_f, with_output)
    y_b, h_b = ssd_chunked(flip(xs), flip(dt_b), a[1], flip(bm), flip(cm), h0_b, with_output)
    y = y_f + flip(y_b) if with_output else None
    return y, h_f, h_b

def fourier_mix(u_f, w_fourier):
    bsz, L, _ = u_f.shape
    u = u_f.astype(jnp.float32).reshape(bsz, L, F_GROUPS, F_GROUP_DIM)
    spec = jnp.fft.fft2(u, axes=(1, 3), norm='ortho').real
    out = jnp.einsum('blgi,gij->blgj', spec, w_fourier.astype(jnp.float32))
    return out.reshape(bsz, L, F_DIM).astype(u_f.dtype)

def mixer_out(u_f, y_ssm, xs, z, d_skip, ssm_norm_w, w_fourier, w_out):
    bsz, L, _ = z.shape
    y = y_ssm + d_skip.astype(jnp.float32)[:, None] * xs.astype(jnp.float32)
    y = y.reshape(bsz, L, D_SSM) * jax.nn.silu(z.astype(jnp.float32))
    yg = y.reshape(bsz, L, SSM_GROUPS, D_SSM // SSM_GROUPS)
    yg = yg * lax.rsqrt(jnp.mean(yg * yg, axis=-1, keepdims=True) + EPS)
    y = (yg.reshape(bsz, L, D_SSM) * ssm_norm_w.astype(jnp.float32)).astype(z.dtype)
    return jnp.concatenate([fourier_mix(u_f, w_fourier), y], axis=-1) @ w_out

def ec_moe(h, w_router, w_gate, w_up, w_down):
    bsz, T, _ = h.shape
    cap = CAPACITY_FACTOR * T // N_EXPERTS
    probs = jax.nn.softmax((h @ w_router).astype(jnp.float32), axis=-1)
    vals, idx = lax.top_k(jnp.swapaxes(probs, 1, 2), cap)
    bidx = jnp.arange(bsz)[:, None, None]
    xg = h[bidx, idx]
    g = jnp.einsum('becd,edf->becf', xg, w_gate)
    u = jnp.einsum('becd,edf->becf', xg, w_up)
    y = jnp.einsum('becf,efd->becd', jax.nn.silu(g) * u, w_down) * vals[..., None].astype(h.dtype)
    return jnp.zeros_like(h).at[bidx, idx].add(y)

def setup_inputs(seed: int = 0) -> dict:
    key = jax.random.key(seed)
    ks = jax.random.split(key, 24)
    nrm = lambda k, shape, s: jax.random.normal(k, shape, jnp.float32) * s
    dt0 = jnp.exp(jax.random.uniform(ks[9], (DEPTH, 2, SSM_HEADS), jnp.float32,
                                     np.log(1e-3).astype(np.float32), np.log(1e-1).astype(np.float32)))
    return {
        'x': nrm(ks[0], (BATCH, SEQ, D_MODEL), 1.0),
        'c': nrm(ks[1], (BATCH, D_MODEL), 1.0),
        'ctx': nrm(ks[2], (BATCH, CTX_LEN, D_MODEL), 1.0),
        'c_ctx': nrm(ks[3], (D_MODEL,), 1.0),
        'w_ada': nrm(ks[4], (DEPTH, D_MODEL, N_MOD * D_MODEL), 0.5 * D_MODEL ** -0.5),
        'b_ada': nrm(ks[5], (DEPTH, N_MOD * D_MODEL), 0.02),
        'norm1_w': 1.0 + nrm(ks[6], (DEPTH, D_MODEL), 0.05),
        'w_in': nrm(ks[7], (DEPTH, D_MODEL, D_IN_PROJ), D_MODEL ** -0.5),
        'conv_w': nrm(ks[8], (DEPTH, CONV_K, CONV_DIM), CONV_K ** -0.5),
        'conv_b': nrm(ks[10], (DEPTH, CONV_DIM), 0.02),
        'dt_bias': dt0 + jnp.log(-jnp.expm1(-dt0)),
        'a_log': jnp.log(jax.random.uniform(ks[11], (DEPTH, 2, SSM_HEADS), jnp.float32, 1.0, 16.0)),
        'd_skip': 1.0 + nrm(ks[12], (DEPTH, SSM_HEADS), 0.1),
        'ssm_norm_w': 1.0 + nrm(ks[13], (DEPTH, D_SSM), 0.05),
        'w_fourier': nrm(ks[14], (DEPTH, F_GROUPS, F_GROUP_DIM, F_GROUP_DIM), F_GROUP_DIM ** -0.5),
        'w_out': nrm(ks[15], (DEPTH, D_MIX, D_MODEL), D_MIX ** -0.5),
        'norm2_w': 1.0 + nrm(ks[16], (DEPTH, D_MODEL), 0.05),
        'w_router': nrm(ks[17], (DEPTH, D_MODEL, N_EXPERTS), D_MODEL ** -0.5),
        'w_gate': nrm(ks[18], (DEPTH, N_EXPERTS, D_MODEL, D_EXPERT), D_MODEL ** -0.5),
        'w_up': nrm(ks[19], (DEPTH, N_EXPERTS, D_MODEL, D_EXPERT), D_MODEL ** -0.5),
        'w_down': nrm(ks[20], (DEPTH, N_EXPERTS, D_EXPERT, D_MODEL), D_EXPERT ** -0.5),
        'final_norm_w': 1.0 + nrm(ks[21], (D_MODEL,), 0.05),
    }

def reference(x, c, ctx, c_ctx, w_ada, b_ada, norm1_w, w_in, conv_w, conv_b, dt_bias, a_log,
              d_skip, ssm_norm_w, w_fourier, w_out, norm2_w, w_router, w_gate, w_up, w_down,
              final_norm_w):
    bsz = x.shape[0]
    for layer in range(DEPTH):
        last = layer == DEPTH - 1
        mod_l = (jax.nn.silu(c) @ w_ada[layer] + b_ada[layer]).reshape(bsz, N_MOD, 1, D_MODEL)
        mod_c = (jax.nn.silu(c_ctx) @ w_ada[layer] + b_ada[layer]).reshape(N_MOD, D_MODEL)
        sh1, sc1, g1, sh2, sc2, g2 = [mod_l[:, i] for i in range(N_MOD)]
        csh1, csc1, cg1, csh2, csc2, cg2 = [mod_c[i] for i in range(N_MOD)]

        h_c = modulate(rms_norm(ctx, norm1_w[layer]), csh1, csc1)
        u_fc, z_c, xs_c, bm_c, cm_c, dtf_c, dtb_c = mixer_inputs(
            h_c, w_in[layer], conv_w[layer], conv_b[layer], dt_bias[layer])
        zeros = jnp.zeros((bsz, SSM_HEADS, SSM_HEAD_DIM, D_STATE), jnp.float32)
        y_c, h_f, h_b = ssd_bidir(xs_c, bm_c, cm_c, dtf_c, dtb_c, a_log[layer], zeros, zeros, not last)

        h_l = modulate(rms_norm(x, norm1_w[layer]), sh1, sc1)
        u_fl, z_l, xs_l, bm_l, cm_l, dtf_l, dtb_l = mixer_inputs(
            h_l, w_in[layer], conv_w[layer], conv_b[layer], dt_bias[layer])
        y_l, _, _ = ssd_bidir(xs_l, bm_l, cm_l, dtf_l, dtb_l, a_log[layer], h_f, h_b, True)
        x = x + g1 * mixer_out(u_fl, y_l, xs_l, z_l, d_skip[layer], ssm_norm_w[layer],
                               w_fourier[layer], w_out[layer])
        if not last:
            ctx = ctx + cg1 * mixer_out(u_fc, y_c, xs_c, z_c, d_skip[layer], ssm_norm_w[layer],
                                        w_fourier[layer], w_out[layer])

        x = x + g2 * ec_moe(modulate(rms_norm(x, norm2_w[layer]), sh2, sc2),
                            w_router[layer], w_gate[layer], w_up[layer], w_down[layer])
        if not last:
            ctx = ctx + cg2 * ec_moe(modulate(rms_norm(ctx, norm2_w[layer]), csh2, csc2),
                                     w_router[layer], w_gate[layer], w_up[layer], w_down[layer])
    return rms_norm(x, final_norm_w)


_drawn_inputs = setup_inputs


def setup_inputs(seed=0):
    import zlib

    import numpy as np

    out = dict(_drawn_inputs(seed))
    spreads = {}
    factors = {'ctx': 4.797,
     'c_ctx': 4.332,
     'norm1_w': 2.706,
     'conv_b': 6.377,
     'd_skip': 24.224,
     'ssm_norm_w': 3.87,
     'norm2_w': 4.787}
    for name, (base, spread) in spreads.items():
        noise = np.random.default_rng([zlib.crc32(name.encode()), seed]).standard_normal(out[name].shape)
        drawn = base * np.exp(spread * noise) if base else spread * noise
        out[name] = __import__('jax').numpy.asarray(drawn.astype(out[name].dtype))
    for name, factor in factors.items():
        out[name] = (out[name] * factor).astype(out[name].dtype)
    return out
```

```python
from contextlib import ExitStack

import numpy as np

import concourse.bass as bass
from concourse import mybir

F32 = mybir.dt.float32
ALU = mybir.AluOpType
ACT = mybir.ActivationFunctionType
AX_X = mybir.AxisListType.X

P = 128
D = 1024
KT = D // P
SEQ, CTX = 512, 256
LT, CT = SEQ // P, CTX // P
TT = CT + LT
TOK = SEQ + CTX
F_DIM, F_GROUP = 512, 64
FT = F_DIM // P
HD = 64
D_SSM = 1536
HEADS = D_SSM // HD
GROUPS = 4
HG = HEADS // GROUPS
GW = HG * HD
XT = GW // P
YT = D_SSM // P
CONV = 5
CONV_TILES = (D_SSM + 2 * GROUPS * P) // P
COL_Z = F_DIM
COL_X = COL_Z + D_SSM
COL_B = COL_X + D_SSM
COL_C = COL_B + GROUPS * P
COL_DT = COL_C + GROUPS * P
EXPERTS, CAP, FE = 16, 64, 2048
EPS = 1e-6
MASKED = -1e30

PAD = CONV // 2
CONV_IN = TOK + 3 * PAD
CONV_OUT = TOK + PAD
LAT0 = CTX + PAD

ADA_W = 512
ADA_N = 6 * D // ADA_W
ADA_FIRST = 4
UNITS = GROUPS * LT
STEPS = CT + LT - 1
RING = 12
CHUNKS = 24
WO_SLOTS = 4


def host_constants():
    c = np.zeros((P, 6 * P + 8 + CAP), np.float32)
    i = np.arange(P)
    c[:, 0:P] = np.eye(P)
    c[:, P:2 * P] = i[:, None] <= i[None, :]
    c[:, 2 * P:3 * P] = i[:, None] >= i[None, :]
    c[:, 3 * P:4 * P] = 1.0
    angle = 2 * np.pi * ((np.arange(F_GROUP)[:, None] * np.arange(F_GROUP)[None, :]) % F_GROUP) / F_GROUP
    scale = 1.0 / np.sqrt(SEQ * F_GROUP)
    for b in range(2):
        s = slice(b * F_GROUP, (b + 1) * F_GROUP)
        c[s, 4 * P + b * F_GROUP:4 * P + (b + 1) * F_GROUP] = np.cos(angle) * scale
        c[s, 5 * P + b * F_GROUP:5 * P + (b + 1) * F_GROUP] = -np.sin(angle) * scale
    for j in range(4):
        for w in range(2):
            c[32 * j + w, 6 * P + 2 * j + w] = 1.0
    c[:, 6 * P + 8:] = np.arange(1, CAP + 1)
    t = np.arange(SEQ)
    seq = 2 * np.pi * ((t[:, None] * t[None, :]) % SEQ) / SEQ
    dft = np.stack([np.cos(seq), np.sin(seq)], 1).astype(np.float32).reshape(LT, P, 2 * SEQ)
    return c, dft


def bank_turns():
    used, turns = [0] * 8, {}

    def take(key, bank):
        turns[key] = (bank, used[bank])
        used[bank] += 1

    take("columns", 4)
    take("fourier_w", 7)
    for k in range(KT):
        take(("xT", k, 0), k % 2)
        take(("xT", k, 1), 2 + k % 2)
    take("ada_a", 6)
    take("mod_a", 4)
    take("dt", 5)
    for r in range(GROUPS + 1):
        g = r - 1
        for i in range(6):
            if r < GROUPS and i < 5:
                n = 5 * r + i
                take(("in", n, 0), n % 2)
                take(("in", n, 1), 2 + n % 2)
            elif r < GROUPS:
                for t in range(LT):
                    take(("z", r, t), t)
            elif i < FT:
                take(("u", i), i % 2)
            elif i == FT:
                for t in range(LT):
                    take(("v", t, 0), 2 * (t % 2))
                    take(("v", t, 1), 2 * (t % 2) + 1)
            else:
                for j in range(FT):
                    take(("f", j), j)
            if r == 0 and i == 0:
                take("ada_b", 6)
                take("ada_c", 5)
                take("mod_b", 4)
                take("cum", 5)
                take("tot", 6)
                take("rows", 7)
            if r < GROUPS and i in (1, 3, 4, 5):
                s = {1: 0, 3: 2, 4: 3, 5: 4}[i]
                take(("T", r, s, 0), 5)
                take(("T", r, s, 1), 6)
            if g >= 0:
                if i == 0:
                    if g > 0:
                        take(("y", 4 * g - 1), 7)
                    for k in range(STEPS):
                        take(("state", g, k, 0), 5)
                        take(("state", g, k, 1), 6)
                if i >= 3:
                    take(("y", 4 * g + i - 3), 7)
                if 2 <= i:
                    take(("diag", 4 * g + i - 2), 7)
                if 1 <= i <= 4:
                    v = 4 * g + i - 1
                    take(("cb", v), 4)
                    take(("off", v, 0), 5)
                    take(("off", v, 1), 6)
    take(("y", UNITS - 1), 7)
    for p in range(2):
        for t in range(2):
            for h in range(2):
                take(("out", 2 * p + t, h), 4 * p + 2 * t + h)
        if p == 0:
            continue
    take("route_bias", 0)
    for t in range(LT):
        take(("nT", t, 0), 1 + t % 2)
        take(("nT", t, 1), 3 + t % 2)
    take("logits", 5)
    take("probsT", 6)
    take("slotT", 7)
    return turns, used


def build(nc, consts, dft, x, c, ctx_tokens, c_ctx, w_ada, b_ada, norm1_w, w_in, conv_w, conv_b, dt_bias, a_log,
          d_skip, ssm_norm_w, w_fourier, w_out, norm2_w, w_router, w_gate, w_up, w_down, final_norm_w, out, stop=None):
    turns, uses = bank_turns()
    with ExitStack() as ctx:
        def sem(name):
            return ctx.enter_context(nc.semaphore(name))

        arena = ctx.enter_context(nc.sbuf_tensor("arena", [P, 53200], F32))
        bank = [ctx.enter_context(nc.psum_tensor(f"bank{b}", [P, 512], F32)) for b in range(8)]
        mod_dram = nc.dram_tensor("mod_rows_dram", (ADA_N, 4, P), F32, kind="Internal").ap()
        cum_dram = nc.dram_tensor("cum_rows_dram", (2 * HEADS, SEQ), F32, kind="Internal").ap()

        def at(offset, *shape):
            n = int(np.prod(shape))
            v = arena[:, offset:offset + n]
            if len(shape) == 2:
                return v.rearrange("p (a b) -> p a b", a=shape[0])
            if len(shape) == 3:
                return v.rearrange("p (a b c) -> p a b c", a=shape[0], b=shape[1])
            return v

        hT = at(0, KT, TOK)
        w_buf = [at(6144 + 3072 * s, 3072) for s in range(2)]
        conv_in = [at(12288 + CONV_IN * s, CONV_IN) for s in range(2)]
        conv_acc = [at(13836 + CONV_OUT * s, CONV_OUT) for s in range(2)]
        bc_ch = [[at(15376 + (2 * s + j) * CONV_OUT, CONV_OUT) for j in range(2)] for s in range(2)]
        tok = [at(18456 + 3072 * s, TT, 512) for s in range(2)]
        ada_rows_b = at(21528, ADA_N * P)
        yT = at(24600, YT, SEQ)
        x_raw = at(24600, TT, D)
        fT = at(30744, FT, SEQ)
        rows_raw = at(30744, 2 * P)
        small_w = at(31000, FT * F_GROUP)
        zs = [at(32792 + 1536 * s, LT, GW) for s in range(2)]
        ada_buf = [at(32792 + 4096 * s, KT, ADA_W) for s in range(3)]
        hp = [at(35864 + 1536 * d, LT, GW) for d in range(2)]
        seg = [at(38936 + 1536 * s, 2, HG, P) for s in range(2)]
        xdt = [at(42008 + 768 * s, 2, GW) for s in range(2)]
        xd = [at(43544 + 384 * s, GW) for s in range(2)]
        yb = [at(44312 + 768 * s, 2, GW) for s in range(2)]
        uT = at(45848, FT, SEQ)
        mod_rows = at(45848, ADA_N * P)
        xw = at(47896, 2, 2, GW)
        st_tmp = at(49432, 2, GW)
        vf = at(0, LT, FT, 2 * P)
        dft_buf = [at(4096 + 1024 * s, 2, SEQ) for s in range(2)]
        wo_buf = [at(32792 + D * s, D) for s in range(WO_SLOTS)]
        x1 = at(36888, LT, D)
        rowbc = {n: at(40984 + D * i, D) for i, n in enumerate(("shift2", "scale2", "gate1", "gate2"))}
        norm2_bc = at(48152, D)
        out_tmp = at(49176, 2, 512)
        ring = [at(2048 * s, 2048) for s in range(RING)]
        h2 = at(45080, LT, D)
        nT = [at(28696 + D * s, KT, P) for s in range(2)]
        small = 31000
        lg = at(small, LT, EXPERTS)
        probs = at(small + 64, LT, EXPERTS)
        slotT = at(small + 128, LT, EXPERTS)
        rowmax = at(small + 192, LT)
        rowsum = at(small + 196, LT)
        route_bias = at(small + 200, EXPERTS)
        pT = at(small + 216, SEQ)
        top8 = at(small + 728, 8)
        mask = at(32792, SEQ)
        cums = at(32792 + 512, SEQ)
        slot1 = at(32792 + 1024, SEQ)
        sel = at(28696, LT, CAP)
        sel_w = at(28952, LT, 2, CAP)
        scatter = at(29464, SEQ)
        xgT = at(29976, KT, CAP)
        silu_g = at(32792, 1024)
        act_e = at(33816, 1024)
        actT = at(34840, 1024)
        y_e = at(35864, 1024)
        moe = at(24600, LT, D)
        gate2 = rowbc["gate2"]
        final_bc = at(40984, D)

        s0 = [50200]

        def keep(*shape):
            o = s0[0]
            s0[0] += int(np.prod(shape))
            return at(o, *shape)

        cst = keep(6 * P + 8 + CAP)
        ident, tri_f, tri_b, ones = (cst[:, P * i:P * (i + 1)] for i in range(4))
        dft_c, dft_s = cst[:, 4 * P:5 * P], cst[:, 5 * P:6 * P]
        sel8, iota1 = cst[:, 6 * P:6 * P + 8], cst[:, 6 * P + 8:6 * P + 8 + CAP]
        cols_a = keep(64)
        cols_b = keep(CONV * CONV_TILES)
        n1w, cb_col, ssm_col, n2w = cols_a[:, 0:8], cols_a[:, 8:28], cols_a[:, 28:40], cols_a[:, 40:48]
        scT = keep(16)
        modc = keep(ADA_N * 4, 2)
        a1 = keep(8, 2)
        stat = keep(32)
        abc, dtb, dbc = keep(48), keep(48), keep(24)
        cum = keep(TT, 48)
        dt = keep(TT, 48)
        ecum = keep(TT, 48)
        toend = keep(TT, 48)
        decay = keep(TT, 48)
        router_w = keep(KT, EXPERTS)
        scaled_router = keep(KT, EXPERTS)
        assert s0[0] <= 53200, s0[0]
        w_dt = at(21528 + 1536, KT, 48)
        dtmp = [at(49176 + 288 * i, TT, 48) for i in range(3)]
        cum_rows = at(49176, SEQ)
        fw = at(30744 + 1024, FT, 2 * P)

        bank_full = [sem(f"bank_full{b}") for b in range(8)]
        bank_free = [sem(f"bank_free{b}") for b in range(8)]
        small_in, ctx_in, lat_in, w_dt_in = sem("small_in"), sem("ctx_in"), sem("lat_in"), sem("w_dt_in")
        ada_in = [sem(f"ada_in{s}") for s in range(3)]
        ada_used = sem("ada_used")
        ada_b_in = sem("ada_b_in")
        w_in_sem = [sem(f"w_in{s}") for s in range(2)]
        pads_zero = sem("pads_zero")
        seg_in = [sem(f"seg_in{s}") for s in range(2)]
        dft_in = [sem(f"dft_in{s}") for s in range(2)]
        dft_used = sem("dft_used")
        mod_out, mod_bc_in, cum_out = sem("mod_out"), sem("mod_bc_in"), sem("cum_out")
        dve, act_s, pool = sem("dve_step"), sem("act_step"), sem("pool_step")
        square_done, xn_done = sem("square_done"), sem("xn_done")
        rstd_x, rstd_y, rstd_x1, rstd_x2 = sem("rstd_x"), sem("rstd_y"), sem("rstd_x1"), sem("rstd_x2")
        silu_c, hmod, zeroed = sem("silu_c"), sem("hmod"), sem("zeroed")
        dt_ready, cum_ready, rows_ready = sem("dt_ready"), sem("cum_ready"), sem("rows_ready")
        exp_small, small_exped = sem("exp_small"), sem("small_exped")
        conv_done, tile_done = sem("conv_done"), sem("tile_done")
        xw_ready, state_ready, xdt_ready = sem("xw_ready"), sem("state_ready"), sem("xdt_ready")
        seg_ready, masked, decays = sem("seg_ready"), sem("masked"), sem("decays")
        offs_summed, gated, squared, y_ready = sem("offs_summed"), sem("gated"), sem("squared"), sem("y_ready")
        wo_in = [sem(f"wo_in{s}") for s in range(WO_SLOTS)]
        wo_used, res_in, x1_ready = sem("wo_used"), sem("res_in"), sem("x1_ready")
        x1_squared, n2_ready, h2_ready = sem("x1_squared"), sem("n2_ready"), sem("h2_ready")
        mod_bc_ready, router_in, router_scaled = sem("mod_bc_ready"), sem("router_in"), sem("router_scaled")
        shifted, exped, probs_ready, slots_ready = sem("shifted"), sem("exped"), sem("probs_ready"), sem("slots_ready")
        ring_in = [sem(f"ring_in{s}") for s in range(RING)]
        ring_used = sem("ring_used")
        e_full = [sem(f"expert_full{b}") for b in range(8)]
        e_free = [sem(f"expert_free{b}") for b in range(8)]
        sel_ready, selw_ready, silu_ready, act_ready = (sem(n) for n in ("sel_ready", "selw_ready", "silu_ready",
                                                                       "act_ready"))
        moe_zero, final_in = sem("moe_zero"), sem("final_in")
        x2_ready, x2_squared, out_ready, out_done = (sem(n) for n in ("x2_ready", "x2_squared", "out_ready",
                                                                      "out_done"))

        def filled(eng, key):
            b, n = turns[key]
            eng.wait_ge(bank_full[b], n + 1)
            return bank[b]

        def emptied(eng, key):
            b, n = turns[key]
            eng.wait_ge(bank_free[b], n + 1)

        def claim(pe, key):
            b, n = turns[key]
            if n:
                pe.wait_ge(bank_free[b], n)
            return bank[b]

        def full(ins, key):
            ins.then_inc(bank_full[turns[key][0]], 1)

        def free(ins, key):
            ins.then_inc(bank_free[turns[key][0]], 1)

        class Chain:

            def __init__(self, eng, s):
                self.eng, self.s, self.n = eng, s, 0

            def __call__(self, ins):
                self.n += 1
                ins.then_inc(self.s, 1)
                self.eng.wait_ge(self.s, self.n)

        def bc(v, *shape):
            return v.to_broadcast(list((P,) + shape))

        def ada_piece_used(eng, i):
            key = ("ada_a", "ada_b", "ada_c")[i // 4]
            if i % 4 == 3:
                filled(eng, key)
            else:
                eng.wait_ge(ada_used, i + 1 - (i + 1) // 4)

        def weights_used(eng, q):
            r, part = divmod(q, 3)
            if r == GROUPS:
                filled(eng, ("u", 2 * part + 1))
            else:
                filled(eng, (("in", 5 * r + 1, 1), ("in", 5 * r + 4, 1), ("z", r, LT - 1))[part])

        def chunk_used(eng, e, ch):
            if ch == 14:
                eng.wait_ge(e_full[1], e * 2 + 1)
            elif ch == 15:
                eng.wait_ge(e_full[3], e * 2 + 1)
            elif ch == 23:
                eng.wait_ge(e_full[5], e * 2 + 2)
            else:
                eng.wait_ge(ring_used, e * (CHUNKS - 3) + (ch + 1 if ch < 14 else ch - 1))

        def head_bc(v, width=HD):
            return v.unsqueeze(2).to_broadcast([P, HG, width])

        def heads(v):
            return v.rearrange("p (h c) -> p h c", h=HG)

        def lat_ctx(v):
            return v[:, LAT0:LAT0 + SEQ], v[:, 0:CTX]

        def chan(v, t):
            o = P * t if t < CT else LAT0 + P * (t - CT)
            return v[:, o:o + P]

        STEP_TILE = [[0, 1, 2, 3, 4], [1, 0, 5, 4, 3]]
        TILE_OF = lambda r, i: (12 + r, 16 + r, 3 * r, 3 * r + 1, 3 * r + 2)[i]
        SMALL_N = 16 * 13

        block = ctx.enter_context(nc.Block())

        @block.sync
        def _(sp):
            sp.dma_start(x_raw[:, 0:CT, :], ctx_tokens[0].rearrange("(t p) d -> p t d", p=P)).then_inc(ctx_in, 16)
            sp.dma_start(x_raw[:, CT:TT, :], x[0].rearrange("(t p) d -> p t d", p=P)).then_inc(lat_in, 16)
            sp.dma_start(w_dt, w_in[0, :, COL_DT:].rearrange("(k p) c -> p k c", p=P)).then_inc(w_dt_in, 16)

            def load_ada(i):
                if i >= 3:
                    ada_piece_used(sp, i - 3)
                sp.dma_start(ada_buf[i % 3], w_ada[0, :, ADA_W * i:ADA_W * (i + 1)].rearrange("(k p) c -> p k c", p=P)
                             ).then_inc(ada_in[i % 3], 16)

            def load_w(q):
                r, part = divmod(q, 3)
                if q >= 2:
                    weights_used(sp, q - 2)
                dst = w_buf[q % 2]
                if r == GROUPS:
                    cols = [(256 * part, 256, 0)]
                    width = 256
                elif part == 0:
                    cols, width = [(COL_B + P * r, P, 0), (COL_C + P * r, P, P)], 256
                elif part == 1:
                    cols, width = [(COL_X + GW * r, GW, 0)], GW
                else:
                    cols, width = [(COL_Z + GW * r, GW, 0)], GW
                v = dst[:, 0:KT * width].rearrange("p (k c) -> p k c", k=KT)
                for col, n, o in cols:
                    sp.dma_start(v[:, :, o:o + n], w_in[0, :, col:col + n].rearrange("(k p) c -> p k c", p=P)
                                 ).then_inc(w_in_sem[q % 2], 16)

            for i in range(ADA_FIRST):
                load_ada(i)
            load_w(0)
            load_w(1)
            for i in range(ADA_FIRST, ADA_N):
                load_ada(i)
            emptied(sp, "ada_c")
            emptied(sp, "ada_b")
            sp.dma_start(mod_dram[4:12].rearrange("m j c -> j m c"),
                         mod_rows[0:P:32, 4 * P:12 * P].rearrange("p (m c) -> p m c", c=P)).then_inc(mod_out, 16)
            sp.wait_ge(rows_ready, 1)
            sp.dma_start(cum_dram, cum_rows[0:48, :]).then_inc(cum_out, 16)
            sp.wait_ge(cum_out, 16)
            q = 2
            for v in range(UNITS):
                g, ch = divmod(v, LT)
                while v == 0 and q < 4:
                    load_w(q)
                    q += 1
                if v >= 2:
                    filled(sp, ("diag", v - 2))
                for d in range(2):
                    src = cum_dram[HEADS * d + HG * g:HEADS * d + HG * (g + 1), P * ch:P * (ch + 1)]
                    sp.dma_start(seg[v % 2][:, d], src.partition_broadcast(P)).then_inc(seg_in[v % 2], 16)
                while q < min(3 * (g + 1) + 1 + ch, 3 * GROUPS + 2):
                    load_w(q)
                    q += 1
            for t in range(LT):
                if t == 0:
                    emptied(sp, ("u", FT - 1))
                if t >= 2:
                    sp.wait_ge(dft_used, t - 1)
                sp.dma_start(dft_buf[t % 2], dft[t].rearrange("p (s l) -> p s l", s=2)).then_inc(dft_in[t % 2], 16)

            def load_chunk(e, ch):
                dst = ring[ch % RING]
                if ch < 16:
                    src = (w_gate if ch % 2 == 0 else w_up)[0, bass.ds(e, 1), P * (ch // 2):P * (ch // 2 + 1), :]
                    sp.dma_start(dst, src.rearrange("a p f -> p (a f)")).then_inc(ring_in[ch % RING], 16)
                else:
                    j = ch - 16
                    src = w_down[0, bass.ds(e, 1)].rearrange("a (h j p) d -> j p (a h) d", h=2, p=P)[j]
                    sp.dma_start(dst.rearrange("p (h d) -> p h d", h=2), src).then_inc(ring_in[ch % RING], 16)

            filled(sp, ("y", UNITS - 1))
            emptied(sp, ("f", FT - 1))
            for n in range(2 * 16):
                m = n - WO_SLOTS
                if m >= 0 and m % 16 == 15:
                    filled(sp, ("out", 2 * (m // 16) + 1, 1))
                elif m >= 0:
                    sp.wait_ge(wo_used, m + 1 - m // 16)
                k = n % 16
                sp.dma_start(wo_buf[n % WO_SLOTS], w_out[0, P * k:P * (k + 1), :]).then_inc(wo_in[n % WO_SLOTS], 16)
                if n == 3:
                    sp.dma_start(x1, x[0].rearrange("(t p) d -> p t d", p=P)).then_inc(res_in, 16)
                    sp.dma_start(router_w, w_router[0].rearrange("(k p) e -> p k e", p=P)).then_inc(router_in, 16)
                    sp.wait_ge(mod_out, 16)
                    for i, (name, m) in enumerate((("shift2", 3), ("scale2", 4), ("gate1", 2), ("gate2", 5))):
                        src = mod_dram[2 * m:2 * m + 2].rearrange("m j c -> (m j c)")
                        sp.dma_start(rowbc[name], src.partition_broadcast(P)).then_inc(mod_bc_in, 16)
                    sp.dma_start(norm2_bc, norm2_w[0].partition_broadcast(P)).then_inc(mod_bc_in, 16)
                if WO_SLOTS <= n < WO_SLOTS + RING:
                    load_chunk(0, n - WO_SLOTS)
            with sp.Fori(0, EXPERTS - 1) as e:
                for ch in range(RING, CHUNKS):
                    if ch != 16:
                        chunk_used(sp, e, ch - RING + (ch == 15))
                    load_chunk(e, ch)
                for ch in range(RING):
                    chunk_used(sp, e, ch + CHUNKS - RING)
                    load_chunk(e + 1, ch)
            for ch in range(RING, CHUNKS):
                chunk_used(sp, EXPERTS - 1, ch - RING)
                load_chunk(EXPERTS - 1, ch)
            sp.dma_start(final_bc, final_norm_w.partition_broadcast(P)).then_inc(final_in, 16)
            for t in range(LT):
                sp.wait_ge(out_ready, t + 1)
                sp.dma_start(out[0, P * t:P * (t + 1), :], moe[:, t]).then_inc(out_done, 16)
            sp.wait_ge(out_done, 16 * LT)

        @block.tensor
        def _(pe):
            mm, tr = pe.matmul, pe.transpose

            pe.wait_ge(small_in, SMALL_N)
            b = claim(pe, "columns")
            tr(b[:, 0:64], rows_raw[0:64, 0:P], ident[0:64, 0:64])
            full(tr(b[:, 64:164], rows_raw[0:100, P:2 * P], ident[0:100, 0:100]), "columns")
            b = claim(pe, "fourier_w")
            mm(b[:, 0:256], dft_c, small_w, start=True, stop=True)
            full(mm(b[:, 256:512], dft_s, small_w, start=True, stop=True), "fourier_w")
            pe.wait_ge(xn_done, TT)
            for k in range(KT):
                for part, (t0, n) in enumerate(((CT, LT), (0, CT))):
                    b = claim(pe, ("xT", k, part))
                    for t in range(n):
                        ins = tr(b[:, P * t:P * (t + 1)], x_raw[:, t0 + t, P * k:P * (k + 1)], ident)
                    full(ins, ("xT", k, part))

            def ada_piece(i, key, col, last):
                pe.wait_ge(ada_in[i % 3], 16 * (i // 3 + 1))
                b = bank[turns[key][0]]
                for k in range(KT):
                    for j in range(4):
                        ins = mm(b[32 * j:32 * j + 2, col:col + P], scT[:, k:k + 9:8],
                                 ada_buf[i % 3][:, k, P * j:P * (j + 1)], start=(k == 0), stop=(k == KT - 1),
                                 skip_group_check=True)
                full(ins, key) if last else ins.then_inc(ada_used, 1)

            def ada(key, first, n):
                claim(pe, key)
                for i in range(first, first + n):
                    ada_piece(i, key, P * (i - first), i == first + n - 1)

            def mod_columns(key, first, n):
                b = claim(pe, key)
                for i in range(n):
                    ins = mm(b[:, 8 * i:8 * i + 8], mod_rows[:, P * (first + i):P * (first + i + 1)], sel8,
                             start=True, stop=True)
                full(ins, key)

            pe.wait_ge(silu_c, 1)
            ada("ada_a", 0, ADA_FIRST)
            emptied(pe, "ada_a")
            mod_columns("mod_a", 0, ADA_FIRST)
            pe.wait_ge(w_dt_in, 16)
            pe.wait_ge(hmod, 2 * KT)
            b = claim(pe, "dt")
            for t in range(TT):
                for k in range(KT):
                    ins = mm(b[:, 48 * t:48 * (t + 1)], hT[:, k, P * t:P * (t + 1)], w_dt[:, k], start=(k == 0),
                             stop=(k == KT - 1))
            full(ins, "dt")

            def w_view(q, width):
                return w_buf[q % 2][:, 0:KT * width].rearrange("p (k c) -> p k c", k=KT)

            def w_wait(q):
                n = sum(32 if (p % 3 == 0 and p < 3 * GROUPS) else 16 for p in range(q % 2, q + 1, 2))
                pe.wait_ge(w_in_sem[q % 2], n)

            def project_channels(r, i):
                n = 5 * r + i
                q, width, col = (3 * r, 256, P * i) if i < 2 else (3 * r + 1, GW, P * (i - 2))
                w_wait(q)
                lat, cx = claim(pe, ("in", n, 0)), claim(pe, ("in", n, 1))
                w = w_view(q, width)
                for k in range(KT):
                    a = mm(lat[:], w[:, k, col:col + P], hT[:, k, CTX:TOK], start=(k == 0), stop=(k == KT - 1))
                    if k == KT - 1:
                        full(a, ("in", n, 0))
                for k in range(KT):
                    a = mm(cx[:, 0:CTX], w[:, k, col:col + P], hT[:, k, 0:CTX], start=(k == 0), stop=(k == KT - 1))
                full(a, ("in", n, 1))

            def project_z(r):
                q = 3 * r + 2
                w_wait(q)
                w = w_view(q, GW)
                for t in range(LT):
                    b = claim(pe, ("z", r, t))
                    for k in range(KT):
                        a = mm(b[:, 0:GW], hT[:, k, CTX + P * t:CTX + P * (t + 1)], w[:, k], start=(k == 0),
                               stop=(k == KT - 1))
                    full(a, ("z", r, t))

            def project_u(i):
                q = 3 * GROUPS + i // 2
                w_wait(q)
                w = w_view(q, 256)
                b = claim(pe, ("u", i))
                for k in range(KT):
                    a = mm(b[:], w[:, k, P * (i % 2):P * (i % 2 + 1)], hT[:, k, CTX:TOK], start=(k == 0),
                           stop=(k == KT - 1))
                full(a, ("u", i))

            def channel_dft():
                emptied(pe, ("u", FT - 1))
                emptied(pe, ("u", FT - 2))
                emptied(pe, "fourier_w")
                for t in range(LT):
                    for j in range(FT):
                        key = ("v", t, j // 2)
                        if j % 2 == 0:
                            b = claim(pe, key)
                        a = mm(b[:, 256 * (j % 2):256 * (j % 2 + 1)], uT[:, j, P * t:P * (t + 1)], fw[:, j],
                               start=True, stop=True)
                        if j % 2:
                            full(a, key)

            def position_dft():
                for t in range(LT):
                    for h in range(2):
                        emptied(pe, ("v", t, h))
                bs = [claim(pe, ("f", j)) for j in range(FT)]
                for t in range(LT):
                    pe.wait_ge(dft_in[t % 2], 16 * (t // 2 + 1))
                    for j in range(FT):
                        for s in range(2):
                            a = mm(bs[j][:], vf[:, t, j, P * s:P * (s + 1)], dft_buf[t % 2][:, s],
                                   start=(t == 0 and s == 0), stop=(t == LT - 1 and s == 1))
                        if t == LT - 1:
                            full(a, ("f", j))
                        elif j == FT - 1:
                            a.then_inc(dft_used, 1)

            def to_tokens(r, s):
                n = 5 * r + s
                src = bc_ch[r % 2][0] if s == 0 else conv_acc[n % 2]
                pe.wait_ge(tile_done, n + 1)
                for part, (t0, m) in enumerate(((CT, LT), (0, CT))):
                    b = claim(pe, ("T", r, s, part))
                    for t in range(m):
                        a = tr(b[:, P * t:P * (t + 1)], chan(src, t0 + t), ident)
                    full(a, ("T", r, s, part))

            def states(g):
                for s in (0, 2, 3, 4):
                    emptied(pe, ("T", g, s, 0))
                    emptied(pe, ("T", g, s, 1))
                for k in range(STEPS):
                    pe.wait_ge(xw_ready, STEPS * g + k + 1)
                    for d in range(2):
                        b = claim(pe, ("state", g, k, d))
                        full(mm(b[:, 0:GW], tok[g % 2][:, STEP_TILE[d][k], 0:P], xw[:, k % 2, d], start=True,
                                stop=True), ("state", g, k, d))

            def unit_pre(v):
                g, ch = divmod(v, LT)
                bm, cm = (chan(bc_ch[g % 2][j], CT + ch) for j in range(2))
                pe.wait_ge(tile_done, 5 * g + 2)
                b = claim(pe, ("cb", v))
                full(mm(b[:, 0:P], bm, cm, start=True, stop=True), ("cb", v))
                pe.wait_ge(state_ready, STEPS * (g + 1))
                for d in range(2):
                    b = claim(pe, ("off", v, d))
                    full(mm(b[:, 0:GW], cm, hp[d][:, ch if d == 0 else LT - 1 - ch], start=True, stop=True),
                         ("off", v, d))

            def unit_post(v):
                emptied(pe, ("cb", v))
                pe.wait_ge(xdt_ready, v + 1)
                b = claim(pe, ("diag", v))
                for h in range(HG):
                    for d in range(2):
                        a = mm(b[:, HD * h:HD * (h + 1)], seg[v % 2][:, d, h], xdt[v % 2][:, d, HD * h:HD * (h + 1)],
                               start=(d == 0), stop=(d == 1))
                full(a, ("diag", v))

            def unit_fin(v):
                pe.wait_ge(y_ready, v + 1)
                b = claim(pe, ("y", v))
                for j in range(XT):
                    a = tr(b[:, P * j:P * (j + 1)], yb[v % 2][:, 0, P * j:P * (j + 1)], ident)
                full(a, ("y", v))

            for r in range(GROUPS + 1):
                g = r - 1
                for i in range(6):
                    if r < GROUPS:
                        project_channels(r, i) if i < 5 else project_z(r)
                    elif i < FT:
                        project_u(i)
                    elif i == FT:
                        channel_dft()
                    else:
                        position_dft()
                    if r == 0 and i == 0:
                        ada("ada_b", 4, 4)
                        ada("ada_c", 8, 4)
                        emptied(pe, "ada_b")
                        emptied(pe, "ada_c")
                        mod_columns("mod_b", 4, 8)
                        pe.wait_ge(dt_ready, 1)
                        b = claim(pe, "cum")
                        bv = b[:, 0:TT * 48].rearrange("p (t h) -> p t h", t=TT)
                        mm(bv[:, :, 0:24], tri_f, dtmp[0][:, :, 0:24], start=True, stop=True)
                        full(mm(bv[:, :, 24:48], tri_b, dtmp[0][:, :, 24:48], start=True, stop=True), "cum")
                        b = claim(pe, "tot")
                        full(mm(b[:, 0:TT * 48].rearrange("p (t h) -> p t h", t=TT), ones, dtmp[0], start=True,
                                stop=True), "tot")
                        emptied(pe, "cum")
                        b = claim(pe, "rows")
                        for t in range(LT):
                            a = tr(b[0:48, P * t:P * (t + 1)], cum[:, CT + t], ident)
                        full(a, "rows")
                    if r < GROUPS and i in (1, 3, 4, 5):
                        to_tokens(r, {1: 0, 3: 2, 4: 3, 5: 4}[i])
                    if g >= 0:
                        if i == 0:
                            if g > 0:
                                unit_fin(4 * g - 1)
                            states(g)
                        if i >= 3:
                            unit_fin(4 * g + i - 3)
                        if i >= 2:
                            unit_post(4 * g + i - 2)
                        if 1 <= i <= 4:
                            unit_pre(4 * g + i - 1)
            unit_fin(UNITS - 1)

            for j in range(FT):
                emptied(pe, ("f", j))
            for v in range(UNITS):
                emptied(pe, ("y", v))
            for p in range(2):
                bs = {(t, h): claim(pe, ("out", t, h)) for t in (2 * p, 2 * p + 1) for h in range(2)}
                for k in range(16):
                    n = 16 * p + k
                    pe.wait_ge(wo_in[n % WO_SLOTS], 16 * (n // WO_SLOTS + 1))
                    for t in (2 * p, 2 * p + 1):
                        lhs = fT[:, k, P * t:P * (t + 1)] if k < FT else yT[:, k - FT, P * t:P * (t + 1)]
                        for h in range(2):
                            a = mm(bs[t, h][:], lhs, wo_buf[n % WO_SLOTS][:, 512 * h:512 * (h + 1)], start=(k == 0),
                                   stop=(k == 15))
                            if k == 15:
                                full(a, ("out", t, h))
                    if k < 15:
                        a.then_inc(wo_used, 1)
            pe.wait_ge(router_scaled, 1)
            b = claim(pe, "route_bias")
            for k in range(KT):
                a = mm(b[:, 0:EXPERTS], modc[:, 24 + k, 0:1].to_broadcast([P, P]), router_w[:, k], start=(k == 0),
                       stop=(k == KT - 1))
            full(a, "route_bias")
            lgb = claim(pe, "logits")
            for t in range(LT):
                pe.wait_ge(n2_ready, t + 1)
                for h in range(2):
                    b = claim(pe, ("nT", t, h))
                    for k in range(4):
                        a = tr(b[:, P * k:P * (k + 1)], h2[:, t, P * (4 * h + k):P * (4 * h + k + 1)], ident)
                    full(a, ("nT", t, h))
                for h in range(2):
                    emptied(pe, ("nT", t, h))
                for k in range(KT):
                    a = mm(lgb[:, EXPERTS * t:EXPERTS * (t + 1)], nT[t % 2][:, k], scaled_router[:, k],
                           start=(k == 0), stop=(k == KT - 1))
            full(a, "logits")
            pe.wait_ge(probs_ready, 1)
            b = claim(pe, "probsT")
            for t in range(LT):
                a = tr(b[0:EXPERTS, P * t:P * (t + 1)], probs[:, t], ident)
            full(a, "probsT")
            pe.wait_ge(slots_ready, 1)
            b = claim(pe, "slotT")
            for t in range(LT):
                a = tr(b[:, EXPERTS * t:EXPERTS * (t + 1)], slot1[0:EXPERTS, P * t:P * (t + 1)],
                       ident[0:EXPERTS, 0:EXPERTS])
            full(a, "slotT")
            pe.wait_ge(h2_ready, LT)
            with pe.Fori(0, EXPERTS) as e:
                pe.wait_ge(sel_ready, e + 1)
                pe.wait_ge(e_free[4], 2 * e + 1)
                for k in range(KT):
                    for t in range(LT):
                        a = mm(bank[4][:, CAP * k:CAP * (k + 1)], h2[:, t, P * k:P * (k + 1)], sel[:, t],
                               start=(t == 0), stop=(t == LT - 1))
                a.then_inc(e_full[4], 1)
                pe.wait_ge(selw_ready, e + 1)
                pe.wait_ge(e_free[5], 2 * e + 1)
                for t in range(LT):
                    a = tr(bank[5][:, P * t:P * (t + 1)], sel_w[:, t].rearrange("p a b -> p (a b)"), ident)
                a.then_inc(e_full[5], 1)
                pe.wait_ge(e_free[4], 2 * e + 2)
                for b in range(4):
                    pe.wait_ge(e_free[b], e + 1)
                for ch in range(16):
                    k, which = divmod(ch, 2)
                    pe.wait_ge(ring_in[ch % RING], (e * 2 + (ch // RING + 1)) * 16)
                    for n in range(2):
                        for h in range(2):
                            a = mm(bank[2 * which + n][CAP * h:CAP * (h + 1), :], xgT[:, k],
                                   ring[ch % RING][:, 1024 * h + 512 * n:1024 * h + 512 * (n + 1)], start=(k == 0),
                                   stop=(k == KT - 1), skip_group_check=True)
                    if k < KT - 1:
                        a.then_inc(ring_used, 1)
                    else:
                        a.then_inc(e_full[2 * which + 1], 1)
                for n in range(2):
                    pe.wait_ge(act_ready, 2 * e + n + 1)
                    pe.wait_ge(e_free[6 + n], 3 * e + 1)
                    for j in range(4):
                        a = tr(bank[6 + n][:, P * j:P * (j + 1)], act_e[:, 512 * n + P * j:512 * n + P * (j + 1)],
                               ident)
                    a.then_inc(e_full[6 + n], 1)
                pe.wait_ge(e_free[5], 2 * e + 2)
                for j in range(8):
                    ch = 16 + j
                    pe.wait_ge(ring_in[ch % RING], (e * 2 + 2) * 16)
                    if j % 4 == 0:
                        pe.wait_ge(e_free[6 + j // 4], 3 * e + 2)
                    for n in range(2):
                        for h in range(2):
                            a = mm(bank[4 + n][CAP * h:CAP * (h + 1), :],
                                   actT[:, P * j + CAP * h:P * j + CAP * (h + 1)],
                                   ring[ch % RING][:, D * h + 512 * n:D * h + 512 * (n + 1)], start=(j == 0),
                                   stop=(j == 7), skip_group_check=True)
                    if j < 7:
                        a.then_inc(ring_used, 1)
                    else:
                        a.then_inc(e_full[5], 1)
                for n in range(2):
                    pe.wait_ge(e_free[4 + n], 2 * e + 3)
                for i in range(8):
                    t, n = divmod(i, 2)
                    b = (6, 7, 0, 1, 2, 3, 6, 7)[i]
                    if b >= 6:
                        pe.wait_ge(e_free[b], 3 * e + 2 + i // 6)
                    mm(bank[b][:], scatter[:, P * t:P * (t + 1)], y_e[:, 512 * n:512 * (n + 1)], start=True,
                       stop=True).then_inc(e_full[b], 1)

        @block.vector
        def _(v_):
            v = v_
            step = Chain(v, dve)
            tt, ts, stt, cp = v.tensor_tensor, v.tensor_scalar, v.scalar_tensor_tensor, v.tensor_copy

            step(v.memset(mod_rows, 0.0))
            for s in range(2):
                for o in (0, LAT0, CONV_IN - PAD):
                    step(v.memset(conv_in[s][:, o:o + PAD], 0.0))
            v.memset(fw, 0.0).then_inc(pads_zero, 1)
            v.wait_ge(pads_zero, 1)
            for t in range(TT):
                v.wait_ge(rstd_x, t + 1)
                ts(x_raw[:, t], x_raw[:, t], stat[:, t:t + 1], None, ALU.mult).then_inc(xn_done, 1)
            b = filled(v, "columns")
            cp(cols_a, b[:, 0:64])
            free(cp(cols_b, b[:, 64:164]), "columns")
            b = filled(v, "fourier_w")
            for s in range(2):
                for h in range(2):
                    src = b[CAP * h:CAP * (h + 1), 256 * s:256 * (s + 1)].rearrange("p (j c) -> p j c", j=FT)
                    ins = cp(fw[CAP * h:CAP * (h + 1), :, P * s + F_GROUP * h:P * s + F_GROUP * (h + 1)], src)
            free(ins, "fourier_w")
            for k in range(KT):
                b = filled(v, ("xT", k, 1))
                free(cp(hT[:, k, 0:CTX], b[:, 0:CTX]), ("xT", k, 1))

            def mod_evac(key, first, n):
                b = filled(v, key)
                for j in range(4):
                    q = slice(32 * j, 32 * j + 2)
                    ins = tt(mod_rows[q, P * first:P * (first + n)], b[q, 0:P * n],
                             ada_rows_b[q, P * first:P * (first + n)], ALU.add)
                free(ins, key)

            v.wait_ge(ada_b_in, 32)
            mod_evac("ada_a", 0, ADA_FIRST)
            b = filled(v, "mod_a")
            free(cp(modc[:, 0:16], b[:, 0:32].rearrange("p (m w) -> p m w", w=2)), "mod_a")
            emptied(v, "mod_a")
            emptied(v, "columns")
            step(stt(a1, modc[:, 8:16], 1.0, n1w.unsqueeze(2).to_broadcast([P, 8, 2]), ALU.add, ALU.mult))
            for k in range(KT):
                emptied(v, ("xT", k, 0))
                emptied(v, ("xT", k, 1))
                for part, sl in ((0, slice(CTX, TOK)), (1, slice(0, CTX))):
                    ts(hT[:, k, sl], hT[:, k, sl], a1[:, k, part:part + 1], modc[:, k, part:part + 1], ALU.mult,
                       ALU.add).then_inc(hmod, 1)

            def dt_chain():
                b = filled(v, "dt")
                raw, e_, u_ = dtmp
                bv = b[:, 0:TT * 48].rearrange("p (t h) -> p t h", t=TT)
                step_free = tt(raw, bv, dtb.unsqueeze(1).to_broadcast([P, TT, 48]), ALU.add)
                free(step_free, "dt")
                emptied(v, "dt")
                stt(e_, raw, -1.0, raw, ALU.mult, ALU.max).then_inc(exp_small, 1)
                v.wait_ge(small_exped, 2)
                step(ts(u_, e_, 1.0, None, ALU.add))
                cp(cum, u_).then_inc(exp_small, 1)
                v.wait_ge(exp_small, 2)
                step(ts(u_, u_, -1.0, None, ALU.add))
                step(tt(e_, e_, u_, ALU.subtract))
                step(ts(raw, raw, 0.0, None, ALU.max))
                step(v.reciprocal(u_, cum))
                step(tt(e_, e_, u_, ALU.mult))
                v.wait_ge(small_exped, 3)
                step(tt(e_, e_, dt, ALU.add))
                step(tt(dt, e_, raw, ALU.add))
                stt(dtmp[0], dt, -1.0, abc.unsqueeze(1).to_broadcast([P, TT, 48]), ALU.mult, ALU.mult
                    ).then_inc(dt_ready, 1)

            def cumulative_sums():
                bcum = filled(v, "cum")
                free(cp(cum, bcum[:, 0:TT * 48].rearrange("p (t h) -> p t h", t=TT)), "cum")
                btot = filled(v, "tot")
                free(cp(dtmp[1], btot[:, 0:TT * 48].rearrange("p (t h) -> p t h", t=TT)), "tot")
                emptied(v, "cum")
                emptied(v, "tot")
                tt(dtmp[2], dtmp[1], cum, ALU.subtract).then_inc(exp_small, 1)
                v.wait_ge(small_exped, 6)
                tt(toend, toend, dt, ALU.mult).then_inc(cum_ready, 1)
                b = filled(v, "rows")
                v.wait_ge(cum_ready, 1)
                free(cp(cum_rows[0:48, :], b[0:48, :]), "rows")
                emptied(v, "rows")
                v.sem_inc(rows_ready, 1)

            def conv(r, i):
                n = 5 * r + i
                ct = TILE_OF(r, i)
                emptied(v, ("in", n, 0))
                emptied(v, ("in", n, 1))
                src, acc = conv_in[n % 2], conv_acc[n % 2]
                if n >= 2:
                    v.wait_ge(tile_done, n - 1)
                    pr, pi = divmod(n - 2, 5)
                    if pi >= 2:
                        filled(v, ("T", pr, pi, 1))
                step(ts(acc, src[:, 0:CONV_OUT], cols_b[:, ct:ct + 1], cb_col[:, ct:ct + 1], ALU.mult, ALU.add))
                for k in range(1, CONV):
                    col = CONV_TILES * k + ct
                    ins = stt(acc, src[:, k:k + CONV_OUT], cols_b[:, col:col + 1], acc, ALU.mult, ALU.add)
                    if k < CONV - 1:
                        step(ins)
                ins.then_inc(conv_done, 1)

            def state_updates(g):
                for k in range(STEPS):
                    for d in range(2):
                        t = STEP_TILE[d][k]
                        dec = head_bc(decay[:, t, HEADS * d + HG * g:HEADS * d + HG * (g + 1)])
                        dst = hp[d][:, max(k - 1, 0)]
                        if k:
                            src = hp[d][:, max(k - 2, 0)]
                            v.wait_ge(state_ready, STEPS * g + k)
                            step(tt(heads(st_tmp[:, d]), heads(src), dec, ALU.mult))
                        b = filled(v, ("state", g, k, d))
                        if k:
                            ins = tt(dst, b[:, 0:GW], st_tmp[:, d], ALU.add)
                        else:
                            ins = cp(dst, b[:, 0:GW])
                        free(ins, ("state", g, k, d))
                    emptied(v, ("state", g, k, 0))
                    emptied(v, ("state", g, k, 1))
                    v.sem_inc(state_ready, 1)

            def unit_segments(u):
                g, ch = divmod(u, LT)
                v.wait_ge(seg_in[u % 2], 32 * (u // 2 + 1))
                for d in range(2):
                    col = HEADS * d + HG * g
                    ins = tt(seg[u % 2][:, d], seg[u % 2][:, d], head_bc(cum[:, CT + ch, col:col + HG], P),
                             ALU.subtract)
                ins.then_inc(seg_ready, 1)

            def unit_weights(u):
                g, ch = divmod(u, LT)
                v.wait_ge(decays, u + 1)
                b = filled(v, ("cb", u))
                for d in range(2):
                    ins = tt(seg[u % 2][:, d], seg[u % 2][:, d], b[:, 0:P].unsqueeze(1).to_broadcast([P, HG, P]),
                             ALU.mult)
                free(ins, ("cb", u))
                for d in range(2):
                    b = filled(v, ("off", u, d))
                    if u >= 2:
                        filled(v, ("y", u - 2))
                    col = HEADS * d + HG * g
                    free(tt(heads(yb[u % 2][:, d]), heads(b[:, 0:GW]), head_bc(ecum[:, CT + ch, col:col + HG]),
                            ALU.mult), ("off", u, d))

            def unit_gate(u):
                g, ch = divmod(u, LT)
                y = yb[u % 2][:, 0]
                v.wait_ge(offs_summed, u + 1)
                b = filled(v, ("diag", u))
                free(tt(y, y, b[:, 0:GW], ALU.add), ("diag", u))
                emptied(v, ("diag", u))
                emptied(v, ("z", g, ch))
                tt(y, y, zs[g % 2][:, ch], ALU.mult).then_inc(gated, 1)

            def unit_norm(u):
                v.wait_ge(rstd_y, u + 1)
                c_ = 16 + u % 2
                ts(yb[u % 2][:, 0], yb[u % 2][:, 0], stat[:, c_:c_ + 1], None, ALU.mult).then_inc(y_ready, 1)

            dt_chain()
            for r in range(GROUPS + 1):
                g = r - 1
                for i in range(6):
                    if r < GROUPS and i < 5:
                        conv(r, i)
                    if r == 0 and i == 0:
                        mod_evac("ada_b", 4, 4)
                        mod_evac("ada_c", 8, 4)
                        b = filled(v, "mod_b")
                        free(cp(modc[:, 16:48], b[:, 0:64].rearrange("p (m w) -> p m w", w=2)), "mod_b")
                        cumulative_sums()
                    if g >= 0:
                        if i == 0:
                            if g == 0:
                                v.wait_ge(cum_out, 16)
                            if g > 0:
                                unit_norm(4 * g - 1)
                            state_updates(g)
                            unit_segments(4 * g)
                        if i >= 3:
                            unit_norm(4 * g + i - 3)
                        if i >= 2:
                            unit_gate(4 * g + i - 2)
                        if 1 <= i <= 4:
                            unit_weights(4 * g + i - 1)
                            if i < 4:
                                unit_segments(4 * g + i)
            unit_norm(UNITS - 1)

            v.wait_ge(res_in, 16)
            v.wait_ge(mod_bc_in, 16 * 5)
            step(stt(rowbc["scale2"], rowbc["scale2"], 1.0, norm2_bc, ALU.add, ALU.mult))
            v.wait_ge(router_in, 16)
            step(ts(stat[:, 20:28], modc[:, 32:40, 0], 1.0, None, ALU.add))
            step(tt(stat[:, 20:28], stat[:, 20:28], n2w, ALU.mult))
            tt(scaled_router, router_w, stat[:, 20:28].unsqueeze(2).to_broadcast([P, KT, EXPERTS]), ALU.mult
               ).then_inc(router_scaled, 1)
            for t in range(LT):
                for h in range(2):
                    sl = slice(512 * h, 512 * (h + 1))
                    b = filled(v, ("out", t, h))
                    free(tt(out_tmp[:, h], b[:], rowbc["gate1"][:, sl], ALU.mult), ("out", t, h))
                    emptied(v, ("out", t, h))
                    tt(x1[:, t, sl], x1[:, t, sl], out_tmp[:, h], ALU.add).then_inc(x1_ready, 1)
                v.wait_ge(rstd_x1, t + 1)
                ts(h2[:, t], x1[:, t], stat[:, t:t + 1], None, ALU.mult).then_inc(n2_ready, 1)
            b = filled(v, "route_bias")
            free(cp(route_bias, b[:, 0:EXPERTS]), "route_bias")
            for t in range(LT):
                b = filled(v, ("nT", t, 1))
                free(cp(nT[t % 2][:, 4:8], b[:].rearrange("p (k c) -> p k c", k=4)), ("nT", t, 1))
            for t in range(LT):
                filled(v, ("nT", t, 0))
                v.wait_ge(n2_ready, LT)
                step(tt(h2[:, t], h2[:, t], rowbc["scale2"], ALU.mult))
                tt(h2[:, t], h2[:, t], rowbc["shift2"], ALU.add).then_inc(h2_ready, 1)
            b = filled(v, "logits")
            emptied(v, "route_bias")
            free(tt(lg, b[:, 0:64].rearrange("p (t e) -> p t e", t=LT),
                    route_bias.unsqueeze(1).to_broadcast([P, LT, EXPERTS]), ALU.add), "logits")
            emptied(v, "logits")
            step(v.tensor_reduce(rowmax, lg, AX_X, ALU.max))
            tt(lg, lg, rowmax.unsqueeze(2).to_broadcast([P, LT, EXPERTS]), ALU.subtract).then_inc(shifted, 1)
            v.wait_ge(exped, 1)
            step(v.tensor_reduce(rowsum, probs, AX_X, ALU.add))
            step(v.reciprocal(rowsum, rowsum))
            tt(probs, probs, rowsum.unsqueeze(2).to_broadcast([P, LT, EXPERTS]), ALU.mult).then_inc(probs_ready, 1)
            b = filled(v, "probsT")
            free(cp(pT[0:EXPERTS], b[0:EXPERTS, :]), "probsT")
            emptied(v, "probsT")
            for _ in range(CAP // 8):
                step(v.max(top8[0:EXPERTS], pT[0:EXPERTS]))
                step(v.match_replace(pT[0:EXPERTS], top8[0:EXPERTS], pT[0:EXPERTS], -1.0))
            step(ts(mask[0:EXPERTS], pT[0:EXPERTS], 0.0, None, ALU.is_lt))
            step(v.tensor_tensor_scan(cums[0:EXPERTS], ones[0:EXPERTS, 0:1].to_broadcast([EXPERTS, SEQ]),
                                      mask[0:EXPERTS], 0.0, ALU.mult, ALU.add))
            tt(slot1[0:EXPERTS], cums[0:EXPERTS], mask[0:EXPERTS], ALU.mult).then_inc(slots_ready, 1)
            b = filled(v, "slotT")
            free(cp(slotT, b[:, 0:64].rearrange("p (t e) -> p t e", t=LT)), "slotT")
            emptied(v, "slotT")
            v.wait_ge(h2_ready, LT)
            v.memset(moe, 0.0).then_inc(moe_zero, 1)
            v.wait_ge(moe_zero, 1)
            for b in range(8):
                v.wait_ge(bank_free[b], uses[b])
                v.sem_inc(e_free[b], 1)
            with v.Fori(0, EXPERTS) as e:
                one = slotT[:, :, bass.ds(e, 1)].to_broadcast([P, LT, CAP])
                tt(sel, iota1.unsqueeze(1).to_broadcast([P, LT, CAP]), one, ALU.is_equal).then_inc(sel_ready, 1)
                v.wait_ge(sel_ready, e + 1)
                for h in range(2):
                    ins = tt(sel_w[:, :, h], sel, probs[:, :, bass.ds(e, 1)].to_broadcast([P, LT, CAP]), ALU.mult)
                ins.then_inc(selw_ready, 1)
                v.wait_ge(e_full[4], e + 1)
                cp(xgT, bank[4][:].rearrange("p (k c) -> p k c", k=KT)).then_inc(e_free[4], 1)
                v.wait_ge(e_full[3], 2 * e + 1)
                for n in range(2):
                    v.wait_ge(silu_ready, 2 * e + n + 1)
                    tt(act_e[:, 512 * n:512 * (n + 1)], silu_g[:, 512 * n:512 * (n + 1)], bank[2 + n][:], ALU.mult
                       ).then_inc(act_ready, 1)
                v.wait_ge(e_full[5], 2 * e + 2)
                cp(y_e[:, 0:512], bank[4][:]).then_inc(e_free[4], 1)
                cp(y_e[:, 512:1024], bank[5][:]).then_inc(e_free[5], 1)
                for i in range(8):
                    t, n = divmod(i, 2)
                    b = (6, 7, 0, 1, 2, 3, 6, 7)[i]
                    if b >= 6:
                        v.wait_ge(e_full[b], 3 * e + 2 + i // 6)
                    elif b in (1, 3):
                        v.wait_ge(e_full[b], 2 * e + 2)
                    else:
                        v.wait_ge(e_full[b], e + 1)
                    sl = slice(512 * n, 512 * (n + 1))
                    tt(moe[:, t, sl], moe[:, t, sl], bank[b][:], ALU.add).then_inc(e_free[b], 1)
            for b, u in ((0, 1), (1, 1), (2, 1), (3, 1), (6, 3), (7, 3)):
                v.wait_ge(e_free[b], u * EXPERTS + 1)
            v.wait_ge(final_in, 16)
            for t in range(LT):
                step(tt(moe[:, t], moe[:, t], gate2, ALU.mult))
                tt(x1[:, t], x1[:, t], moe[:, t], ALU.add).then_inc(x2_ready, 1)
            for t in range(LT):
                v.wait_ge(rstd_x2, t + 1)
                stt(moe[:, t], x1[:, t], stat[:, t:t + 1], final_bc, ALU.mult, ALU.mult).then_inc(out_ready, 1)

        @block.scalar
        def _(act):
            ac = act.activation

            def ld(dst, src):
                act.dma_start(dst, src).then_inc(small_in, 16)

            ld(cst, consts)
            row = 0
            for src, n in ((norm1_w, 8), (conv_b, 20), (ssm_norm_w, 12), (norm2_w, 8), (c, 8)):
                ld(rows_raw[row:row + n, 0:P], src[0].rearrange("(r c) -> r c", c=P))
                row += n
            ld(rows_raw[row:row + 8, 0:P], c_ctx.rearrange("(r c) -> r c", c=P))
            ld(rows_raw[0:100, P:2 * P], conv_w[0].rearrange("k (r c) -> (k r) c", c=P))
            for h in range(2):
                ld(small_w[64 * h:64 * (h + 1), :].rearrange("p (j c) -> p j c", j=FT),
                   w_fourier[0].rearrange("(j h) i c -> h i j c", h=2)[h])
            ld(abc, a_log[0].rearrange("d h -> (d h)").partition_broadcast(P))
            ld(dtb, dt_bias[0].rearrange("d h -> (d h)").partition_broadcast(P))
            ld(dbc, d_skip[0].partition_broadcast(P))
            for w in range(2):
                act.dma_start(ada_rows_b[w:w + 97:32, :].rearrange("p (m c) -> p m c", m=ADA_N),
                              b_ada[0].rearrange("(m j c) -> j m c", m=ADA_N, c=P)).then_inc(ada_b_in, 16)
            for t in range(TT):
                act.wait_ge(ctx_in if t < CT else lat_in, 16)
                ac(hT.rearrange("p k t -> p (k t)")[:, D * t:D * (t + 1)], x_raw[:, t], ACT.Square,
                   accum_out=stat[:, 8 + t:9 + t]).then_inc(square_done, 1)
            act.wait_ge(square_done, TT)
            emptied(act, "columns")
            ac(scT, cols_a[:, 48:64], ACT.Silu).then_inc(silu_c, 1)
            for k in range(KT):
                b = filled(act, ("xT", k, 0))
                free(ac(hT[:, k, CTX:TOK], b[:], ACT.Copy), ("xT", k, 0))

            def evac_in(r, i):
                n = 5 * r + i
                if n >= 2:
                    act.wait_ge(conv_done, n - 1)
                if n < 2:
                    act.wait_ge(pads_zero, 1)
                b = filled(act, ("in", n, 0))
                free(ac(conv_in[n % 2][:, PAD + LAT0:PAD + LAT0 + SEQ], b[:], ACT.Copy), ("in", n, 0))
                b = filled(act, ("in", n, 1))
                free(ac(conv_in[n % 2][:, PAD:PAD + CTX], b[:, 0:CTX], ACT.Copy), ("in", n, 1))

            def silu_tile(r, i):
                n = 5 * r + i
                act.wait_ge(conv_done, n + 1)
                dst = bc_ch[r % 2][i] if i < 2 else conv_acc[n % 2]
                ac(dst, conv_acc[n % 2], ACT.Silu).then_inc(tile_done, 1)

            def evac_tokens(r, s):
                o = 0 if s == 0 else P * (s - 1)
                for part, (t0, m) in enumerate(((CT, LT), (0, CT))):
                    b = filled(act, ("T", r, s, part))
                    free(ac(tok[r % 2][:, t0:t0 + m, o:o + P], b[:, 0:P * m].rearrange("p (t c) -> p t c", t=m),
                            ACT.Copy), ("T", r, s, part))

            def dt_chain():
                act.wait_ge(exp_small, 1)
                ac(dtmp[1], dtmp[1], ACT.Exp, scale=-1.0).then_inc(small_exped, 1)
                ac(abc, abc, ACT.Exp).then_inc(small_exped, 1)
                act.wait_ge(exp_small, 2)
                ac(dt, cum, ACT.Ln).then_inc(small_exped, 1)

            def exp_of_sums():
                act.wait_ge(exp_small, 3)
                ac(toend, dtmp[2], ACT.Exp).then_inc(small_exped, 1)
                ac(decay, dtmp[1], ACT.Exp).then_inc(small_exped, 1)
                ac(ecum, cum, ACT.Exp).then_inc(small_exped, 1)

            def unit_exp(u):
                act.wait_ge(masked, u + 1)
                w = seg[u % 2].rearrange("p d h l -> p (d h l)")
                ac(w, w, ACT.Exp).then_inc(decays, 1)

            def unit_square(u):
                act.wait_ge(gated, u + 1)
                act.wait_ge(offs_summed, u + 1)
                ac(yb[u % 2][:, 1], yb[u % 2][:, 0], ACT.Square, accum_out=stat[:, 18 + u % 2:19 + u % 2]
                   ).then_inc(squared, 1)

            def unit_evac(u):
                g, ch = divmod(u, LT)
                b = filled(act, ("y", u))
                for j in range(XT):
                    ins = ac(yT[:, XT * g + j, P * ch:P * (ch + 1)], b[:, P * j:P * (j + 1)], ACT.Identity,
                             bias=0.0, scale=ssm_col[:, XT * g + j:XT * g + j + 1])
                free(ins, ("y", u))

            dt_chain()
            for r in range(GROUPS + 1):
                g = r - 1
                for i in range(6):
                    if r < GROUPS and i < 5:
                        evac_in(r, i)
                        silu_tile(r, i)
                    elif r < GROUPS:
                        for t in range(LT):
                            b = filled(act, ("z", r, t))
                            free(ac(zs[r % 2][:, t], b[:, 0:GW], ACT.Silu), ("z", r, t))
                    elif i < FT:
                        act.wait_ge(mod_out, 16)
                        b = filled(act, ("u", i))
                        free(ac(uT[:, i], b[:], ACT.Copy), ("u", i))
                    elif i == FT:
                        for t in range(LT):
                            for h in range(2):
                                b = filled(act, ("v", t, h))
                                free(ac(vf[:, t, 2 * h:2 * h + 2], b[:].rearrange("p (j c) -> p j c", j=2), ACT.Copy),
                                     ("v", t, h))
                    if r == 0 and i == 0:
                        exp_of_sums()
                    if r < GROUPS and i in (1, 3, 4, 5):
                        evac_tokens(r, {1: 0, 3: 2, 4: 3, 5: 4}[i])
                    if g >= 0:
                        if i == 0:
                            if g > 0:
                                unit_evac(4 * g - 1)
                            unit_exp(4 * g)
                        if i >= 3:
                            unit_evac(4 * g + i - 3)
                        if i >= 2:
                            unit_square(4 * g + i - 2)
                        if 1 <= i <= 3:
                            unit_exp(4 * g + i)
                    if r == GROUPS and i == 5:
                        for j in range(FT):
                            b = filled(act, ("f", j))
                            free(ac(fT[:, j], b[:], ACT.Copy), ("f", j))
            unit_evac(UNITS - 1)
            for t in range(LT):
                act.wait_ge(x1_ready, 2 * t + 2)
                ac(h2[:, t], x1[:, t], ACT.Square, accum_out=stat[:, 8 + t:9 + t]
                   ).then_inc(x1_squared, 1)
            act.wait_ge(x1_squared, LT)
            for t in range(LT):
                b = filled(act, ("nT", t, 0))
                free(ac(nT[t % 2][:, 0:4], b[:].rearrange("p (k c) -> p k c", k=4), ACT.Copy), ("nT", t, 0))
            act.wait_ge(shifted, 1)
            ac(probs, lg, ACT.Exp).then_inc(exped, 1)
            with act.Fori(0, EXPERTS) as e:
                act.wait_ge(e_full[5], 2 * e + 1)
                ac(scatter, bank[5][:], ACT.Copy).then_inc(e_free[5], 1)
                act.wait_ge(e_full[1], 2 * e + 1)
                for n in range(2):
                    ac(silu_g[:, 512 * n:512 * (n + 1)], bank[n][:], ACT.Silu).then_inc(silu_ready, 1)
                for n in range(2):
                    act.wait_ge(e_full[6 + n], 3 * e + 1)
                    ac(actT[:, 512 * n:512 * (n + 1)], bank[6 + n][:], ACT.Copy).then_inc(e_free[6 + n], 1)
            for t in range(LT):
                act.wait_ge(x2_ready, t + 1)
                ac(moe[:, t], x1[:, t], ACT.Square, accum_out=stat[:, 8 + t:9 + t]).then_inc(x2_squared, 1)

        @block.gpsimd
        def _(gp):
            step = Chain(gp, pool)
            tt = gp.tensor_tensor

            def state_inputs(g):
                for s in (0, 2, 3, 4):
                    emptied(gp, ("T", g, s, 0))
                    emptied(gp, ("T", g, s, 1))
                for k in range(STEPS):
                    if k >= 2:
                        filled(gp, ("state", g, k - 2, 1))
                    for d in range(2):
                        t = STEP_TILE[d][k]
                        col = HEADS * d + HG * g
                        ins = tt(heads(xw[:, k % 2, d]), heads(tok[g % 2][:, t, P:]), head_bc(toend[:, t, col:col + HG]),
                                 ALU.mult)
                    ins.then_inc(xw_ready, 1)

            def unit_inputs(u):
                g, ch = divmod(u, LT)
                if u >= 2:
                    filled(gp, ("diag", u - 2))
                xs = heads(tok[g % 2][:, CT + ch, P:])
                tt(heads(xd[u % 2]), xs, head_bc(dbc[:, HG * g:HG * (g + 1)]), ALU.mult)
                for d in range(2):
                    col = HEADS * d + HG * g
                    ins = tt(heads(xdt[u % 2][:, d]), xs, head_bc(dt[:, CT + ch, col:col + HG]), ALU.mult)
                ins.then_inc(xdt_ready, 1)

            def unit_mask(u):
                gp.wait_ge(seg_ready, u + 1)
                for d, sign in ((0, 1), (1, -1)):
                    ins = gp.affine_select(out=seg[u % 2][:, d], in_=seg[u % 2][:, d], compare_op=ALU.is_ge,
                                           fill=MASKED, base=0, pattern=[[0, HG], [sign, P]],
                                           channel_multiplier=-sign)
                ins.then_inc(masked, 1)

            def unit_sum(u):
                emptied(gp, ("off", u, 0))
                emptied(gp, ("off", u, 1))
                gp.wait_ge(xdt_ready, u + 1)
                y = yb[u % 2]
                step(tt(y[:, 0], y[:, 0], y[:, 1], ALU.add))
                tt(y[:, 0], y[:, 0], xd[u % 2], ALU.add).then_inc(offs_summed, 1)

            def rstd(dst, src, width, ready):
                step(gp.tensor_scalar(dst, src, 1.0 / width, EPS, ALU.mult, ALU.add))
                tt(dst, dst, stat[:, 28:29], ALU.pow).then_inc(ready, 1)

            def unit_rstd(u):
                gp.wait_ge(squared, u + 1)
                c_ = 16 + u % 2
                rstd(stat[:, c_:c_ + 1], stat[:, c_ + 2:c_ + 3], GW, rstd_y)

            def row_rstd(squares, ready, n):
                for t in range(n):
                    gp.wait_ge(squares, t + 1)
                    rstd(stat[:, t:t + 1], stat[:, 8 + t:9 + t], D, ready)

            step(gp.memset(stat[:, 28:29], -0.5))
            row_rstd(square_done, rstd_x, TT)
            gp.wait_ge(cum_ready, 1)
            gp.wait_ge(cum_out, 16)
            for g in range(GROUPS):
                if g:
                    unit_rstd(4 * g - 1)
                state_inputs(g)
                unit_inputs(4 * g)
                unit_mask(4 * g)
                for ch in range(LT):
                    u = 4 * g + ch
                    unit_sum(u)
                    if ch < LT - 1:
                        unit_inputs(u + 1)
                        unit_mask(u + 1)
                    if ch:
                        unit_rstd(u - 1)
            unit_rstd(UNITS - 1)
            row_rstd(x1_squared, rstd_x1, LT)
            row_rstd(x2_squared, rstd_x2, LT)


_INS = ['x', 'c', 'ctx', 'c_ctx', 'w_ada', 'b_ada', 'norm1_w', 'w_in', 'conv_w', 'conv_b', 'dt_bias', 'a_log',
        'd_skip', 'ssm_norm_w', 'w_fourier', 'w_out', 'norm2_w', 'w_router', 'w_gate', 'w_up', 'w_down',
        'final_norm_w']


def kernel(**inputs):
    import numpy as _np
    import concourse.bacc as _bacc
    from concourse import mybir as _mybir
    from concourse.bass_utils import run_bass_kernel_spmd as _run

    nc = _bacc.Bacc("TRN2", target_bir_lowering=False, num_devices=1)
    consts, dft = host_constants()
    arrays, args = {}, []
    for name, a in [("consts", consts), ("dft", dft)] + [(n, _np.ascontiguousarray(inputs[n])) for n in _INS]:
        arrays[f"in_{name}_dram"] = a
        args.append(nc.dram_tensor(f"in_{name}_dram", a.shape, _mybir.dt.from_np(a.dtype), kind="ExternalInput").ap())
    args.append(nc.dram_tensor("out_0_dram", (1, SEQ, D), F32, kind="ExternalOutput").ap())
    build(nc, *args)
    r = _run(nc, [arrays], core_ids=[0])
    return r.results[0]["out_0_dram"]
```

```python
from contextlib import ExitStack

import numpy as np

import concourse.bass as bass
from concourse import mybir

F32 = mybir.dt.float32
ALU = mybir.AluOpType
ACT = mybir.ActivationFunctionType
AX_X = mybir.AxisListType.X

P = 128
D = 1024
KT = D // P
SEQ, CTX = 512, 256
LT, CT = SEQ // P, CTX // P
TT = CT + LT
TOK = SEQ + CTX
F_DIM, F_GROUP = 512, 64
FT = F_DIM // P
HD = 64
D_SSM = 1536
HEADS = D_SSM // HD
GROUPS = 4
HG = HEADS // GROUPS
GW = HG * HD
XT = GW // P
YT = D_SSM // P
CONV = 5
CONV_TILES = (D_SSM + 2 * GROUPS * P) // P
COL_Z = F_DIM
COL_X = COL_Z + D_SSM
COL_B = COL_X + D_SSM
COL_C = COL_B + GROUPS * P
COL_DT = COL_C + GROUPS * P
DT_W = 64
EXPERTS, CAP, FE = 16, 64, 2048
EPS = 1e-6
MASKED = -1e30

PAD = CONV // 2
CONV_IN = TOK + 3 * PAD
CONV_OUT = TOK + PAD
LAT0 = CTX + PAD

ADA_W = 512
ADA_N = 6 * D // ADA_W
ADA_FIRST = 4
UNITS = GROUPS * LT
STEPS = CT + LT - 1
RING = 12
CHUNKS = 24
WO_SLOTS = 4
WO_ORDER = [*range(4, 13), *range(4), *range(13, 16)]
TOKENS_AT = {1: 0, 3: 2, 4: 3, 5: 4}


def host_constants():
    c = np.zeros((P, 6 * P + 8 + CAP), np.float32)
    i = np.arange(P)
    c[:, 0:P] = np.eye(P)
    c[:, P:2 * P] = i[:, None] <= i[None, :]
    c[:, 2 * P:3 * P] = i[:, None] >= i[None, :]
    c[:, 3 * P:4 * P] = 1.0
    angle = 2 * np.pi * ((np.arange(F_GROUP)[:, None] * np.arange(F_GROUP)[None, :]) % F_GROUP) / F_GROUP
    scale = 1.0 / np.sqrt(SEQ * F_GROUP)
    for b in range(2):
        s = slice(b * F_GROUP, (b + 1) * F_GROUP)
        c[s, 4 * P + b * F_GROUP:4 * P + (b + 1) * F_GROUP] = np.cos(angle) * scale
        c[s, 5 * P + b * F_GROUP:5 * P + (b + 1) * F_GROUP] = -np.sin(angle) * scale
    for j in range(4):
        for w in range(2):
            c[32 * j + w, 6 * P + 2 * j + w] = 1.0
    c[:, 6 * P + 8:] = np.arange(1, CAP + 1)
    t = np.arange(SEQ)
    seq = 2 * np.pi * ((t[:, None] * t[None, :]) % SEQ) / SEQ
    dft = np.stack([np.cos(seq), np.sin(seq)], 1).astype(np.float32).reshape(LT, P, 2 * SEQ)
    return c, dft


def bank_turns():
    used, turns = [0] * 8, {}

    def take(key, bank):
        turns[key] = (bank, used[bank])
        used[bank] += 1

    take("columns", 4)
    take("fourier_w", 7)
    for k in range(KT):
        take(("xT", k, 0), k % 2)
        take(("xT", k, 1), 2 + k % 2)
    take("ada_a", 6)
    take("mod_a", 4)
    for r in range(GROUPS + 1):
        g = r - 1
        for i in range(6):
            if r < GROUPS and i < 5:
                n = 5 * r + i
                take(("in", n, 0), n % 2)
                take(("in", n, 1), 2 + n % 2)
            elif r < GROUPS:
                for t in range(LT):
                    take(("z", r, t), t)
            elif i < FT:
                take(("u", i), i % 2)
            elif i == FT:
                for t in range(LT):
                    take(("v", t, 0), 2 * (t % 2))
                    take(("v", t, 1), 2 * (t % 2) + 1)
            if r < GROUPS and i in TOKENS_AT:
                take(("T", r, TOKENS_AT[i], 0), 5)
                take(("T", r, TOKENS_AT[i], 1), 6)
            if r == 0:
                for key, bank in ((), (("ada_b", 4), ("cum", 7), ("tot", 6)), (("rows", 7),), (("ada_c", 7),), (),
                                  (("mod_b", 4),))[i] if i else (("dt", 5),):
                    take(key, bank)
            if g >= 0:
                if i == 0:
                    if g > 0:
                        take(("y", 4 * g - 1), 7)
                    for k in range(STEPS):
                        take(("state", g, k, 0), (5, 4)[k % 2])
                        take(("state", g, k, 1), (6, 7)[k % 2])
                if i >= 3:
                    take(("y", 4 * g + i - 3), 7)
                if 2 <= i:
                    take(("diag", 4 * g + i - 2), 7)
                if 1 <= i <= 4:
                    v = 4 * g + i - 1
                    take(("cb", v), 4)
                    take(("off", v, 0), 5)
                    take(("off", v, 1), 6)
    for j in range(FT):
        take(("f", j), j)
    take(("y", UNITS - 1), 7)
    for t in range(LT):
        for h in range(2):
            take(("out", t, h), 2 * t + h)
    for t in range(LT):
        take(("nT", t, 0), 3 if t == LT - 1 else 1)
        take(("nT", t, 1), 4 if t == LT - 1 else 2)
    take("logits", 0)
    take("probsT", 6)
    take("slotT", 7)
    return turns, used


def build(nc, consts, dft, x, c, ctx_tokens, c_ctx, w_ada, b_ada, norm1_w, w_in, conv_w, conv_b, dt_bias, a_log,
          d_skip, ssm_norm_w, w_fourier, w_out, norm2_w, w_router, w_gate, w_up, w_down, final_norm_w, out, stop=None):
    turns, uses = bank_turns()
    with ExitStack() as ctx:
        def sem(name):
            return ctx.enter_context(nc.semaphore(name))

        arena = ctx.enter_context(nc.sbuf_tensor("arena", [P, 53200], F32))
        bank = [ctx.enter_context(nc.psum_tensor(f"bank{b}", [P, 512], F32)) for b in range(8)]
        mod_dram = nc.dram_tensor("mod_rows_dram", (ADA_N, 4, P), F32, kind="Internal").ap()
        cum_dram = nc.dram_tensor("cum_rows_dram", (2 * HEADS, SEQ), F32, kind="Internal").ap()

        def at(offset, *shape):
            n = int(np.prod(shape))
            v = arena[:, offset:offset + n]
            if len(shape) == 2:
                return v.rearrange("p (a b) -> p a b", a=shape[0])
            if len(shape) == 3:
                return v.rearrange("p (a b c) -> p a b c", a=shape[0], b=shape[1])
            return v

        hT = at(0, KT, TOK)
        w_buf = [at(6144 + 3072 * s, 3072) for s in range(2)]
        conv_in = [at(12288 + CONV_IN * s, CONV_IN) for s in range(2)]
        conv_acc = [at(13836 + CONV_OUT * s, CONV_OUT) for s in range(2)]
        bc_ch = [[at(15376 + (2 * s + j) * CONV_OUT, CONV_OUT) for j in range(2)] for s in range(2)]
        tok = [at(18456 + 3072 * s, TT, 512) for s in range(2)]
        ada_rows_b = at(21528, ADA_N * P)
        yT = at(24600, YT, SEQ)
        x_raw = at(24600, TT, D)
        fT = at(30744, FT, SEQ)
        rows_raw = at(30744, 2 * P)
        small_w = at(31000, FT * F_GROUP)
        zs = [at(32792 + 1536 * s, LT, GW) for s in range(2)]
        ada_buf = [at(32792 + 4096 * s, KT, ADA_W) for s in range(3)]
        hp = [at(35864 + 1536 * d, LT, GW) for d in range(2)]
        seg = [at(38936 + 1536 * s, 2, HG, P) for s in range(2)]
        xdt = [at(42008 + 768 * s, 2, GW) for s in range(2)]
        xd = [at(43544 + 384 * s, GW) for s in range(2)]
        yb = [at(44312 + 768 * s, 2, GW) for s in range(2)]
        uT = at(45848, FT, SEQ)
        mod_rows = at(45848, ADA_N * P)
        xw = at(47896, 2, 2, GW)
        st_tmp = at(49432, 2, GW)
        vf = at(0, LT, FT, 2 * P)
        dft_buf = [at(4096 + 1024 * s, 2, SEQ) for s in range(2)]
        wo_buf = [at(o, D) for o in (48152, 49176, 47128, 32792)]
        x1 = at(36888, LT, D)
        rowbc = {n: at(40984 + D * i, D) for i, n in enumerate(("shift2", "scale2", "gate1", "gate2"))}
        norm2_bc = at(33816, D)
        out_tmp = at(34840, 2, 512)
        ring = [at(2048 * s, 2048) for s in range(RING)]
        h2 = at(45080, LT, D)
        nT = [at(o, KT, P) for o in (35864, 33816)]
        small = 31000
        lg = at(small, LT, EXPERTS)
        probs = at(small + 64, LT, EXPERTS)
        slotT = at(small + 128, LT, EXPERTS)
        rowmax = at(small + 192, LT)
        rowsum = at(small + 196, LT)
        pT = at(small + 216, SEQ)
        top8 = at(small + 728, 8)
        mask = at(32792, SEQ)
        cums = at(32792 + 512, SEQ)
        slot1 = at(32792 + 1024, SEQ)
        sel = at(28696, LT, CAP)
        sel_w = at(28952, LT, 2, CAP)
        scatter = at(29464, SEQ)
        xgT = at(29976, KT, CAP)
        silu_g = at(32792, 1024)
        act_e = at(33816, 1024)
        actT = at(34840, 1024)
        y_e = at(35864, 1024)
        out_rows = at(24600, LT, D)
        gate2 = rowbc["gate2"]
        final_bc = at(40984, D)

        s0 = [50200]

        def keep(*shape):
            o = s0[0]
            s0[0] += int(np.prod(shape))
            return at(o, *shape)

        cst = keep(6 * P + 8 + CAP)
        ident, tri_f, tri_b, ones = (cst[:, P * i:P * (i + 1)] for i in range(4))
        dft_c, dft_s = cst[:, 4 * P:5 * P], cst[:, 5 * P:6 * P]
        sel8, iota1 = cst[:, 6 * P:6 * P + 8], cst[:, 6 * P + 8:6 * P + 8 + CAP]
        cols_a = keep(64)
        cols_b = keep(CONV * CONV_TILES)
        n1w, cb_col, ssm_col, n2w = cols_a[:, 0:8], cols_a[:, 8:28], cols_a[:, 28:40], cols_a[:, 40:48]
        scT = keep(16)
        modc = keep(ADA_N * 4, 2)
        a1 = keep(8, 2)
        stat = keep(32)
        abc, dtb, dbc = keep(48), keep(48), keep(24)
        cum = keep(TT, 48)
        dt = keep(TT, 48)
        ecum = keep(TT, 48)
        toend = keep(TT, 48)
        decay = keep(TT, 48)
        router_w = keep(KT, EXPERTS)
        assert s0[0] <= 53200, s0[0]
        w_dt = at(21528 + 1536, KT, DT_W)
        dtmp = [at(49176 + 288 * i, TT, 48) for i in range(3)]
        cum_rows = at(49176, SEQ)
        fw = at(30744 + 1024, FT, 2 * P)

        bank_full = [sem(f"bank_full{b}") for b in range(8)]
        bank_free = [sem(f"bank_free{b}") for b in range(8)]
        small_in, ctx_in, lat_in, w_dt_in = sem("small_in"), sem("ctx_in"), sem("lat_in"), sem("w_dt_in")
        ada_in = [sem(f"ada_in{s}") for s in range(3)]
        ada_used = sem("ada_used")
        ada_b_in = sem("ada_b_in")
        w_in_sem = [sem(f"w_in{s}") for s in range(2)]
        pads_zero = sem("pads_zero")
        seg_in = [sem(f"seg_in{s}") for s in range(2)]
        dft_in = [sem(f"dft_in{s}") for s in range(2)]
        dft_used = sem("dft_used")
        mod_out, mod_bc_in, cum_out = sem("mod_out"), sem("mod_bc_in"), sem("cum_out")
        dve, act_s, pool = sem("dve_step"), sem("act_step"), sem("pool_step")
        square_done, xn_done = sem("square_done"), sem("xn_done")
        rstd_x, rstd_y, rstd_x1, rstd_x2 = sem("rstd_x"), sem("rstd_y"), sem("rstd_x1"), sem("rstd_x2")
        silu_c, hmod, zeroed = sem("silu_c"), sem("hmod"), sem("zeroed")
        dt_ready, cum_ready, rows_ready = sem("dt_ready"), sem("cum_ready"), sem("rows_ready")
        exp_small, small_exped = sem("exp_small"), sem("small_exped")
        conv_done, tile_done = sem("conv_done"), sem("tile_done")
        xw_ready, state_ready, xdt_ready = sem("xw_ready"), sem("state_ready"), sem("xdt_ready")
        seg_ready, masked, decays = sem("seg_ready"), sem("masked"), sem("decays")
        offs_summed, gated, squared, y_ready = sem("offs_summed"), sem("gated"), sem("squared"), sem("y_ready")
        wo_in = [sem(f"wo_in{s}") for s in range(WO_SLOTS)]
        wo_used, res_in, x1_ready = sem("wo_used"), sem("res_in"), sem("x1_ready")
        x1_squared, h2_ready, router_in = sem("x1_squared"), sem("h2_ready"), sem("router_in")
        shifted, exped, probs_ready, slots_ready = sem("shifted"), sem("exped"), sem("probs_ready"), sem("slots_ready")
        ring_in = [sem(f"ring_in{s}") for s in range(RING)]
        ring_used = sem("ring_used")
        e_full = [sem(f"expert_full{b}") for b in range(8)]
        e_free = [sem(f"expert_free{b}") for b in range(8)]
        sel_ready, selw_ready, silu_ready, act_ready = (sem(n) for n in ("sel_ready", "selw_ready", "silu_ready",
                                                                       "act_ready"))
        final_in = sem("final_in")
        x2_squared, out_ready, out_done = sem("x2_squared"), sem("out_ready"), sem("out_done")

        def filled(eng, key):
            b, n = turns[key]
            eng.wait_ge(bank_full[b], n + 1)
            return bank[b]

        def emptied(eng, key):
            b, n = turns[key]
            eng.wait_ge(bank_free[b], n + 1)

        def claim(pe, key):
            b, n = turns[key]
            if n:
                pe.wait_ge(bank_free[b], n)
            return bank[b]

        def full(ins, key):
            ins.then_inc(bank_full[turns[key][0]], 1)

        def free(ins, key):
            ins.then_inc(bank_free[turns[key][0]], 1)

        class Chain:

            def __init__(self, eng, s):
                self.eng, self.s, self.n = eng, s, 0

            def __call__(self, ins):
                self.n += 1
                ins.then_inc(self.s, 1)
                self.eng.wait_ge(self.s, self.n)

        def bc(v, *shape):
            return v.to_broadcast(list((P,) + shape))

        def ada_piece_used(eng, i):
            key = ("ada_a", "ada_b", "ada_c")[i // 4]
            if i % 4 == 3:
                filled(eng, key)
            else:
                eng.wait_ge(ada_used, i + 1 - (i + 1) // 4)

        def weights_used(eng, q):
            r, part = divmod(q, 3)
            if r == GROUPS:
                filled(eng, ("u", 2 * part + 1))
            else:
                filled(eng, (("in", 5 * r + 1, 1), ("in", 5 * r + 4, 1), ("z", r, LT - 1))[part])

        def chunk_used(eng, e, ch):
            if ch == 14:
                eng.wait_ge(e_full[1], e * 2 + 1)
            elif ch == 15:
                eng.wait_ge(e_full[3], e * 2 + 1)
            elif ch == 23:
                eng.wait_ge(e_full[5], e * 2 + 2)
            else:
                eng.wait_ge(ring_used, e * (CHUNKS - 3) + (ch + 1 if ch < 14 else ch - 1))

        def head_bc(v, width=HD):
            return v.unsqueeze(2).to_broadcast([P, HG, width])

        def heads(v):
            return v.rearrange("p (h c) -> p h c", h=HG)

        def lat_ctx(v):
            return v[:, LAT0:LAT0 + SEQ], v[:, 0:CTX]

        def chan(v, t):
            o = P * t if t < CT else LAT0 + P * (t - CT)
            return v[:, o:o + P]

        STEP_TILE = [[0, 1, 2, 3, 4], [1, 0, 5, 4, 3]]
        TILE_OF = lambda r, i: (12 + r, 16 + r, 3 * r, 3 * r + 1, 3 * r + 2)[i]
        SMALL_N = 16 * 13

        block = ctx.enter_context(nc.Block())

        @block.sync
        def _(sp):
            sp.dma_start(x_raw[:, 0:CT, :], ctx_tokens[0].rearrange("(t p) d -> p t d", p=P)).then_inc(ctx_in, 16)
            sp.dma_start(x_raw[:, CT:TT, :], x[0].rearrange("(t p) d -> p t d", p=P)).then_inc(lat_in, 16)

            def ld(dst, src):
                sp.dma_start(dst, src).then_inc(small_in, 16)

            ld(cst, consts)
            row = 0
            for src, n in ((norm1_w, 8), (conv_b, 20), (ssm_norm_w, 12), (norm2_w, 8), (c, 8)):
                ld(rows_raw[row:row + n, 0:P], src[0].rearrange("(r c) -> r c", c=P))
                row += n
            ld(rows_raw[row:row + 8, 0:P], c_ctx.rearrange("(r c) -> r c", c=P))
            ld(rows_raw[0:100, P:2 * P], conv_w[0].rearrange("k (r c) -> (k r) c", c=P))
            for h in range(2):
                ld(small_w[64 * h:64 * (h + 1), :].rearrange("p (j c) -> p j c", j=FT),
                   w_fourier[0].rearrange("(j h) i c -> h i j c", h=2)[h])
            ld(abc, a_log[0].rearrange("d h -> (d h)").partition_broadcast(P))
            ld(dtb, dt_bias[0].rearrange("d h -> (d h)").partition_broadcast(P))
            ld(dbc, d_skip[0].partition_broadcast(P))
            for w in range(2):
                sp.dma_start(ada_rows_b[w:w + 97:32, :].rearrange("p (m c) -> p m c", m=ADA_N),
                              b_ada[0].rearrange("(m j c) -> j m c", m=ADA_N, c=P)).then_inc(ada_b_in, 16)
            sp.dma_start(w_dt, w_in[0, :, COL_DT + 48 - DT_W:].rearrange("(k p) c -> p k c", p=P)).then_inc(w_dt_in, 16)

            def load_ada(i):
                if i >= 3:
                    ada_piece_used(sp, i - 3)
                sp.dma_start(ada_buf[i % 3], w_ada[0, :, ADA_W * i:ADA_W * (i + 1)].rearrange("(k p) c -> p k c", p=P)
                             ).then_inc(ada_in[i % 3], 16)

            def load_w(q):
                r, part = divmod(q, 3)
                if q >= 2:
                    weights_used(sp, q - 2)
                dst = w_buf[q % 2]
                if r == GROUPS:
                    cols = [(256 * part, 256, 0)]
                    width = 256
                elif part == 0:
                    cols, width = [(COL_B + P * r, P, 0), (COL_C + P * r, P, P)], 256
                elif part == 1:
                    cols, width = [(COL_X + GW * r, GW, 0)], GW
                else:
                    cols, width = [(COL_Z + GW * r, GW, 0)], GW
                v = dst[:, 0:KT * width].rearrange("p (k c) -> p k c", k=KT)
                for col, n, o in cols:
                    sp.dma_start(v[:, :, o:o + n], w_in[0, :, col:col + n].rearrange("(k p) c -> p k c", p=P)
                                 ).then_inc(w_in_sem[q % 2], 16)

            for i in range(ADA_FIRST):
                load_ada(i)
            load_w(0)
            load_w(1)
            for i in range(ADA_FIRST, ADA_N):
                load_ada(i)
                if i == 8:
                    load_w(2)
            filled(sp, "ada_c")
            sp.wait_ge(cum_out, 16)
            load_w(3)
            q = 4
            for v in range(UNITS):
                g, ch = divmod(v, LT)
                if v >= 2:
                    filled(sp, ("diag", v - 2))
                for d in range(2):
                    src = cum_dram[HEADS * d + HG * g:HEADS * d + HG * (g + 1), P * ch:P * (ch + 1)]
                    sp.dma_start(seg[v % 2][:, d], src.partition_broadcast(P)).then_inc(seg_in[v % 2], 16)
                while q < min(3 * (g + 1) + 1 + ch, 3 * GROUPS + 2):
                    load_w(q)
                    q += 1
            def load_wo(n):
                sp.dma_start(wo_buf[n % WO_SLOTS], w_out[0, P * WO_ORDER[n % 16]:P * (WO_ORDER[n % 16] + 1), :]
                             ).then_inc(wo_in[n % WO_SLOTS], 16)

            for t in range(LT):
                if t == 0:
                    emptied(sp, ("u", FT - 1))
                if t >= 2:
                    sp.wait_ge(dft_used, t - 1)
                if t == 2:
                    emptied(sp, ("state", GROUPS - 1, STEPS - 1, 1))
                    filled(sp, ("v", LT - 1, 1))
                    sp.wait_ge(gated, 4 * (GROUPS - 1))
                    for n in range(WO_SLOTS):
                        load_wo(n)
                sp.dma_start(dft_buf[t % 2], dft[t].rearrange("p (s l) -> p s l", s=2)).then_inc(dft_in[t % 2], 16)

            def load_chunk(e, ch):
                dst = ring[ch % RING]
                if ch < 16:
                    src = (w_gate if ch % 2 == 0 else w_up)[0, bass.ds(e, 1), P * (ch // 2):P * (ch // 2 + 1), :]
                    sp.dma_start(dst, src.rearrange("a p f -> p (a f)")).then_inc(ring_in[ch % RING], 16)
                else:
                    j = ch - 16
                    src = w_down[0, bass.ds(e, 1)].rearrange("a (h j p) d -> j p (a h) d", h=2, p=P)[j]
                    sp.dma_start(dst.rearrange("p (h d) -> p h d", h=2), src).then_inc(ring_in[ch % RING], 16)

            filled(sp, ("y", UNITS - 1))
            emptied(sp, ("f", FT - 1))
            sp.dma_start(x1, x[0].rearrange("(t p) d -> p t d", p=P)).then_inc(res_in, 16)
            sp.dma_start(router_w, w_router[0].rearrange("(k p) e -> p k e", p=P)).then_inc(router_in, 16)
            sp.wait_ge(mod_out, 16)
            for name, m in (("gate1", 2), ("scale2", 4), ("shift2", 3), ("gate2", 5)):
                src = mod_dram[2 * m:2 * m + 2].rearrange("m j c -> (m j c)")
                sp.dma_start(rowbc[name], src.partition_broadcast(P)).then_inc(mod_bc_in, 16)
            sp.dma_start(norm2_bc, norm2_w[0].partition_broadcast(P)).then_inc(mod_bc_in, 16)
            for n in range(WO_SLOTS, 2 * 16):
                m = n - WO_SLOTS
                if m % 16 == 15:
                    filled(sp, ("out", 2 * (m // 16) + 1, 1))
                else:
                    sp.wait_ge(wo_used, m + 1 - m // 16)
                load_wo(n)
                if n % 2 == 0 and n // 2 - 3 in range(RING):
                    load_chunk(0, n // 2 - 3)
            with sp.Fori(0, EXPERTS - 1) as e:
                for ch in range(RING, CHUNKS):
                    if ch != 16:
                        chunk_used(sp, e, ch - RING + (ch == 15))
                    load_chunk(e, ch)
                for ch in range(RING):
                    chunk_used(sp, e, ch + CHUNKS - RING)
                    load_chunk(e + 1, ch)
            for ch in range(RING, CHUNKS):
                chunk_used(sp, EXPERTS - 1, ch - RING)
                load_chunk(EXPERTS - 1, ch)
            sp.dma_start(final_bc, final_norm_w.partition_broadcast(P)).then_inc(final_in, 16)
            for t in range(LT):
                sp.wait_ge(out_ready, t + 1)
                sp.dma_start(out[0, P * t:P * (t + 1), :], out_rows[:, t]).then_inc(out_done, 16)
            sp.wait_ge(out_done, 16 * LT)

        @block.tensor
        def _(pe):
            mm, tr = pe.matmul, pe.transpose

            pe.wait_ge(small_in, SMALL_N)
            b = claim(pe, "columns")
            tr(b[:, 0:64], rows_raw[0:64, 0:P], ident[0:64, 0:64])
            full(tr(b[:, 64:164], rows_raw[0:100, P:2 * P], ident[0:100, 0:100]), "columns")
            b = claim(pe, "fourier_w")
            mm(b[:, 0:256], dft_c, small_w, start=True, stop=True)
            full(mm(b[:, 256:512], dft_s, small_w, start=True, stop=True), "fourier_w")
            pe.wait_ge(xn_done, TT)
            for k in range(KT):
                for part, (t0, n) in enumerate(((CT, LT), (0, CT))):
                    b = claim(pe, ("xT", k, part))
                    for t in range(n):
                        ins = tr(b[:, P * t:P * (t + 1)], x_raw[:, t0 + t, P * k:P * (k + 1)], ident)
                    full(ins, ("xT", k, part))

            def ada_piece(i, key, col, last):
                pe.wait_ge(ada_in[i % 3], 16 * (i // 3 + 1))
                b = bank[turns[key][0]]
                for k in range(KT):
                    for j in range(4):
                        ins = mm(b[32 * j:32 * j + 2, col:col + P], scT[:, k:k + 9:8],
                                 ada_buf[i % 3][:, k, P * j:P * (j + 1)], start=(k == 0), stop=(k == KT - 1),
                                 skip_group_check=True)
                full(ins, key) if last else ins.then_inc(ada_used, 1)

            def ada(key, bank_first, first, n):
                for i in range(first, first + n):
                    if i == bank_first:
                        claim(pe, key)
                    ada_piece(i, key, P * (i - bank_first), i == bank_first + 3)

            def mod_columns(key, first, n):
                b = claim(pe, key)
                for i in range(n):
                    ins = mm(b[:, 8 * i:8 * i + 8], mod_rows[:, P * (first + i):P * (first + i + 1)], sel8,
                             start=True, stop=True)
                full(ins, key)

            pe.wait_ge(silu_c, 1)
            ada("ada_a", 0, 0, ADA_FIRST)
            emptied(pe, "ada_a")
            mod_columns("mod_a", 0, ADA_FIRST)

            def project_dt():
                pe.wait_ge(w_dt_in, 16)
                b = claim(pe, "dt")
                for t in range(TT):
                    for k in range(KT):
                        ins = mm(b[:, DT_W * t:DT_W * (t + 1)], hT[:, k, P * t:P * (t + 1)], w_dt[:, k],
                                 start=(k == 0), stop=(k == KT - 1))
                full(ins, "dt")

            def cumulative_sums():
                pe.wait_ge(dt_ready, 1)
                b = claim(pe, "cum")
                bv = b[:, 0:TT * 48].rearrange("p (t h) -> p t h", t=TT)
                mm(bv[:, :, 0:24], tri_f, dtmp[0][:, :, 0:24], start=True, stop=True)
                full(mm(bv[:, :, 24:48], tri_b, dtmp[0][:, :, 24:48], start=True, stop=True), "cum")
                b = claim(pe, "tot")
                full(mm(b[:, 0:TT * 48].rearrange("p (t h) -> p t h", t=TT), ones, dtmp[0], start=True, stop=True),
                     "tot")

            def sums_as_rows():
                emptied(pe, "cum")
                b = claim(pe, "rows")
                for t in range(LT):
                    a = tr(b[0:48, P * t:P * (t + 1)], cum[:, CT + t], ident)
                full(a, "rows")

            def w_view(q, width):
                return w_buf[q % 2][:, 0:KT * width].rearrange("p (k c) -> p k c", k=KT)

            def w_wait(q):
                n = sum(32 if (p % 3 == 0 and p < 3 * GROUPS) else 16 for p in range(q % 2, q + 1, 2))
                pe.wait_ge(w_in_sem[q % 2], n)

            def project_channels(r, i):
                n = 5 * r + i
                q, width, col = (3 * r, 256, P * i) if i < 2 else (3 * r + 1, GW, P * (i - 2))
                w_wait(q)
                lat, cx = claim(pe, ("in", n, 0)), claim(pe, ("in", n, 1))
                w = w_view(q, width)
                for k in range(KT):
                    if n == 0:
                        pe.wait_ge(hmod, 2 * k + 2)
                    a = mm(lat[:], w[:, k, col:col + P], hT[:, k, CTX:TOK], start=(k == 0), stop=(k == KT - 1))
                    if k == KT - 1:
                        full(a, ("in", n, 0))
                for k in range(KT):
                    a = mm(cx[:, 0:CTX], w[:, k, col:col + P], hT[:, k, 0:CTX], start=(k == 0), stop=(k == KT - 1))
                full(a, ("in", n, 1))

            def project_z(r):
                q = 3 * r + 2
                w_wait(q)
                w = w_view(q, GW)
                for t in range(LT):
                    b = claim(pe, ("z", r, t))
                    for k in range(KT):
                        a = mm(b[:, 0:GW], hT[:, k, CTX + P * t:CTX + P * (t + 1)], w[:, k], start=(k == 0),
                               stop=(k == KT - 1))
                    full(a, ("z", r, t))

            def project_u(i):
                q = 3 * GROUPS + i // 2
                w_wait(q)
                w = w_view(q, 256)
                b = claim(pe, ("u", i))
                for k in range(KT):
                    a = mm(b[:], w[:, k, P * (i % 2):P * (i % 2 + 1)], hT[:, k, CTX:TOK], start=(k == 0),
                           stop=(k == KT - 1))
                full(a, ("u", i))

            def channel_dft():
                emptied(pe, ("u", FT - 1))
                emptied(pe, ("u", FT - 2))
                emptied(pe, "fourier_w")
                for t in range(LT):
                    for j in range(FT):
                        key = ("v", t, j // 2)
                        if j % 2 == 0:
                            b = claim(pe, key)
                        a = mm(b[:, 256 * (j % 2):256 * (j % 2 + 1)], uT[:, j, P * t:P * (t + 1)], fw[:, j],
                               start=True, stop=True)
                        if j % 2:
                            full(a, key)

            def position_dft():
                for t in range(LT):
                    for h in range(2):
                        emptied(pe, ("v", t, h))
                bs = [claim(pe, ("f", j)) for j in range(FT)]
                for t in range(LT):
                    pe.wait_ge(dft_in[t % 2], 16 * (t // 2 + 1))
                    for j in range(FT):
                        for s in range(2):
                            a = mm(bs[j][:], vf[:, t, j, P * s:P * (s + 1)], dft_buf[t % 2][:, s],
                                   start=(t == 0 and s == 0), stop=(t == LT - 1 and s == 1))
                        if t == LT - 1:
                            full(a, ("f", j))
                        elif j == FT - 1:
                            a.then_inc(dft_used, 1)

            def to_tokens(r, s):
                n = 5 * r + s
                src = bc_ch[r % 2][0] if s == 0 else conv_acc[n % 2]
                pe.wait_ge(tile_done, n + 1)
                for part, (t0, m) in enumerate(((CT, LT), (0, CT))):
                    b = claim(pe, ("T", r, s, part))
                    for t in range(m):
                        a = tr(b[:, P * t:P * (t + 1)], chan(src, t0 + t), ident)
                    full(a, ("T", r, s, part))

            def states(g):
                for s in (0, 2, 3, 4):
                    emptied(pe, ("T", g, s, 0))
                    emptied(pe, ("T", g, s, 1))
                for k in range(STEPS):
                    pe.wait_ge(xw_ready, STEPS * g + k + 1)
                    for d in range(2):
                        b = claim(pe, ("state", g, k, d))
                        full(mm(b[:, 0:GW], tok[g % 2][:, STEP_TILE[d][k], 0:P], xw[:, k % 2, d], start=True,
                                stop=True), ("state", g, k, d))

            def unit_pre(v):
                g, ch = divmod(v, LT)
                bm, cm = (chan(bc_ch[g % 2][j], CT + ch) for j in range(2))
                pe.wait_ge(tile_done, 5 * g + 2)
                b = claim(pe, ("cb", v))
                full(mm(b[:, 0:P], bm, cm, start=True, stop=True), ("cb", v))
                pe.wait_ge(state_ready, STEPS * (g + 1))
                for d in range(2):
                    b = claim(pe, ("off", v, d))
                    full(mm(b[:, 0:GW], cm, hp[d][:, ch if d == 0 else LT - 1 - ch], start=True, stop=True),
                         ("off", v, d))

            def unit_post(v):
                emptied(pe, ("cb", v))
                pe.wait_ge(xdt_ready, v + 1)
                b = claim(pe, ("diag", v))
                for h in range(HG):
                    for d in range(2):
                        a = mm(b[:, HD * h:HD * (h + 1)], seg[v % 2][:, d, h], xdt[v % 2][:, d, HD * h:HD * (h + 1)],
                               start=(d == 0), stop=(d == 1))
                full(a, ("diag", v))

            def unit_fin(v):
                pe.wait_ge(y_ready, v + 1)
                b = claim(pe, ("y", v))
                for j in range(XT):
                    a = tr(b[:, P * j:P * (j + 1)], yb[v % 2][:, 0, P * j:P * (j + 1)], ident)
                full(a, ("y", v))

            for r in range(GROUPS + 1):
                g = r - 1
                for i in range(6):
                    if r < GROUPS:
                        project_channels(r, i) if i < 5 else project_z(r)
                    elif i < FT:
                        project_u(i)
                    elif i == FT:
                        channel_dft()
                    if r < GROUPS and i in TOKENS_AT:
                        to_tokens(r, TOKENS_AT[i])
                    if r == 0 and i == 0:
                        project_dt()
                    elif r == 0 and i == 1:
                        ada("ada_b", 4, 4, 2)
                        cumulative_sums()
                    elif r == 0 and i == 2:
                        sums_as_rows()
                        ada("ada_b", 4, 6, 2)
                    elif r == 0 and i == 3:
                        ada("ada_c", 8, 8, 2)
                    elif r == 0 and i == 4:
                        ada("ada_c", 8, 10, 2)
                    elif r == 0:
                        emptied(pe, "ada_b")
                        emptied(pe, "ada_c")
                        mod_columns("mod_b", 4, 8)
                    if g >= 0:
                        if i == 0:
                            if g > 0:
                                unit_fin(4 * g - 1)
                            states(g)
                        if i >= 3:
                            unit_fin(4 * g + i - 3)
                        if i >= 2:
                            unit_post(4 * g + i - 2)
                        if 1 <= i <= 4:
                            unit_pre(4 * g + i - 1)
            position_dft()
            unit_fin(UNITS - 1)

            def route_transpose(t):
                pe.wait_ge(h2_ready, t + 1)
                for h in range(2):
                    b = claim(pe, ("nT", t, h))
                    for k in range(4):
                        a = tr(b[:, P * k:P * (k + 1)], h2[:, t, P * (4 * h + k):P * (4 * h + k + 1)], ident)
                    full(a, ("nT", t, h))

            def route_logits(t):
                if t == 0:
                    pe.wait_ge(router_in, 16)
                    claim(pe, "logits")
                for h in range(2):
                    emptied(pe, ("nT", t, h))
                for k in range(KT):
                    a = mm(bank[0][:, EXPERTS * t:EXPERTS * (t + 1)], nT[t % 2][:, k], router_w[:, k],
                           start=(k == 0), stop=(k == KT - 1))
                if t == LT - 1:
                    full(a, "logits")

            for p in range(2):
                bs = {(t, h): claim(pe, ("out", t, h)) for t in (2 * p, 2 * p + 1) for h in range(2)}
                for k in range(16):
                    n, row = 16 * p + k, WO_ORDER[k]
                    if p == 0 and k == 0:
                        for u in range(LT * (GROUPS - 1)):
                            emptied(pe, ("y", u))
                    elif p == 0 and row == 0:
                        for j in range(FT):
                            emptied(pe, ("f", j))
                    elif p == 0 and row == FT + XT * (GROUPS - 1):
                        for u in range(LT * (GROUPS - 1), UNITS):
                            emptied(pe, ("y", u))
                    pe.wait_ge(wo_in[n % WO_SLOTS], 16 * (n // WO_SLOTS + 1))
                    for t in (2 * p, 2 * p + 1):
                        lhs = fT[:, row, P * t:P * (t + 1)] if row < FT else yT[:, row - FT, P * t:P * (t + 1)]
                        for h in range(2):
                            a = mm(bs[t, h][:], lhs, wo_buf[n % WO_SLOTS][:, 512 * h:512 * (h + 1)], start=(k == 0),
                                   stop=(k == 15))
                            if k == 15:
                                full(a, ("out", t, h))
                    if k < 15:
                        a.then_inc(wo_used, 1)
                    if p == 1 and k in (5, 10):
                        route_transpose(k // 10)
                    elif p == 1 and k in (6, 11):
                        route_logits(k // 11)
            route_transpose(2)
            route_transpose(3)
            route_logits(2)
            route_logits(3)
            pe.wait_ge(probs_ready, 1)
            b = claim(pe, "probsT")
            for t in range(LT):
                a = tr(b[0:EXPERTS, P * t:P * (t + 1)], probs[:, t], ident)
            full(a, "probsT")
            pe.wait_ge(slots_ready, 1)
            b = claim(pe, "slotT")
            for t in range(LT):
                a = tr(b[:, EXPERTS * t:EXPERTS * (t + 1)], slot1[0:EXPERTS, P * t:P * (t + 1)],
                       ident[0:EXPERTS, 0:EXPERTS])
            full(a, "slotT")
            pe.wait_ge(h2_ready, LT)
            with pe.Fori(0, EXPERTS) as e:
                pe.wait_ge(sel_ready, e + 1)
                pe.wait_ge(e_free[4], 2 * e + 1)
                for k in range(KT):
                    for t in range(LT):
                        a = mm(bank[4][:, CAP * k:CAP * (k + 1)], h2[:, t, P * k:P * (k + 1)], sel[:, t],
                               start=(t == 0), stop=(t == LT - 1))
                a.then_inc(e_full[4], 1)
                pe.wait_ge(selw_ready, e + 1)
                pe.wait_ge(e_free[5], 2 * e + 1)
                for t in range(LT):
                    a = tr(bank[5][:, P * t:P * (t + 1)], sel_w[:, t].rearrange("p a b -> p (a b)"), ident)
                a.then_inc(e_full[5], 1)
                pe.wait_ge(e_free[4], 2 * e + 2)
                for b in range(4):
                    pe.wait_ge(e_free[b], e + 1)
                for ch in range(16):
                    k, which = divmod(ch, 2)
                    pe.wait_ge(ring_in[ch % RING], (e * 2 + (ch // RING + 1)) * 16)
                    for n in range(2):
                        for h in range(2):
                            a = mm(bank[2 * which + n][CAP * h:CAP * (h + 1), :], xgT[:, k],
                                   ring[ch % RING][:, 1024 * h + 512 * n:1024 * h + 512 * (n + 1)], start=(k == 0),
                                   stop=(k == KT - 1), skip_group_check=True)
                    if k < KT - 1:
                        a.then_inc(ring_used, 1)
                    else:
                        a.then_inc(e_full[2 * which + 1], 1)
                for n in range(2):
                    pe.wait_ge(act_ready, 2 * e + n + 1)
                    pe.wait_ge(e_free[6 + n], 3 * e + 1)
                    for j in range(4):
                        a = tr(bank[6 + n][:, P * j:P * (j + 1)], act_e[:, 512 * n + P * j:512 * n + P * (j + 1)],
                               ident)
                    a.then_inc(e_full[6 + n], 1)
                pe.wait_ge(e_free[5], 2 * e + 2)
                for j in range(8):
                    ch = 16 + j
                    pe.wait_ge(ring_in[ch % RING], (e * 2 + 2) * 16)
                    if j % 4 == 0:
                        pe.wait_ge(e_free[6 + j // 4], 3 * e + 2)
                    for n in range(2):
                        for h in range(2):
                            a = mm(bank[4 + n][CAP * h:CAP * (h + 1), :],
                                   actT[:, P * j + CAP * h:P * j + CAP * (h + 1)],
                                   ring[ch % RING][:, D * h + 512 * n:D * h + 512 * (n + 1)], start=(j == 0),
                                   stop=(j == 7), skip_group_check=True)
                    if j < 7:
                        a.then_inc(ring_used, 1)
                    else:
                        a.then_inc(e_full[5], 1)
                for n in range(2):
                    pe.wait_ge(e_free[4 + n], 2 * e + 3)
                for i in range(8):
                    t, n = divmod(i, 2)
                    b = (6, 7, 0, 1, 2, 3, 6, 7)[i]
                    if b >= 6:
                        pe.wait_ge(e_free[b], 3 * e + 2 + i // 6)
                    mm(bank[b][:], scatter[:, P * t:P * (t + 1)], y_e[:, 512 * n:512 * (n + 1)], start=True,
                       stop=True).then_inc(e_full[b], 1)

        @block.vector
        def _(v_):
            v = v_
            step = Chain(v, dve)
            tt, ts, stt, cp = v.tensor_tensor, v.tensor_scalar, v.scalar_tensor_tensor, v.tensor_copy

            step(v.memset(mod_rows, 0.0))
            for s in range(2):
                for o in (0, LAT0, CONV_IN - PAD):
                    step(v.memset(conv_in[s][:, o:o + PAD], 0.0))
            v.memset(fw, 0.0).then_inc(pads_zero, 1)
            v.wait_ge(pads_zero, 1)
            for t in range(TT):
                v.wait_ge(rstd_x, t + 1)
                ts(x_raw[:, t], x_raw[:, t], stat[:, t:t + 1], None, ALU.mult).then_inc(xn_done, 1)
            b = filled(v, "columns")
            cp(cols_a, b[:, 0:64])
            free(cp(cols_b, b[:, 64:164]), "columns")
            b = filled(v, "fourier_w")
            for s in range(2):
                for h in range(2):
                    src = b[CAP * h:CAP * (h + 1), 256 * s:256 * (s + 1)].rearrange("p (j c) -> p j c", j=FT)
                    ins = cp(fw[CAP * h:CAP * (h + 1), :, P * s + F_GROUP * h:P * s + F_GROUP * (h + 1)], src)
            free(ins, "fourier_w")
            for k in range(KT):
                b = filled(v, ("xT", k, 1))
                free(cp(hT[:, k, 0:CTX], b[:, 0:CTX]), ("xT", k, 1))

            def mod_evac(key, first, n):
                b = filled(v, key)
                for j in range(4):
                    q = slice(32 * j, 32 * j + 2)
                    ins = tt(mod_rows[q, P * first:P * (first + n)], b[q, 0:P * n],
                             ada_rows_b[q, P * first:P * (first + n)], ALU.add)
                free(ins, key)

            v.wait_ge(ada_b_in, 32)
            mod_evac("ada_a", 0, ADA_FIRST)
            b = filled(v, "mod_a")
            free(cp(modc[:, 0:16], b[:, 0:32].rearrange("p (m w) -> p m w", w=2)), "mod_a")
            emptied(v, "mod_a")
            emptied(v, "columns")
            step(stt(a1, modc[:, 8:16], 1.0, n1w.unsqueeze(2).to_broadcast([P, 8, 2]), ALU.add, ALU.mult))
            for k in range(KT):
                emptied(v, ("xT", k, 0))
                emptied(v, ("xT", k, 1))
                for part, sl in ((0, slice(CTX, TOK)), (1, slice(0, CTX))):
                    ts(hT[:, k, sl], hT[:, k, sl], a1[:, k, part:part + 1], modc[:, k, part:part + 1], ALU.mult,
                       ALU.add).then_inc(hmod, 1)

            def dt_chain():
                b = filled(v, "dt")
                raw, e_, u_ = dtmp
                bv = b[:, 0:TT * DT_W].rearrange("p (t h) -> p t h", t=TT)[:, :, DT_W - 48:]
                step_free = tt(raw, bv, dtb.unsqueeze(1).to_broadcast([P, TT, 48]), ALU.add)
                free(step_free, "dt")
                emptied(v, "dt")
                stt(e_, raw, -1.0, raw, ALU.mult, ALU.max).then_inc(exp_small, 1)
                v.wait_ge(small_exped, 2)
                step(ts(u_, e_, 1.0, None, ALU.add))
                cp(cum, u_).then_inc(exp_small, 1)
                v.wait_ge(exp_small, 2)
                step(ts(u_, u_, -1.0, None, ALU.add))
                step(tt(e_, e_, u_, ALU.subtract))
                step(ts(raw, raw, 0.0, None, ALU.max))
                step(v.reciprocal(u_, cum))
                step(tt(e_, e_, u_, ALU.mult))
                v.wait_ge(small_exped, 3)
                step(tt(e_, e_, dt, ALU.add))
                step(tt(dt, e_, raw, ALU.add))
                stt(dtmp[0], dt, -1.0, abc.unsqueeze(1).to_broadcast([P, TT, 48]), ALU.mult, ALU.mult
                    ).then_inc(dt_ready, 1)

            def cumulative_sums():
                bcum = filled(v, "cum")
                free(cp(cum, bcum[:, 0:TT * 48].rearrange("p (t h) -> p t h", t=TT)), "cum")
                btot = filled(v, "tot")
                free(cp(dtmp[1], btot[:, 0:TT * 48].rearrange("p (t h) -> p t h", t=TT)), "tot")
                emptied(v, "cum")
                emptied(v, "tot")
                tt(dtmp[2], dtmp[1], cum, ALU.subtract).then_inc(exp_small, 1)
                v.wait_ge(small_exped, 6)
                tt(toend, toend, dt, ALU.mult).then_inc(cum_ready, 1)

            def sums_as_rows():
                b = filled(v, "rows")
                v.wait_ge(cum_ready, 1)
                free(cp(cum_rows[0:48, :], b[0:48, :]), "rows")
                emptied(v, "rows")
                v.sem_inc(rows_ready, 1)

            def conv(r, i):
                n = 5 * r + i
                ct = TILE_OF(r, i)
                emptied(v, ("in", n, 0))
                emptied(v, ("in", n, 1))
                src, acc = conv_in[n % 2], conv_acc[n % 2]
                if n >= 2:
                    v.wait_ge(tile_done, n - 1)
                    pr, pi = divmod(n - 2, 5)
                    if pi >= 2:
                        filled(v, ("T", pr, pi, 1))
                step(ts(acc, src[:, 0:CONV_OUT], cols_b[:, ct:ct + 1], cb_col[:, ct:ct + 1], ALU.mult, ALU.add))
                for k in range(1, CONV):
                    col = CONV_TILES * k + ct
                    ins = stt(acc, src[:, k:k + CONV_OUT], cols_b[:, col:col + 1], acc, ALU.mult, ALU.add)
                    if k < CONV - 1:
                        step(ins)
                ins.then_inc(conv_done, 1)

            def state_updates(g):
                for k in range(STEPS):
                    for d in range(2):
                        t = STEP_TILE[d][k]
                        dec = head_bc(decay[:, t, HEADS * d + HG * g:HEADS * d + HG * (g + 1)])
                        dst = hp[d][:, max(k - 1, 0)]
                        if k:
                            src = hp[d][:, max(k - 2, 0)]
                            v.wait_ge(state_ready, STEPS * g + k)
                            step(tt(heads(st_tmp[:, d]), heads(src), dec, ALU.mult))
                        b = filled(v, ("state", g, k, d))
                        if k:
                            ins = tt(dst, b[:, 0:GW], st_tmp[:, d], ALU.add)
                        else:
                            ins = cp(dst, b[:, 0:GW])
                        free(ins, ("state", g, k, d))
                    emptied(v, ("state", g, k, 0))
                    emptied(v, ("state", g, k, 1))
                    v.sem_inc(state_ready, 1)

            def unit_segments(u):
                g, ch = divmod(u, LT)
                v.wait_ge(seg_in[u % 2], 32 * (u // 2 + 1))
                for d in range(2):
                    col = HEADS * d + HG * g
                    ins = tt(seg[u % 2][:, d], seg[u % 2][:, d], head_bc(cum[:, CT + ch, col:col + HG], P),
                             ALU.subtract)
                ins.then_inc(seg_ready, 1)

            def unit_weights(u):
                g, ch = divmod(u, LT)
                v.wait_ge(decays, u + 1)
                b = filled(v, ("cb", u))
                for d in range(2):
                    ins = tt(seg[u % 2][:, d], seg[u % 2][:, d], b[:, 0:P].unsqueeze(1).to_broadcast([P, HG, P]),
                             ALU.mult)
                free(ins, ("cb", u))
                for d in range(2):
                    b = filled(v, ("off", u, d))
                    if u >= 2:
                        filled(v, ("y", u - 2))
                    col = HEADS * d + HG * g
                    free(tt(heads(yb[u % 2][:, d]), heads(b[:, 0:GW]), head_bc(ecum[:, CT + ch, col:col + HG]),
                            ALU.mult), ("off", u, d))

            def unit_gate(u):
                g, ch = divmod(u, LT)
                y = yb[u % 2][:, 0]
                v.wait_ge(offs_summed, u + 1)
                b = filled(v, ("diag", u))
                free(tt(y, y, b[:, 0:GW], ALU.add), ("diag", u))
                emptied(v, ("diag", u))
                emptied(v, ("z", g, ch))
                tt(y, y, zs[g % 2][:, ch], ALU.mult).then_inc(gated, 1)

            def unit_norm(u):
                v.wait_ge(rstd_y, u + 1)
                c_ = 16 + u % 2
                ts(yb[u % 2][:, 0], yb[u % 2][:, 0], stat[:, c_:c_ + 1], None, ALU.mult).then_inc(y_ready, 1)

            for r in range(GROUPS + 1):
                g = r - 1
                for i in range(6):
                    if g >= 0 and i == 0:
                        if g == 0:
                            v.wait_ge(cum_out, 16)
                        else:
                            unit_norm(4 * g - 1)
                        unit_segments(4 * g)
                        state_updates(g)
                    elif g >= 0 and i >= 3:
                        unit_norm(4 * g + i - 3)
                    if r < GROUPS and i < 5:
                        conv(r, i)
                    if r == GROUPS and i == FT:
                        for t in range(LT):
                            b = filled(v, ("v", t, 1))
                            free(cp(vf[:, t, 2:4], b[:].rearrange("p (j c) -> p j c", j=2)), ("v", t, 1))
                    if r == 0 and i == 0:
                        dt_chain()
                    elif r == 0 and i == 1:
                        cumulative_sums()
                    elif r == 0 and i == 2:
                        sums_as_rows()
                        mod_evac("ada_b", 4, 4)
                    elif r == 0 and i == 4:
                        mod_evac("ada_c", 8, 4)
                    elif r == 0 and i == 5:
                        b = filled(v, "mod_b")
                        free(cp(modc[:, 16:48], b[:, 0:64].rearrange("p (m w) -> p m w", w=2)), "mod_b")
                    if g >= 0:
                        if i >= 2:
                            unit_gate(4 * g + i - 2)
                        if 1 <= i <= 4:
                            unit_weights(4 * g + i - 1)
                            if i < 4:
                                unit_segments(4 * g + i)
            unit_norm(UNITS - 1)
            for j in (2, 3):
                b = filled(v, ("f", j))
                free(cp(fT[:, j], b[:]), ("f", j))

            v.wait_ge(res_in, 16)
            v.wait_ge(mod_bc_in, 16 * 5)
            step(stt(rowbc["scale2"], rowbc["scale2"], 1.0, norm2_bc, ALU.add, ALU.mult))

            def residual(t):
                for h in range(2):
                    sl = slice(512 * h, 512 * (h + 1))
                    b = filled(v, ("out", t, h))
                    if t:
                        v.wait_ge(x1_ready, 2 * t + h - 1)
                    free(tt(out_tmp[:, h], b[:], rowbc["gate1"][:, sl], ALU.mult), ("out", t, h))
                    emptied(v, ("out", t, h))
                    tt(x1[:, t, sl], x1[:, t, sl], out_tmp[:, h], ALU.add).then_inc(x1_ready, 1)

            def second_norm(t):
                v.wait_ge(rstd_x1, t + 1)
                step(stt(h2[:, t], x1[:, t], stat[:, t:t + 1], rowbc["scale2"], ALU.mult, ALU.mult))
                tt(h2[:, t], h2[:, t], rowbc["shift2"], ALU.add).then_inc(h2_ready, 1)

            def copy_nT(t):
                b = filled(v, ("nT", t, 1))
                free(cp(nT[t % 2][:, 4:8], b[:].rearrange("p (k c) -> p k c", k=4)), ("nT", t, 1))

            for t in range(LT // 2):
                residual(t)
                second_norm(t)
            copy_nT(0)
            copy_nT(1)
            residual(2)
            second_norm(2)
            residual(3)
            copy_nT(2)
            second_norm(3)
            copy_nT(3)
            b = filled(v, "logits")
            logits = b[:, 0:64].rearrange("p (t e) -> p t e", t=LT)
            step(v.tensor_reduce(rowmax, logits, AX_X, ALU.max))
            free(tt(lg, logits, rowmax.unsqueeze(2).to_broadcast([P, LT, EXPERTS]), ALU.subtract), "logits")
            v.wait_ge(exped, 1)
            step(v.tensor_reduce(rowsum, probs, AX_X, ALU.add))
            step(v.reciprocal(rowsum, rowsum))
            tt(probs, probs, rowsum.unsqueeze(2).to_broadcast([P, LT, EXPERTS]), ALU.mult).then_inc(probs_ready, 1)
            b = filled(v, "probsT")
            free(cp(pT[0:EXPERTS], b[0:EXPERTS, :]), "probsT")
            emptied(v, "probsT")
            for _ in range(CAP // 8):
                step(v.max(top8[0:EXPERTS], pT[0:EXPERTS]))
                step(v.match_replace(pT[0:EXPERTS], top8[0:EXPERTS], pT[0:EXPERTS], -1.0))
            step(ts(mask[0:EXPERTS], pT[0:EXPERTS], 0.0, None, ALU.is_lt))
            step(v.tensor_tensor_scan(cums[0:EXPERTS], ones[0:EXPERTS, 0:1].to_broadcast([EXPERTS, SEQ]),
                                      mask[0:EXPERTS], 0.0, ALU.mult, ALU.add))
            tt(slot1[0:EXPERTS], cums[0:EXPERTS], mask[0:EXPERTS], ALU.mult).then_inc(slots_ready, 1)
            b = filled(v, "slotT")
            free(cp(slotT, b[:, 0:64].rearrange("p (t e) -> p t e", t=LT)), "slotT")
            emptied(v, "slotT")
            for b in range(8):
                v.wait_ge(bank_free[b], uses[b])
                v.sem_inc(e_free[b], 1)
            with v.Fori(0, EXPERTS) as e:
                one = slotT[:, :, bass.ds(e, 1)].to_broadcast([P, LT, CAP])
                tt(sel, iota1.unsqueeze(1).to_broadcast([P, LT, CAP]), one, ALU.is_equal).then_inc(sel_ready, 1)
                v.wait_ge(sel_ready, e + 1)
                for h in range(2):
                    ins = tt(sel_w[:, :, h], sel, probs[:, :, bass.ds(e, 1)].to_broadcast([P, LT, CAP]), ALU.mult)
                ins.then_inc(selw_ready, 1)
                v.wait_ge(e_full[4], e + 1)
                cp(xgT, bank[4][:].rearrange("p (k c) -> p k c", k=KT)).then_inc(e_free[4], 1)
                v.wait_ge(e_full[3], 2 * e + 1)
                for n in range(2):
                    v.wait_ge(silu_ready, 2 * e + n + 1)
                    tt(act_e[:, 512 * n:512 * (n + 1)], silu_g[:, 512 * n:512 * (n + 1)], bank[2 + n][:], ALU.mult
                       ).then_inc(act_ready, 1)
                v.wait_ge(e_full[5], 2 * e + 2)
                tt(y_e[:, 0:512], bank[4][:], gate2[:, 0:512], ALU.mult).then_inc(e_free[4], 1)
                tt(y_e[:, 512:1024], bank[5][:], gate2[:, 512:1024], ALU.mult).then_inc(e_free[5], 1)
                for i in range(8):
                    t, n = divmod(i, 2)
                    b = (6, 7, 0, 1, 2, 3, 6, 7)[i]
                    if b >= 6:
                        v.wait_ge(e_full[b], 3 * e + 2 + i // 6)
                    elif b in (1, 3):
                        v.wait_ge(e_full[b], 2 * e + 2)
                    else:
                        v.wait_ge(e_full[b], e + 1)
                    sl = slice(512 * n, 512 * (n + 1))
                    tt(x1[:, t, sl], x1[:, t, sl], bank[b][:], ALU.add).then_inc(e_free[b], 1)
            v.wait_ge(final_in, 16)
            for t in range(LT):
                v.wait_ge(rstd_x2, t + 1)
                stt(out_rows[:, t], x1[:, t], stat[:, t:t + 1], final_bc, ALU.mult, ALU.mult).then_inc(out_ready, 1)

        @block.scalar
        def _(act):
            ac = act.activation

            for t in range(TT):
                act.wait_ge(ctx_in if t < CT else lat_in, 16)
                ac(hT.rearrange("p k t -> p (k t)")[:, D * t:D * (t + 1)], x_raw[:, t], ACT.Square,
                   accum_out=stat[:, 8 + t:9 + t]).then_inc(square_done, 1)
            act.wait_ge(square_done, TT)
            emptied(act, "columns")
            ac(scT, cols_a[:, 48:64], ACT.Silu).then_inc(silu_c, 1)
            for k in range(KT):
                b = filled(act, ("xT", k, 0))
                free(ac(hT[:, k, CTX:TOK], b[:], ACT.Copy), ("xT", k, 0))

            def evac_in(r, i):
                n = 5 * r + i
                if n >= 2:
                    act.wait_ge(conv_done, n - 1)
                if n < 2:
                    act.wait_ge(pads_zero, 1)
                b = filled(act, ("in", n, 0))
                free(ac(conv_in[n % 2][:, PAD + LAT0:PAD + LAT0 + SEQ], b[:], ACT.Copy), ("in", n, 0))
                b = filled(act, ("in", n, 1))
                free(ac(conv_in[n % 2][:, PAD:PAD + CTX], b[:, 0:CTX], ACT.Copy), ("in", n, 1))

            def silu_tile(r, i):
                n = 5 * r + i
                act.wait_ge(conv_done, n + 1)
                dst = bc_ch[r % 2][i] if i < 2 else conv_acc[n % 2]
                ac(dst, conv_acc[n % 2], ACT.Silu).then_inc(tile_done, 1)

            def evac_tokens(r, s):
                o = 0 if s == 0 else P * (s - 1)
                for part, (t0, m) in enumerate(((CT, LT), (0, CT))):
                    b = filled(act, ("T", r, s, part))
                    free(ac(tok[r % 2][:, t0:t0 + m, o:o + P], b[:, 0:P * m].rearrange("p (t c) -> p t c", t=m),
                            ACT.Copy), ("T", r, s, part))

            def dt_chain():
                act.wait_ge(exp_small, 1)
                ac(dtmp[1], dtmp[1], ACT.Exp, scale=-1.0).then_inc(small_exped, 1)
                ac(abc, abc, ACT.Exp).then_inc(small_exped, 1)
                act.wait_ge(exp_small, 2)
                ac(dt, cum, ACT.Ln).then_inc(small_exped, 1)

            def exp_of_sums():
                act.wait_ge(exp_small, 3)
                ac(toend, dtmp[2], ACT.Exp).then_inc(small_exped, 1)
                ac(decay, dtmp[1], ACT.Exp).then_inc(small_exped, 1)
                ac(ecum, cum, ACT.Exp).then_inc(small_exped, 1)

            def unit_exp(u):
                act.wait_ge(masked, u + 1)
                w = seg[u % 2].rearrange("p d h l -> p (d h l)")
                ac(w, w, ACT.Exp).then_inc(decays, 1)

            def unit_square(u):
                act.wait_ge(gated, u + 1)
                act.wait_ge(offs_summed, u + 1)
                ac(yb[u % 2][:, 1], yb[u % 2][:, 0], ACT.Square, accum_out=stat[:, 18 + u % 2:19 + u % 2]
                   ).then_inc(squared, 1)

            def unit_evac(u):
                g, ch = divmod(u, LT)
                b = filled(act, ("y", u))
                for j in range(XT):
                    ins = ac(yT[:, XT * g + j, P * ch:P * (ch + 1)], b[:, P * j:P * (j + 1)], ACT.Identity,
                             bias=0.0, scale=ssm_col[:, XT * g + j:XT * g + j + 1])
                free(ins, ("y", u))

            for r in range(GROUPS + 1):
                g = r - 1
                for i in range(6):
                    if r < GROUPS and i < 5:
                        evac_in(r, i)
                    elif r < GROUPS:
                        for t in range(LT):
                            b = filled(act, ("z", r, t))
                            free(ac(zs[r % 2][:, t], b[:, 0:GW], ACT.Silu), ("z", r, t))
                    elif i < FT:
                        act.wait_ge(mod_out, 16)
                        b = filled(act, ("u", i))
                        free(ac(uT[:, i], b[:], ACT.Copy), ("u", i))
                    elif i == FT:
                        for t in range(LT):
                            b = filled(act, ("v", t, 0))
                            free(ac(vf[:, t, 0:2], b[:].rearrange("p (j c) -> p j c", j=2), ACT.Copy), ("v", t, 0))
                    if r < GROUPS and i in TOKENS_AT:
                        evac_tokens(r, TOKENS_AT[i])
                    if g > 0 and i == 0:
                        unit_evac(4 * g - 1)
                    if g >= 0 and i >= 3:
                        unit_evac(4 * g + i - 3)
                    if g >= 0 and 1 <= i <= 4:
                        unit_exp(4 * g + i - 1)
                    if r < GROUPS and i < 5:
                        silu_tile(r, i)
                    if r == 0 and i == 0:
                        dt_chain()
                    elif r == 0 and i == 1:
                        exp_of_sums()
                    if g >= 0 and i >= 2:
                        unit_square(4 * g + i - 2)
            for j in (0, 1):
                b = filled(act, ("f", j))
                free(ac(fT[:, j], b[:], ACT.Copy), ("f", j))
            unit_evac(UNITS - 1)

            def square_x1(t):
                act.wait_ge(x1_ready, 2 * t + 2)
                ac(h2[:, t], x1[:, t], ACT.Square, accum_out=stat[:, 8 + t:9 + t]).then_inc(x1_squared, 1)

            def copy_nT(t):
                b = filled(act, ("nT", t, 0))
                free(ac(nT[t % 2][:, 0:4], b[:].rearrange("p (k c) -> p k c", k=4), ACT.Copy), ("nT", t, 0))

            for t in range(LT // 2):
                square_x1(t)
            copy_nT(0)
            copy_nT(1)
            square_x1(2)
            square_x1(3)
            copy_nT(2)
            copy_nT(3)
            emptied(act, "logits")
            ac(probs, lg, ACT.Exp).then_inc(exped, 1)
            with act.Fori(0, EXPERTS) as e:
                act.wait_ge(e_full[5], 2 * e + 1)
                ac(scatter, bank[5][:], ACT.Copy).then_inc(e_free[5], 1)
                act.wait_ge(e_full[1], 2 * e + 1)
                for n in range(2):
                    ac(silu_g[:, 512 * n:512 * (n + 1)], bank[n][:], ACT.Silu).then_inc(silu_ready, 1)
                for n in range(2):
                    act.wait_ge(e_full[6 + n], 3 * e + 1)
                    ac(actT[:, 512 * n:512 * (n + 1)], bank[6 + n][:], ACT.Copy).then_inc(e_free[6 + n], 1)
            for t, (b, n) in enumerate(((6, 3 * EXPERTS), (0, EXPERTS + 1), (2, EXPERTS + 1), (6, 3 * EXPERTS + 1))):
                act.wait_ge(e_free[b], n)
                act.wait_ge(e_free[b + 1], n)
                ac(out_rows[:, t], x1[:, t], ACT.Square, accum_out=stat[:, 8 + t:9 + t]).then_inc(x2_squared, 1)

        @block.gpsimd
        def _(gp):
            step = Chain(gp, pool)
            tt = gp.tensor_tensor

            def state_inputs(g):
                for s in (0, 2, 3, 4):
                    emptied(gp, ("T", g, s, 0))
                    emptied(gp, ("T", g, s, 1))
                for k in range(STEPS):
                    if k >= 2:
                        filled(gp, ("state", g, k - 2, 1))
                    for d in range(2):
                        t = STEP_TILE[d][k]
                        col = HEADS * d + HG * g
                        ins = tt(heads(xw[:, k % 2, d]), heads(tok[g % 2][:, t, P:]), head_bc(toend[:, t, col:col + HG]),
                                 ALU.mult)
                    ins.then_inc(xw_ready, 1)

            def unit_inputs(u):
                g, ch = divmod(u, LT)
                if u >= 2:
                    filled(gp, ("diag", u - 2))
                xs = heads(tok[g % 2][:, CT + ch, P:])
                tt(heads(xd[u % 2]), xs, head_bc(dbc[:, HG * g:HG * (g + 1)]), ALU.mult)
                for d in range(2):
                    col = HEADS * d + HG * g
                    ins = tt(heads(xdt[u % 2][:, d]), xs, head_bc(dt[:, CT + ch, col:col + HG]), ALU.mult)
                ins.then_inc(xdt_ready, 1)

            def unit_mask(u):
                gp.wait_ge(seg_ready, u + 1)
                for d, sign in ((0, 1), (1, -1)):
                    ins = gp.affine_select(out=seg[u % 2][:, d], in_=seg[u % 2][:, d], compare_op=ALU.is_ge,
                                           fill=MASKED, base=0, pattern=[[0, HG], [sign, P]],
                                           channel_multiplier=-sign)
                ins.then_inc(masked, 1)

            def unit_sum(u):
                emptied(gp, ("off", u, 0))
                emptied(gp, ("off", u, 1))
                gp.wait_ge(xdt_ready, u + 1)
                y = yb[u % 2]
                step(tt(y[:, 0], y[:, 0], y[:, 1], ALU.add))
                tt(y[:, 0], y[:, 0], xd[u % 2], ALU.add).then_inc(offs_summed, 1)

            def rstd(dst, src, width, ready):
                step(gp.tensor_scalar(dst, src, 1.0 / width, EPS, ALU.mult, ALU.add))
                tt(dst, dst, stat[:, 28:29], ALU.pow).then_inc(ready, 1)

            def unit_rstd(u):
                gp.wait_ge(squared, u + 1)
                c_ = 16 + u % 2
                rstd(stat[:, c_:c_ + 1], stat[:, c_ + 2:c_ + 3], GW, rstd_y)

            def row_rstd(squares, ready, n):
                for t in range(n):
                    gp.wait_ge(squares, t + 1)
                    rstd(stat[:, t:t + 1], stat[:, 8 + t:9 + t], D, ready)

            step(gp.memset(stat[:, 28:29], -0.5))
            row_rstd(square_done, rstd_x, TT)
            gp.wait_ge(rows_ready, 1)
            gp.dma_start(cum_dram, cum_rows[0:48, :]).then_inc(cum_out, 16)
            emptied(gp, "ada_c")
            emptied(gp, "ada_b")
            gp.dma_start(mod_dram[4:12].rearrange("m j c -> j m c"),
                         mod_rows[0:P:32, 4 * P:12 * P].rearrange("p (m c) -> p m c", c=P)).then_inc(mod_out, 16)
            gp.wait_ge(cum_ready, 1)
            gp.wait_ge(cum_out, 16)
            for g in range(GROUPS):
                if g:
                    unit_rstd(4 * g - 1)
                state_inputs(g)
                unit_inputs(4 * g)
                unit_mask(4 * g)
                for ch in range(LT):
                    u = 4 * g + ch
                    if ch:
                        unit_rstd(u - 1)
                    unit_sum(u)
                    if ch < LT - 1:
                        unit_inputs(u + 1)
                        unit_mask(u + 1)
            unit_rstd(UNITS - 1)
            row_rstd(x1_squared, rstd_x1, LT)
            row_rstd(x2_squared, rstd_x2, LT)


_INS = ['x', 'c', 'ctx', 'c_ctx', 'w_ada', 'b_ada', 'norm1_w', 'w_in', 'conv_w', 'conv_b', 'dt_bias', 'a_log',
        'd_skip', 'ssm_norm_w', 'w_fourier', 'w_out', 'norm2_w', 'w_router', 'w_gate', 'w_up', 'w_down',
        'final_norm_w']


def kernel(**inputs):
    import numpy as _np
    import concourse.bacc as _bacc
    from concourse import mybir as _mybir
    from concourse.bass_utils import run_bass_kernel_spmd as _run

    nc = _bacc.Bacc("TRN2", target_bir_lowering=False, num_devices=1)
    consts, dft = host_constants()
    arrays, args = {}, []
    for name, a in [("consts", consts), ("dft", dft)] + [(n, _np.ascontiguousarray(inputs[n])) for n in _INS]:
        arrays[f"in_{name}_dram"] = a
        args.append(nc.dram_tensor(f"in_{name}_dram", a.shape, _mybir.dt.from_np(a.dtype), kind="ExternalInput").ap())
    args.append(nc.dram_tensor("out_0_dram", (1, SEQ, D), F32, kind="ExternalOutput").ap())
    build(nc, *args)
    r = _run(nc, [arrays], core_ids=[0])
    return r.results[0]["out_0_dram"]
```

```python
from contextlib import ExitStack

import numpy as np

import concourse.bass as bass
from concourse import mybir

F32 = mybir.dt.float32
F32R = mybir.dt.float32r
ALU = mybir.AluOpType
ACT = mybir.ActivationFunctionType
AX_X = mybir.AxisListType.X

P = 128
D = 1024
KT = D // P
SEQ, CTX = 512, 256
LT, CT = SEQ // P, CTX // P
TT = CT + LT
TOK = SEQ + CTX
HALF = SEQ // 2
F_DIM, F_GROUP = 512, 64
FT = F_DIM // P
HD = 64
D_SSM = 1536
HEADS = D_SSM // HD
GROUPS = 4
HG = HEADS // GROUPS
GW = HG * HD
XT = GW // P
YT = D_SSM // P
CONV = 5
CONV_TILES = (D_SSM + 2 * GROUPS * P) // P
COL_Z = F_DIM
COL_X = COL_Z + D_SSM
COL_B = COL_X + D_SSM
COL_C = COL_B + GROUPS * P
COL_DT = COL_C + GROUPS * P
DT_W = 64
EXPERTS, CAP, FE = 16, 64, 2048
EPS = 1e-6
MASKED = -1e30

PAD = CONV // 2
CONV_IN = TOK + 3 * PAD
CONV_OUT = TOK + PAD
LAT0 = CTX + PAD

ADA_W = 512
ADA_N = 6 * D // ADA_W
ADA_ORDER = [0, 2, 1, 3, *range(4, ADA_N)]
ADA_FIRST = 4
UNITS = GROUPS * LT
W_TILES = 8
W_ALL = W_TILES * GROUPS + FT
C_TILE = 1
STEPS = CT + LT - 1
LOW = 24600
RING = 12
CHUNKS = 24
WO_SLOTS = 4
ROUTE_W = 64
WO_ORDER = [4, *range(9, 13), *range(5, 9), *range(4), *range(13, 16)]
MIX_AT = {3: (0, 1), 4: (2, 3), 5: (4,)}
MIX_EARLY = 5
TOKENS_AT = {2: 0, 3: 2, 4: 3, 5: 4}


def host_constants():
    c = np.zeros((P, 6 * P + 8 + CAP), np.float32)
    i = np.arange(P)
    c[:, 0:P] = np.eye(P)
    c[:, P:2 * P] = i[:, None] <= i[None, :]
    c[:, 2 * P:3 * P] = i[:, None] >= i[None, :]
    c[:, 3 * P:4 * P] = 1.0
    angle = 2 * np.pi * ((np.arange(F_GROUP)[:, None] * np.arange(F_GROUP)[None, :]) % F_GROUP) / F_GROUP
    scale = 1.0 / np.sqrt(SEQ * F_GROUP)
    for b in range(2):
        s = slice(b * F_GROUP, (b + 1) * F_GROUP)
        c[s, 4 * P + b * F_GROUP:4 * P + (b + 1) * F_GROUP] = np.cos(angle) * scale
        c[s, 5 * P + b * F_GROUP:5 * P + (b + 1) * F_GROUP] = -np.sin(angle) * scale
    for j in range(4):
        for w in range(2):
            c[32 * j + w, 6 * P + 2 * j + w] = 1.0
    c[:, 6 * P + 8:] = np.arange(1, CAP + 1)
    t = np.arange(SEQ)
    seq = 2 * np.pi * ((t[:, None] * t[None, :]) % SEQ) / SEQ
    dft = np.concatenate([np.cos(seq)[:, :HALF + 1], np.sin(seq)[:, 1:HALF]], 1).astype(np.float32).reshape(LT, P, SEQ)
    return c, dft


def bank_turns():
    used, turns = [0] * 8, {}

    def take(key, bank):
        turns[key] = (bank, used[bank])
        used[bank] += 1

    take("columns", 4)
    for k in range(KT):
        take(("xT", k, 0), k % 2)
        take(("xT", k, 1), 2 + k % 2)
    take("ada_a", 6)
    take("mod_a", 4)
    take("ada_a2", 5)
    take("mod_a2", 7)
    for r in range(GROUPS + 1):
        g = r - 1
        for i in range(6):
            if r < GROUPS and i < 5:
                n = 5 * r + i
                take(("in", n, 0), n % 2)
                if i != C_TILE:
                    take(("in", n, 1), 2 + n % 2)
            elif r < GROUPS:
                for c in range(XT):
                    take(("z", r, c), c)
                    if c:
                        take(("zT", r, c - 1), 3)
                take(("zT", r, XT - 1), 3)
            elif i < 2:
                take(("u", 2 * i), 0)
                take(("u", 2 * i + 1), 1)
                if i == 1:
                    take("fourier_w", 2)
            elif i == 2:
                for t in range(LT):
                    take(("v", t, 0), 2 * (t % 2))
                    take(("v", t, 1), 2 * (t % 2) + 1)
            if r < GROUPS and i in TOKENS_AT:
                take(("T", r, TOKENS_AT[i], 0), 5)
                take(("T", r, TOKENS_AT[i], 1), 6)
            if r == 0:
                for key, bank in ((("dtT", 5), ("dtT_ctx", 6)), (("dt", 7), ("ada_b", 4)), (("cum", 7), ("tot", 6)),
                                  (("rows", 7),), (("ada_c", 7),), ())[i]:
                    take(key, bank)
            if g >= 0:
                if i == 0:
                    if g > 0:
                        take(("y", 4 * g - 1), 4)
                    for k in range(STEPS):
                        take(("state", g, k, 0), (5, 7)[k % 2])
                        take(("state", g, k, 1), (6, 4)[k % 2])
                if i >= 3:
                    take(("y", 4 * g + i - 3), 4)
                if 2 <= i:
                    take(("diag", 4 * g + i - 2), 7)
                if 1 <= i <= 4:
                    v = 4 * g + i - 1
                    take(("cb", v), 4)
                    take(("off", v, 0), 5)
                    take(("off", v, 1), 6)
    for j in range(FT):
        take(("f", j), j)
    take(("y", UNITS - 1), 4)
    for t in range(LT):
        for h in range(2):
            take(("out", t, h), 2 * t + h)
    for t in range(LT):
        take(("nT", t, 0), 3 if t == LT - 1 else 1)
        take(("nT", t, 1), 4 if t == LT - 1 else 2)
    take("logits", 0)
    take("probsT", 6)
    take("slotT", 7)
    return turns, used


def build(nc, consts, dft, x, c, ctx_tokens, c_ctx, w_ada, b_ada, norm1_w, w_in, conv_w, conv_b, dt_bias, a_log,
          d_skip, ssm_norm_w, w_fourier, w_out, norm2_w, w_router, w_gate, w_up, w_down, final_norm_w, out):
    turns, uses = bank_turns()
    with ExitStack() as ctx:
        def sem(name):
            return ctx.enter_context(nc.semaphore(name))

        def rounded(offset, *shape):
            name, n = f"rounded_{offset}_{len(shape)}", int(np.prod(shape))
            with nc.sbuf_tensor(f"before_{name}", [P, offset], F32) if offset else ExitStack():
                with nc.sbuf_tensor(name, [P, n], F32R) as t:
                    v = t[:]
            return shaped(v, shape)

        def shaped(v, shape):
            if len(shape) == 2:
                return v.rearrange("p (a b) -> p a b", a=shape[0])
            if len(shape) == 3:
                return v.rearrange("p (a b c) -> p a b c", a=shape[0], b=shape[1])
            return v

        hT_lo = rounded(0, KT, TOK)
        hi_lat, hi_ctx = [rounded(6144, FT, SEQ), rounded(30744, FT, SEQ)], rounded(45848, KT, CTX)
        W_RAW = (8192, 9216, 29208)
        w_lo, w_hi = [rounded(o, KT, P) for o in W_RAW], [rounded(o, KT, P) for o in (10240, 11264)]
        w_dt_lo, w_dt_hi = rounded(23064, KT, DT_W), rounded(23576, KT, DT_W)
        WO_RAW = (48152, 49176, 47128, 32792)
        wo_lo, wo_hi = [rounded(o, D) for o in WO_RAW], [rounded(14336 + D * s, D) for s in range(2)]
        mix_lo, mix_hi = rounded(24600, 16, SEQ), rounded(16384, 16, SEQ)
        low = ctx.enter_context(nc.sbuf_tensor("low_arena", [P, LOW], F32))
        high = ctx.enter_context(nc.sbuf_tensor("high_arena", [P, 53200 - LOW], F32))
        bank = [ctx.enter_context(nc.psum_tensor(f"bank{b}", [P, 512], F32)) for b in range(8)]
        mod_dram = nc.dram_tensor("mod_rows_dram", (ADA_N, 4, P), F32, kind="Internal").ap()
        cum_dram = nc.dram_tensor("cum_rows_dram", (2 * HEADS, SEQ), F32, kind="Internal").ap()

        def at(offset, *shape):
            arena, o = (low, offset) if offset < LOW else (high, offset - LOW)
            return shaped(arena[:, o:o + int(np.prod(shape))], shape)

        hT = at(0, KT, TOK)
        w_raw = [at(o, KT, P) for o in W_RAW]
        conv_in = [at(12288 + CONV_IN * s, CONV_IN) for s in range(2)]
        conv_acc = [at(13836 + CONV_OUT * s, CONV_OUT) for s in range(2)]
        z_ch = [b[:, PAD + LAT0:PAD + LAT0 + SEQ] for b in conv_in]
        bc_ch = [[at(15376 + (2 * s + j) * CONV_OUT, CONV_OUT) for j in range(2)] for s in range(2)]
        tok = [at(18456 + 3072 * s, TT, 512) for s in range(2)]
        ada_rows_b = at(21528, ADA_N * P)
        yT = at(24600, YT, SEQ)
        x_raw = at(24600, TT, D)
        rows_raw = at(30744, 2 * P)
        small_w = at(18456, FT * F_GROUP)
        zs = [at(32792 + 1536 * s, LT, GW) for s in range(2)]
        ada_buf = [at(32792 + 4096 * s, KT, ADA_W) for s in range(3)]
        hp = [at(35864 + 1536 * d, LT, GW) for d in range(2)]
        seg = [at(38936 + 1536 * s, 2, HG, P) for s in range(2)]
        xdt = [at(42008 + 768 * s, 2, GW) for s in range(2)]
        xd = [at(43544 + 384 * s, GW) for s in range(2)]
        yb = [at(44312 + 768 * s, 2, GW) for s in range(2)]
        uT = at(12288, FT, SEQ)
        fw = at(14336, FT, 2 * P)
        mod_rows = at(24600, ADA_N * P)
        xw = at(47896, 2, 2, GW)
        st_tmp = at(49432, 2, GW)
        vf = at(0, LT, FT, 2 * P)
        dft_rows = at(4096, LT, SEQ)
        wo_buf = [at(o, D) for o in WO_RAW]
        mixT = at(24600, 16, SEQ)
        x1 = at(36888, LT, D)
        rowbc = {n: at(40984 + D * i, D) for i, n in enumerate(("shift2", "scale2", "gate1", "gate2"))}
        norm2_bc = at(33816, D)
        out_tmp = at(34840, 2, 512)
        ring = [at(2048 * s, 2048) for s in range(RING)]
        h2 = at(45080, LT, D)
        nT = [at(o, KT, P) for o in (35864, 33816)]
        small = 31000
        lg = at(small, LT, EXPERTS)
        probs = at(small + 64, LT, EXPERTS)
        slotT = at(small + 128, LT, EXPERTS)
        rowmax = at(small + 192, LT)
        rowsum = at(small + 196, LT)
        pT = at(small + 216, SEQ)
        top8 = at(small + 728, 8)
        mask = at(32792, SEQ)
        cums = at(32792 + 512, SEQ)
        slot1 = at(32792 + 1024, SEQ)
        sel = at(28696, LT, CAP)
        sel_w = at(28952, LT, 2, CAP)
        scatter = at(29464, SEQ)
        xgT = at(29976, KT, CAP)
        silu_g = at(32792, 1024)
        act_e = at(33816, 1024)
        actT = at(34840, 1024)
        y_e = at(35864, 1024)
        out_rows = at(24600, LT, D)
        gate2 = rowbc["gate2"]
        final_bc = at(40984, D)

        s0 = [50200]

        def keep(*shape):
            o = s0[0]
            s0[0] += int(np.prod(shape))
            return at(o, *shape)

        cst = keep(6 * P + 8 + CAP)
        ident, tri_f, tri_b, ones = (cst[:, P * i:P * (i + 1)] for i in range(4))
        dft_c, dft_s = cst[:, 4 * P:5 * P], cst[:, 5 * P:6 * P]
        sel8, iota1 = cst[:, 6 * P:6 * P + 8], cst[:, 6 * P + 8:6 * P + 8 + CAP]
        cols_a = keep(56)
        cols_b = keep(CONV * CONV_TILES)
        n1w, cb_col, ssm_col = cols_a[:, 0:8], cols_a[:, 8:28], cols_a[:, 28:40]
        scT = keep(16)
        modc = keep(ADA_FIRST * 4, 2)
        a1 = keep(8, 2)
        stat = keep(32)
        abc, dtb, dbc = keep(48), keep(48), keep(24)
        cum = keep(TT, 48)
        dt = keep(TT, 48)
        ecum = keep(TT, 48)
        toend = keep(TT, 48)
        decay = keep(TT, 48)
        router_w = keep(KT + 3, EXPERTS)
        assert s0[0] <= 53200, s0[0]
        w_dt = at(23064, KT, DT_W)
        dtmp = [at(49176 + 288 * i, TT, 48) for i in range(3)]
        cum_rows = at(49176, SEQ)
        dt_rows = at(49176, TOK)

        bank_full = [sem(f"bank_full{b}") for b in range(8)]
        bank_free = [sem(f"bank_free{b}") for b in range(8)]
        small_in, ctx_in, lat_in, w_dt_in = sem("small_in"), sem("ctx_in"), sem("lat_in"), sem("w_dt_in")
        ada_in = [sem(f"ada_in{s}") for s in range(3)]
        ada_used = sem("ada_used")
        ada_b_in = sem("ada_b_in")
        w_in_sem = [sem(f"w_in{s}") for s in range(3)]
        w_hi_ready, w_lo_ready, dt_w_hi, dt_w_lo = (sem(n) for n in ("w_hi_ready", "w_lo_ready", "dt_w_hi", "dt_w_lo"))
        modulated, h_hi_ready = sem("modulated"), sem("h_hi_ready")
        wo_hi_ready, wo_lo_ready, mix_hi_ready, mix_lo_ready = (sem(n) for n in ("wo_hi_ready", "wo_lo_ready",
                                                                                "mix_hi_ready", "mix_lo_ready"))
        fourier_w_in, fw_zero = sem("fourier_w_in"), sem("fw_zero")
        pads_zero = sem("pads_zero")
        seg_in = [sem(f"seg_in{s}") for s in range(2)]
        dft_in = sem("dft_in")
        mod_out, mod_bc_in, cum_out = sem("mod_out"), sem("mod_bc_in"), sem("cum_out")
        dve_step, pool_step = sem("dve_step"), sem("pool_step")
        square_done, xn_done = sem("square_done"), sem("xn_done")
        rstd_x, rstd_y, rstd_x1, rstd_x2 = sem("rstd_x"), sem("rstd_y"), sem("rstd_x1"), sem("rstd_x2")
        silu_c, hmod = sem("silu_c"), sem("hmod")
        dt_ready, cum_ready, rows_ready = sem("dt_ready"), sem("cum_ready"), sem("rows_ready")
        exp_small, small_exped = sem("exp_small"), sem("small_exped")
        conv_done, tile_done = sem("conv_done"), sem("tile_done")
        xw_ready, state_ready, xdt_ready = sem("xw_ready"), sem("state_ready"), sem("xdt_ready")
        seg_ready, masked, decays = sem("seg_ready"), sem("masked"), sem("decays")
        offs_summed, gated, squared, y_ready = sem("offs_summed"), sem("gated"), sem("squared"), sem("y_ready")
        wo_in = [sem(f"wo_in{s}") for s in range(WO_SLOTS)]
        wo_used, res_in, x1_ready = sem("wo_used"), sem("res_in"), sem("x1_ready")
        x1_squared, h2_ready, router_in = sem("x1_squared"), sem("h2_ready"), sem("router_in")
        exped, probs_ready, slots_ready = sem("exped"), sem("probs_ready"), sem("slots_ready")
        ring_in = [sem(f"ring_in{s}") for s in range(RING)]
        ring_used = sem("ring_used")
        e_full = [sem(f"expert_full{b}") for b in range(8)]
        e_free = [sem(f"expert_free{b}") for b in range(8)]
        sel_ready, selw_ready, silu_ready, act_ready = (sem(n) for n in ("sel_ready", "selw_ready", "silu_ready",
                                                                       "act_ready"))
        gate2_in, final_in = sem("gate2_in"), sem("final_in")
        x2_squared, out_ready, out_done = sem("x2_squared"), sem("out_ready"), sem("out_done")

        def filled(eng, key):
            b, n = turns[key]
            eng.wait_ge(bank_full[b], n + 1)
            return bank[b]

        def emptied(eng, key):
            b, n = turns[key]
            eng.wait_ge(bank_free[b], n + 1)

        def claim(pe, key):
            b, n = turns[key]
            if n:
                pe.wait_ge(bank_free[b], n)
            return bank[b]

        def full(ins, key):
            ins.then_inc(bank_full[turns[key][0]], 1)

        def free(ins, key):
            ins.then_inc(bank_free[turns[key][0]], 1)

        class Chain:

            def __init__(self, eng, s):
                self.eng, self.s, self.n = eng, s, 0

            def __call__(self, ins):
                self.n += 1
                ins.then_inc(self.s, 1)
                self.eng.wait_ge(self.s, self.n)

        ADA_LAST = {1: "ada_a", 3: "ada_a2", 7: "ada_b", 11: "ada_c"}

        def ada_piece_used(eng, i):
            if i in ADA_LAST:
                filled(eng, ADA_LAST[i])
            else:
                eng.wait_ge(ada_used, i + 1 - sum(p < i for p in ADA_LAST))

        def weights_used(eng, q):
            r, i = divmod(q, W_TILES)
            if r == GROUPS:
                filled(eng, ("u", i))
            elif i < 5:
                filled(eng, ("in", 5 * r + i, 0 if i == C_TILE else 1))
            else:
                filled(eng, ("z", r, i - 5))

        def raw_slot(q):
            return (q + 1) % 3, sum((p + 1) % 3 == (q + 1) % 3 for p in range(q + 1))

        def slot_tiles(r, i):
            q = W_TILES * r + i
            if r == GROUPS:
                return [q + i, q + i + 1] if i < 2 else []
            return [q] if i < 5 else [q, q + 1, q + 2]

        def split_ahead(r, i):
            if 0 < r < GROUPS and i <= 1:
                return [W_TILES * r + 1] if i == 0 else []
            return [q + 1 for q in slot_tiles(r, i) if q + 1 < W_ALL]

        def whole(v):
            return v.bitcast(F32)

        def chunk_used(eng, e, ch):
            if ch == 14:
                eng.wait_ge(e_full[1], e * 2 + 1)
            elif ch == 15:
                eng.wait_ge(e_full[3], e * 2 + 1)
            elif ch == 23:
                eng.wait_ge(e_full[5], e * 2 + 2)
            else:
                eng.wait_ge(ring_used, e * (CHUNKS - 3) + (ch + 1 if ch < 14 else ch - 1))

        def head_bc(v, width=HD):
            return v.unsqueeze(2).to_broadcast([P, HG, width])

        def heads(v):
            return v.rearrange("p (h c) -> p h c", h=HG)

        def chan(v, t):
            o = P * t if t < CT else LAT0 + P * (t - CT)
            return v[:, o:o + P]

        STEP_TILE = [[0, 1, 2, 3, 4], [1, 0, 5, 4, 3]]
        TILE_OF = lambda r, i: (12 + r, 16 + r, 3 * r, 3 * r + 1, 3 * r + 2)[i]
        SMALL_N = 16 * 10

        block = ctx.enter_context(nc.Block())

        @block.sync
        def _(sp):
            sp.dma_start(x_raw[:, 0:CT, :], ctx_tokens[0].rearrange("(t p) d -> p t d", p=P)).then_inc(ctx_in, 16)
            sp.dma_start(x_raw[:, CT:TT, :], x[0].rearrange("(t p) d -> p t d", p=P)).then_inc(lat_in, 16)

            def ld(dst, src):
                sp.dma_start(dst, src).then_inc(small_in, 16)

            ld(cst, consts)
            row = 0
            for src, n in ((norm1_w, 8), (conv_b, 20), (ssm_norm_w, 12), (c, 8)):
                ld(rows_raw[row:row + n, 0:P], src[0].rearrange("(r c) -> r c", c=P))
                row += n
            ld(rows_raw[row:row + 8, 0:P], c_ctx.rearrange("(r c) -> r c", c=P))
            ld(rows_raw[0:100, P:2 * P], conv_w[0].rearrange("k (r c) -> (k r) c", c=P))
            ld(abc, a_log[0].rearrange("d h -> (d h)").partition_broadcast(P))
            ld(dtb, dt_bias[0].rearrange("d h -> (d h)").partition_broadcast(P))
            ld(dbc, d_skip[0].partition_broadcast(P))
            for w in range(2):
                sp.dma_start(ada_rows_b[w:w + 97:32, :].rearrange("p (m c) -> p m c", m=ADA_N),
                              b_ada[0].rearrange("(m j c) -> j m c", m=ADA_N, c=P)).then_inc(ada_b_in, 16)
            def load_ada(i):
                if i >= 3:
                    ada_piece_used(sp, i - 3)
                col = ADA_W * ADA_ORDER[i]
                sp.dma_start(ada_buf[i % 3], w_ada[0, :, col:col + ADA_W].rearrange("(k p) c -> p k c", p=P)
                             ).then_inc(ada_in[i % 3], 16)

            def load_w(q):
                r, i = divmod(q, W_TILES)
                if q >= 3:
                    weights_used(sp, q - 3)
                if r == GROUPS:
                    col = P * i
                elif i < 5:
                    col = (COL_B + P * r, COL_C + P * r, *(COL_X + GW * r + P * j for j in range(XT)))[i]
                else:
                    col = COL_Z + GW * r + P * (i - 5)
                slot = raw_slot(q)[0]
                sp.dma_start(w_raw[slot], w_in[0, :, col:col + P].rearrange("(k p) c -> p k c", p=P)
                             ).then_inc(w_in_sem[slot], 16)

            for i in range(ADA_FIRST - 1):
                load_ada(i)
            load_w(0)
            load_ada(ADA_FIRST - 1)
            sp.dma_start(w_dt, w_in[0, :, COL_DT + 48 - DT_W:].rearrange("(k p) c -> p k c", p=P)).then_inc(w_dt_in, 16)
            filled(sp, ("xT", KT - 1, 1))
            load_w(1)
            load_w(2)
            for i in range(ADA_FIRST, 7):
                load_ada(i)

            def load_wo(n):
                sp.dma_start(wo_buf[n % WO_SLOTS], w_out[0, P * WO_ORDER[n % 16]:P * (WO_ORDER[n % 16] + 1), :]
                             ).then_inc(wo_in[n % WO_SLOTS], 16)

            for r in range(GROUPS + 1):
                g = r - 1
                for i in range(6):
                    if r == 1 and i == 0:
                        filled(sp, "ada_c")
                        sp.wait_ge(cum_out, 16)
                    if g >= 0 and i < LT:
                        v = LT * g + i
                        if v >= 2:
                            filled(sp, ("diag", v - 2))
                        for d in range(2):
                            src = cum_dram[HEADS * d + HG * g:HEADS * d + HG * (g + 1), P * i:P * (i + 1)]
                            sp.dma_start(seg[v % 2][:, d], src.partition_broadcast(P)).then_inc(seg_in[v % 2], 16)
                    for q in slot_tiles(r, i):
                        if q + 3 < W_ALL:
                            load_w(q + 3)
                    for p in ((), (7, 8), (9, 10), (), (11,), ())[i] if r == 0 else ():
                        load_ada(p)
                    if r == GROUPS and i == 0:
                        for h in range(2):
                            sp.dma_start(small_w[64 * h:64 * (h + 1), :].rearrange("p (j c) -> p j c", j=FT),
                                         w_fourier[0].rearrange("(j h) i c -> h i j c", h=2)[h]
                                         ).then_inc(fourier_w_in, 16)
                    elif r == GROUPS and i == 1:
                        emptied(sp, ("u", FT - 1))
                        sp.dma_start(dft_rows, dft.rearrange("t p l -> p t l")).then_inc(dft_in, 16)
                    elif r == GROUPS and i == 3:
                        filled(sp, ("v", LT - 1, 1))
                        emptied(sp, ("state", GROUPS - 1, STEPS - 1, 1))
                        sp.wait_ge(gated, 4 * (GROUPS - 1))
                        for n in range(WO_SLOTS):
                            load_wo(n)
            def load_chunk(e, ch):
                dst = ring[ch % RING]
                if ch < 16:
                    src = (w_gate if ch % 2 == 0 else w_up)[0, bass.ds(e, 1), P * (ch // 2):P * (ch // 2 + 1), :]
                    sp.dma_start(dst, src.rearrange("a p f -> p (a f)")).then_inc(ring_in[ch % RING], 16)
                else:
                    j = ch - 16
                    src = w_down[0, bass.ds(e, 1)].rearrange("a (h j p) d -> j p (a h) d", h=2, p=P)[j]
                    sp.dma_start(dst.rearrange("p (h d) -> p h d", h=2), src).then_inc(ring_in[ch % RING], 16)

            filled(sp, ("y", UNITS - 1))
            emptied(sp, ("f", FT - 1))
            MOD_ROWS_AT = {9: ("gate1", 2), 10: ("scale2", 4), 11: ("shift2", 3), 30: ("gate2", 5)}
            CHUNK_AT = (14, 17, 19, 22, 25, 28, 31)
            early = len(CHUNK_AT)
            for n in range(WO_SLOTS, 2 * 16):
                m = n - WO_SLOTS
                if m % 16 == 15:
                    filled(sp, ("out", 2 * (m // 16) + 1, 1))
                else:
                    sp.wait_ge(wo_used, m + 1 - m // 16)
                load_wo(n)
                if n in (5, 6, 7, 8):
                    sp.dma_start(x1[:, n - 5], x[0, P * (n - 5):P * (n - 4), :]).then_inc(res_in, 16)
                elif n in MOD_ROWS_AT:
                    name, m = MOD_ROWS_AT[n]
                    sp.wait_ge(mod_out, 16)
                    src = mod_dram[2 * m:2 * m + 2].rearrange("m j c -> (m j c)")
                    sp.dma_start(rowbc[name], src.partition_broadcast(P)).then_inc(
                        gate2_in if name == "gate2" else mod_bc_in, 16)
                if n == 12:
                    sp.dma_start(norm2_bc, norm2_w[0].partition_broadcast(P)).then_inc(mod_bc_in, 16)
                    sp.dma_start(router_w[:, 0:KT], w_router[0].rearrange("(k p) e -> p k e", p=P)).then_inc(router_in, 16)
                if n in CHUNK_AT:
                    load_chunk(0, CHUNK_AT.index(n))
            filled(sp, ("out", LT - 1, 1))
            for ch in range(early, RING):
                load_chunk(0, ch)
            with sp.Fori(0, EXPERTS - 1) as e:
                for ch in range(RING, CHUNKS):
                    if ch != 16:
                        chunk_used(sp, e, ch - RING + (ch == 15))
                    load_chunk(e, ch)
                for ch in range(RING):
                    chunk_used(sp, e, ch + CHUNKS - RING)
                    load_chunk(e + 1, ch)
            for ch in range(RING, CHUNKS):
                chunk_used(sp, EXPERTS - 1, ch - RING)
                load_chunk(EXPERTS - 1, ch)
            sp.dma_start(final_bc, final_norm_w.partition_broadcast(P)).then_inc(final_in, 16)
            for t in range(LT):
                sp.wait_ge(out_ready, t + 1)
                sp.dma_start(out[0, P * t:P * (t + 1), :], out_rows[:, t]).then_inc(out_done, 16)
            sp.wait_ge(out_done, 16 * LT)

        @block.tensor
        def _(pe):
            mm, tr = pe.matmul, pe.transpose

            pe.wait_ge(small_in, SMALL_N)
            b = claim(pe, "columns")
            tr(b[:, 0:56], rows_raw[0:56, 0:P], ident[0:56, 0:56])
            full(tr(b[:, 64:164], rows_raw[0:100, P:2 * P], ident[0:100, 0:100]), "columns")
            pe.wait_ge(xn_done, TT)
            for k in range(KT):
                for part, (t0, n) in enumerate(((CT, LT), (0, CT))):
                    b = claim(pe, ("xT", k, part))
                    for t in range(n):
                        ins = tr(b[:, P * t:P * (t + 1)], x_raw[:, t0 + t, P * k:P * (k + 1)], ident)
                    full(ins, ("xT", k, part))

            def ada_piece(i, key, col):
                pe.wait_ge(ada_in[i % 3], 16 * (i // 3 + 1))
                b = bank[turns[key][0]]
                n = 2 if i < ADA_FIRST else 1
                for k in range(KT):
                    for j in range(4):
                        ins = mm(b[32 * j:32 * j + n, col:col + P], scT[:, k:k + 8 * n - 7:8],
                                 ada_buf[i % 3][:, k, P * j:P * (j + 1)], start=(k == 0), stop=(k == KT - 1),
                                 skip_group_check=True)
                full(ins, key) if i in ADA_LAST else ins.then_inc(ada_used, 1)

            def ada(key, bank_first, first, n):
                for i in range(first, first + n):
                    if i == bank_first:
                        claim(pe, key)
                    ada_piece(i, key, P * (i - bank_first))

            def mod_columns(key, pieces):
                b = claim(pe, key)
                for i, piece in enumerate(pieces):
                    ins = mm(b[:, 8 * i:8 * i + 8], mod_rows[:, P * piece:P * (piece + 1)], sel8,
                             start=True, stop=True)
                full(ins, key)

            pe.wait_ge(silu_c, 1)
            ada("ada_a", 0, 0, 2)
            emptied(pe, "ada_a")
            mod_columns("mod_a", (0, 2))
            ada("ada_a2", 2, 2, 2)
            emptied(pe, "ada_a2")
            mod_columns("mod_a2", (1, 3))

            def split_product(dst, a_hi, a_lo, b_hi, b_lo, first, last):
                mm(dst, a_hi, b_hi, start=first, stop=False)
                mm(dst, a_hi, b_lo, start=False, stop=False)
                return mm(dst, a_lo, b_hi, start=False, stop=last)

            def h_latent(k):
                return hi_lat[k // FT][:, k % FT], hT_lo[:, k, CTX:TOK]

            def project_dt():
                pe.wait_ge(dt_w_lo, 1)
                lat, cx = claim(pe, "dtT"), claim(pe, "dtT_ctx")
                for k in range(KT):
                    a = split_product(lat[0:DT_W, :], w_dt_hi[:, k], w_dt_lo[:, k], *h_latent(k), k == 0, k == KT - 1)
                full(a, "dtT")
                for k in range(KT):
                    a = split_product(cx[0:DT_W, 0:CTX], w_dt_hi[:, k], w_dt_lo[:, k], hi_ctx[:, k], hT_lo[:, k, 0:CTX],
                                      k == 0, k == KT - 1)
                full(a, "dtT_ctx")

            def dt_to_tokens():
                emptied(pe, "dtT")
                emptied(pe, "dtT_ctx")
                b = claim(pe, "dt")
                for t in range(TT):
                    a = tr(b[:, DT_W * t:DT_W * (t + 1)], dt_rows[0:DT_W, P * t:P * (t + 1)], ident[0:DT_W, 0:DT_W])
                full(a, "dt")

            def cumulative_sums():
                pe.wait_ge(dt_ready, 1)
                b = claim(pe, "cum")
                bv = b[:, 0:TT * 48].rearrange("p (t h) -> p t h", t=TT)
                mm(bv[:, :, 0:24], tri_f, dtmp[0][:, :, 0:24], start=True, stop=True)
                full(mm(bv[:, :, 24:48], tri_b, dtmp[0][:, :, 24:48], start=True, stop=True), "cum")
                b = claim(pe, "tot")
                full(mm(b[:, 0:TT * 48].rearrange("p (t h) -> p t h", t=TT), ones, dtmp[0], start=True, stop=True),
                     "tot")

            def sums_as_rows():
                emptied(pe, "cum")
                b = claim(pe, "rows")
                for t in range(LT):
                    a = tr(b[0:48, P * t:P * (t + 1)], cum[:, CT + t], ident)
                full(a, "rows")

            def w_wait(q):
                pe.wait_ge(w_lo_ready, q + 1)
                return w_hi[q % 2], w_lo[raw_slot(q)[0]]

            def project_channels(r, i):
                n = 5 * r + i
                hi, lo = w_wait(W_TILES * r + i)
                lat = claim(pe, ("in", n, 0))
                for k in range(KT):
                    if n == 0:
                        pe.wait_ge(hmod, 2 * k + 2)
                    a = split_product(lat[:], hi[:, k], lo[:, k], *h_latent(k), k == 0, k == KT - 1)
                full(a, ("in", n, 0))
                if i == C_TILE:
                    return
                cx = claim(pe, ("in", n, 1))
                for k in range(KT):
                    a = split_product(cx[:, 0:CTX], hi[:, k], lo[:, k], hi_ctx[:, k], hT_lo[:, k, 0:CTX], k == 0,
                                      k == KT - 1)
                full(a, ("in", n, 1))

            def project_z(r):
                for c_ in range(XT):
                    hi, lo = w_wait(W_TILES * r + 5 + c_)
                    b = claim(pe, ("z", r, c_))
                    for k in range(KT):
                        a = split_product(b[:], hi[:, k], lo[:, k], *h_latent(k), k == 0, k == KT - 1)
                    full(a, ("z", r, c_))
                    if c_:
                        z_to_tokens(r, c_ - 1)

            def z_to_tokens(r, c_):
                emptied(pe, ("z", r, c_))
                b = claim(pe, ("zT", r, c_))
                for t in range(LT):
                    a = tr(b[:, P * t:P * (t + 1)], z_ch[(5 * r + 5 + c_) % 2][:, P * t:P * (t + 1)], ident)
                full(a, ("zT", r, c_))

            def project_u(i):
                hi, lo = w_wait(W_TILES * GROUPS + i)
                b = claim(pe, ("u", i))
                for k in range(KT):
                    a = split_product(b[:], hi[:, k], lo[:, k], *h_latent(k), k == 0, k == KT - 1)
                full(a, ("u", i))

            def fourier_weights():
                pe.wait_ge(fourier_w_in, 32)
                b = claim(pe, "fourier_w")
                mm(b[:, 0:256], dft_c, small_w, start=True, stop=True)
                full(mm(b[:, 256:512], dft_s, small_w, start=True, stop=True), "fourier_w")

            def channel_dft():
                emptied(pe, ("u", FT - 1))
                emptied(pe, ("u", FT - 2))
                emptied(pe, "fourier_w")
                for t in range(LT):
                    for j in range(FT):
                        key = ("v", t, j // 2)
                        if j % 2 == 0:
                            b = claim(pe, key)
                        a = mm(b[:, 256 * (j % 2):256 * (j % 2 + 1)], uT[:, j, P * t:P * (t + 1)], fw[:, j],
                               start=True, stop=True)
                        if j % 2:
                            full(a, key)

            def position_dft(j):
                if j == 0:
                    pe.wait_ge(dft_in, 16)
                    for h in range(2):
                        for t in range(LT):
                            emptied(pe, ("v", t, h))
                b = claim(pe, ("f", j))
                for s, part in enumerate((slice(0, HALF + 1), slice(HALF + 1, SEQ))):
                    for t in range(LT):
                        a = mm(b[:, part], vf[:, t, j, P * s:P * (s + 1)], dft_rows[:, t, part], start=(t == 0),
                               stop=(t == LT - 1))
                full(a, ("f", j))

            def to_tokens(r, s):
                n = 5 * r + s
                src = bc_ch[r % 2][0] if s == 0 else conv_acc[n % 2]
                pe.wait_ge(tile_done, n + 1)
                for part, (t0, m) in enumerate(((CT, LT), (0, CT))):
                    b = claim(pe, ("T", r, s, part))
                    for t in range(m):
                        a = tr(b[:, P * t:P * (t + 1)], chan(src, t0 + t), ident)
                    full(a, ("T", r, s, part))

            def states(g):
                for s in (0, 2, 3, 4):
                    emptied(pe, ("T", g, s, 0))
                    emptied(pe, ("T", g, s, 1))
                for k in range(STEPS):
                    pe.wait_ge(xw_ready, STEPS * g + k + 1)
                    for d in range(2):
                        b = claim(pe, ("state", g, k, d))
                        full(mm(b[:, 0:GW], tok[g % 2][:, STEP_TILE[d][k], 0:P], xw[:, k % 2, d], start=True,
                                stop=True), ("state", g, k, d))

            def unit_pre(v):
                g, ch = divmod(v, LT)
                bm, cm = (chan(bc_ch[g % 2][j], CT + ch) for j in range(2))
                pe.wait_ge(tile_done, 5 * g + 2)
                b = claim(pe, ("cb", v))
                full(mm(b[:, 0:P], bm, cm, start=True, stop=True), ("cb", v))
                pe.wait_ge(state_ready, STEPS * (g + 1))
                for d in range(2):
                    b = claim(pe, ("off", v, d))
                    full(mm(b[:, 0:GW], cm, hp[d][:, ch if d == 0 else LT - 1 - ch], start=True, stop=True),
                         ("off", v, d))

            def unit_post(v):
                emptied(pe, ("cb", v))
                pe.wait_ge(xdt_ready, v + 1)
                b = claim(pe, ("diag", v))
                for h in range(HG):
                    for d in range(2):
                        a = mm(b[:, HD * h:HD * (h + 1)], seg[v % 2][:, d, h], xdt[v % 2][:, d, HD * h:HD * (h + 1)],
                               start=(d == 0), stop=(d == 1))
                full(a, ("diag", v))

            def unit_fin(v):
                pe.wait_ge(y_ready, v + 1)
                b = claim(pe, ("y", v))
                for j in range(XT):
                    a = tr(b[:, P * j:P * (j + 1)], yb[v % 2][:, 0, P * j:P * (j + 1)], ident)
                full(a, ("y", v))

            for r in range(GROUPS + 1):
                g = r - 1
                for i in range(6):
                    if r < GROUPS:
                        project_channels(r, i) if i < 5 else project_z(r)
                    elif i < 2:
                        project_u(2 * i)
                        project_u(2 * i + 1)
                        if i == 1:
                            fourier_weights()
                    elif i == 2:
                        channel_dft()
                    else:
                        position_dft(i - 3)
                    if r < GROUPS and i in TOKENS_AT:
                        to_tokens(r, TOKENS_AT[i])
                    if r < GROUPS and i == 5:
                        z_to_tokens(r, XT - 1)
                    if r == 0 and i == 0:
                        project_dt()
                    elif r == 0 and i == 1:
                        dt_to_tokens()
                        ada("ada_b", 4, 4, 2)
                    elif r == 0 and i == 2:
                        ada("ada_b", 4, 6, 2)
                        cumulative_sums()
                    elif r == 0 and i == 3:
                        sums_as_rows()
                    elif r == 0 and i == 4:
                        ada("ada_c", 8, 8, 2)
                    elif r == 0:
                        ada("ada_c", 8, 10, 2)
                    if g >= 0:
                        if i == 0:
                            if g > 0:
                                unit_fin(4 * g - 1)
                            states(g)
                        if i >= 3:
                            unit_fin(4 * g + i - 3)
                        if i >= 2:
                            unit_post(4 * g + i - 2)
                        if 1 <= i <= 4:
                            unit_pre(4 * g + i - 1)
            position_dft(3)

            def route_transpose(t):
                pe.wait_ge(h2_ready, t + 1)
                for h in range(2):
                    b = claim(pe, ("nT", t, h))
                    for k in range(4):
                        a = tr(b[:, P * k:P * (k + 1)], h2[:, t, P * (4 * h + k):P * (4 * h + k + 1)], ident)
                    full(a, ("nT", t, h))

            def route_logits(t):
                if t == 0:
                    pe.wait_ge(router_in, 16)
                    pe.wait_ge(pads_zero, 1)
                    claim(pe, "logits")
                for h in range(2):
                    emptied(pe, ("nT", t, h))
                for k in range(KT):
                    w = router_w[:, k:k + ROUTE_W // EXPERTS].rearrange("p k e -> p (k e)")
                    a = mm(bank[0][:, ROUTE_W * t:ROUTE_W * (t + 1)], nT[t % 2][:, k], w, start=(k == 0),
                           stop=(k == KT - 1))
                if t == LT - 1:
                    full(a, "logits")

            for p in range(2):
                bs = {(t, h): claim(pe, ("out", t, h)) for t in (2 * p, 2 * p + 1) for h in range(2)}
                for k in range(16):
                    n, row = 16 * p + k, WO_ORDER[k]
                    if p == 0:
                        pe.wait_ge(mix_lo_ready, k + 1)
                    pe.wait_ge(wo_lo_ready, n + 1)
                    tile = (row - FT) % 16
                    for t in (2 * p, 2 * p + 1):
                        for h in range(2):
                            sl = slice(512 * h, 512 * (h + 1))
                            a = split_product(bs[t, h][:], mix_hi[:, tile, P * t:P * (t + 1)],
                                              mix_lo[:, tile, P * t:P * (t + 1)], wo_hi[n % 2][:, sl],
                                              wo_lo[n % WO_SLOTS][:, sl], k == 0, k == 15)
                            if k == 15:
                                full(a, ("out", t, h))
                    if k < 15:
                        a.then_inc(wo_used, 1)
                    if p == 0 and k == 1:
                        unit_fin(UNITS - 1)
                    elif p == 1 and k in (8, 12):
                        route_transpose(k // 12)
                    elif p == 1 and k == 13:
                        route_logits(0)
            route_logits(1)
            route_transpose(2)
            route_logits(2)
            route_transpose(3)
            route_logits(3)
            pe.wait_ge(probs_ready, 1)
            b = claim(pe, "probsT")
            for t in range(LT):
                a = tr(b[0:EXPERTS, P * t:P * (t + 1)], probs[:, t], ident)
            full(a, "probsT")
            pe.wait_ge(slots_ready, 1)
            b = claim(pe, "slotT")
            for t in range(LT):
                a = tr(b[:, EXPERTS * t:EXPERTS * (t + 1)], slot1[0:EXPERTS, P * t:P * (t + 1)],
                       ident[0:EXPERTS, 0:EXPERTS])
            full(a, "slotT")
            pe.wait_ge(h2_ready, LT)
            with pe.Fori(0, EXPERTS) as e:
                pe.wait_ge(sel_ready, e + 1)
                pe.wait_ge(e_free[4], 2 * e + 1)
                for k in range(KT):
                    for t in range(LT):
                        a = mm(bank[4][:, CAP * k:CAP * (k + 1)], h2[:, t, P * k:P * (k + 1)], sel[:, t],
                               start=(t == 0), stop=(t == LT - 1))
                a.then_inc(e_full[4], 1)
                pe.wait_ge(selw_ready, e + 1)
                pe.wait_ge(e_free[5], 2 * e + 1)
                for t in range(LT):
                    a = tr(bank[5][:, P * t:P * (t + 1)], sel_w[:, t].rearrange("p a b -> p (a b)"), ident)
                a.then_inc(e_full[5], 1)
                pe.wait_ge(e_free[4], 2 * e + 2)
                for b in range(4):
                    pe.wait_ge(e_free[b], e + 1)
                for ch in range(16):
                    k, which = divmod(ch, 2)
                    pe.wait_ge(ring_in[ch % RING], (e * 2 + (ch // RING + 1)) * 16)
                    for n in range(2):
                        for h in range(2):
                            a = mm(bank[2 * which + n][CAP * h:CAP * (h + 1), :], xgT[:, k],
                                   ring[ch % RING][:, 1024 * h + 512 * n:1024 * h + 512 * (n + 1)], start=(k == 0),
                                   stop=(k == KT - 1), skip_group_check=True)
                    if k < KT - 1:
                        a.then_inc(ring_used, 1)
                    else:
                        a.then_inc(e_full[2 * which + 1], 1)
                for n in range(2):
                    pe.wait_ge(act_ready, 2 * e + n + 1)
                    pe.wait_ge(e_free[6 + n], 3 * e + 1)
                    for j in range(4):
                        a = tr(bank[6 + n][:, P * j:P * (j + 1)], act_e[:, 512 * n + P * j:512 * n + P * (j + 1)],
                               ident)
                    a.then_inc(e_full[6 + n], 1)
                pe.wait_ge(e_free[5], 2 * e + 2)
                for j in range(8):
                    ch = 16 + j
                    pe.wait_ge(ring_in[ch % RING], (e * 2 + 2) * 16)
                    if j % 4 == 0:
                        pe.wait_ge(e_free[6 + j // 4], 3 * e + 2)
                    for n in range(2):
                        for h in range(2):
                            a = mm(bank[4 + n][CAP * h:CAP * (h + 1), :],
                                   actT[:, P * j + CAP * h:P * j + CAP * (h + 1)],
                                   ring[ch % RING][:, D * h + 512 * n:D * h + 512 * (n + 1)], start=(j == 0),
                                   stop=(j == 7), skip_group_check=True)
                    if j < 7:
                        a.then_inc(ring_used, 1)
                    else:
                        a.then_inc(e_full[5], 1)
                for n in range(2):
                    pe.wait_ge(e_free[4 + n], 2 * e + 3)
                for i in range(8):
                    t, n = divmod(i, 2)
                    b = (6, 7, 0, 1, 2, 3, 6, 7)[i]
                    if b >= 6:
                        pe.wait_ge(e_free[b], 3 * e + 2 + i // 6)
                    mm(bank[b][:], scatter[:, P * t:P * (t + 1)], y_e[:, 512 * n:512 * (n + 1)], start=True,
                       stop=True).then_inc(e_full[b], 1)

        @block.vector
        def _(v):
            step = Chain(v, dve_step)
            tt, ts, stt, cp = v.tensor_tensor, v.tensor_scalar, v.scalar_tensor_tensor, v.tensor_copy

            for s in range(2):
                for o in (0, LAT0, CONV_IN - PAD):
                    ins = v.memset(conv_in[s][:, o:o + PAD], 0.0)
            step(ins)
            v.memset(router_w[:, KT:], 0.0).then_inc(pads_zero, 1)
            v.wait_ge(pads_zero, 1)
            for t in range(TT):
                v.wait_ge(rstd_x, t + 1)
                ts(x_raw[:, t], x_raw[:, t], stat[:, t:t + 1], None, ALU.mult).then_inc(xn_done, 1)
            b = filled(v, "columns")
            cp(cols_a, b[:, 0:56])
            free(cp(cols_b, b[:, 64:164]), "columns")
            for k in range(KT):
                b = filled(v, ("xT", k, 1))
                free(cp(hT[:, k, 0:CTX], b[:, 0:CTX]), ("xT", k, 1))
            step(v.memset(mod_rows, 0.0))

            row_pieces = mod_rows.rearrange("p (m c) -> p m c", m=ADA_N)
            bias_pieces = ada_rows_b.rearrange("p (m c) -> p m c", m=ADA_N)
            column_pieces = modc.rearrange("p (m j) w -> p m (j w)", m=ADA_FIRST)

            def mod_evac(key, pieces, n):
                b = filled(v, key)
                for j in range(4):
                    q = slice(32 * j, 32 * j + (2 if n == 2 else 1))
                    ins = tt(row_pieces[q, pieces], b[q, 0:P * n].rearrange("p (m c) -> p m c", m=n),
                             bias_pieces[q, pieces], ALU.add)
                free(ins, key)

            def columns_evac(key, pieces, n):
                b = filled(v, key)
                free(cp(column_pieces[:, pieces], b[:, 0:8 * n].rearrange("p (m c) -> p m c", m=n)), key)

            def w_remainder(q):
                v.wait_ge(w_hi_ready, q + 1)
                slot = raw_slot(q)[0]
                tt(w_lo[slot], w_raw[slot], whole(w_hi[q % 2]), ALU.subtract).then_inc(w_lo_ready, 1)

            v.wait_ge(ada_b_in, 32)
            mod_evac("ada_a", slice(0, 3, 2), 2)
            columns_evac("mod_a", slice(0, 3, 2), 2)
            emptied(v, "mod_a")
            emptied(v, "columns")

            def h_remainder(k):
                v.wait_ge(h_hi_ready, 2 * k + 2)
                tt(hT_lo[:, k, CTX:TOK], hT[:, k, CTX:TOK], whole(hi_lat[k // FT][:, k % FT]), ALU.subtract
                   ).then_inc(hmod, 1)
                tt(hT_lo[:, k, 0:CTX], hT[:, k, 0:CTX], whole(hi_ctx[:, k]), ALU.subtract).then_inc(hmod, 1)

            for k in range(KT):
                if k == 4:
                    mod_evac("ada_a2", slice(1, 4, 2), 2)
                    columns_evac("mod_a2", slice(1, 4, 2), 2)
                    emptied(v, "mod_a2")
                if k % 4 == 0:
                    step(stt(a1[:, k:k + 4], modc[:, 8 + k:12 + k], 1.0,
                             n1w[:, k:k + 4].unsqueeze(2).to_broadcast([P, 4, 2]), ALU.add, ALU.mult))
                emptied(v, ("xT", k, 0))
                emptied(v, ("xT", k, 1))
                for part, sl in ((0, slice(CTX, TOK)), (1, slice(0, CTX))):
                    ts(hT[:, k, sl], hT[:, k, sl], a1[:, k, part:part + 1], modc[:, k, part:part + 1], ALU.mult,
                       ALU.add).then_inc(modulated, 1)
                if k == 0:
                    w_remainder(0)
                else:
                    h_remainder(k - 1)
            h_remainder(KT - 1)
            v.wait_ge(dt_w_hi, 1)
            tt(w_dt_lo, w_dt, whole(w_dt_hi), ALU.subtract).then_inc(dt_w_lo, 1)

            def dt_chain():
                b = filled(v, "dt")
                raw, e_, u_ = dtmp
                bv = b[:, 0:TT * DT_W].rearrange("p (t h) -> p t h", t=TT)[:, :, DT_W - 48:]
                free(tt(raw, bv, dtb.unsqueeze(1).to_broadcast([P, TT, 48]), ALU.add), "dt")
                emptied(v, "dt")
                stt(e_, raw, -1.0, raw, ALU.mult, ALU.max).then_inc(exp_small, 1)
                v.wait_ge(small_exped, 2)
                step(ts(u_, e_, 1.0, None, ALU.add))
                cp(cum, u_).then_inc(exp_small, 1)
                v.wait_ge(exp_small, 2)
                step(ts(u_, u_, -1.0, None, ALU.add))
                step(tt(e_, e_, u_, ALU.subtract))
                step(ts(raw, raw, 0.0, None, ALU.max))
                step(v.reciprocal(u_, cum))
                step(tt(e_, e_, u_, ALU.mult))
                v.wait_ge(small_exped, 3)
                step(tt(e_, e_, dt, ALU.add))
                step(tt(dt, e_, raw, ALU.add))
                stt(dtmp[0], dt, -1.0, abc.unsqueeze(1).to_broadcast([P, TT, 48]), ALU.mult, ALU.mult
                    ).then_inc(dt_ready, 1)

            def cumulative_sums():
                bcum = filled(v, "cum")
                free(cp(cum, bcum[:, 0:TT * 48].rearrange("p (t h) -> p t h", t=TT)), "cum")
                btot = filled(v, "tot")
                free(cp(dtmp[1], btot[:, 0:TT * 48].rearrange("p (t h) -> p t h", t=TT)), "tot")
                emptied(v, "cum")
                emptied(v, "tot")
                tt(dtmp[2], dtmp[1], cum, ALU.subtract).then_inc(exp_small, 1)
                v.wait_ge(small_exped, 6)
                tt(toend, toend, dt, ALU.mult).then_inc(cum_ready, 1)

            def sums_as_rows():
                b = filled(v, "rows")
                v.wait_ge(cum_ready, 1)
                free(cp(cum_rows[0:48, :], b[0:48, :]), "rows")
                emptied(v, "rows")
                v.sem_inc(rows_ready, 1)

            def conv(r, i):
                n = 5 * r + i
                ct = TILE_OF(r, i)
                emptied(v, ("in", n, 0))
                if i != C_TILE:
                    emptied(v, ("in", n, 1))
                first, count = (LAT0, SEQ) if i == C_TILE else (0, CONV_OUT)
                src, acc = conv_in[n % 2][:, first:], conv_acc[n % 2][:, first:first + count]
                if n >= 2:
                    v.wait_ge(tile_done, n - 1)
                    pr, pi = divmod(n - 2, 5)
                    if pi >= 2:
                        filled(v, ("T", pr, pi, 1))
                step(ts(acc, src[:, 0:count], cols_b[:, ct:ct + 1], cb_col[:, ct:ct + 1], ALU.mult, ALU.add))
                for k in range(1, CONV):
                    col = CONV_TILES * k + ct
                    ins = stt(acc, src[:, k:k + count], cols_b[:, col:col + 1], acc, ALU.mult, ALU.add)
                    if k < CONV - 1:
                        step(ins)
                ins.then_inc(conv_done, 1)

            def state_updates(g):
                for k in range(STEPS):
                    for d in range(2):
                        t = STEP_TILE[d][k]
                        dec = head_bc(decay[:, t, HEADS * d + HG * g:HEADS * d + HG * (g + 1)])
                        dst = hp[d][:, max(k - 1, 0)]
                        if k:
                            src = hp[d][:, max(k - 2, 0)]
                            v.wait_ge(state_ready, STEPS * g + k)
                            step(tt(heads(st_tmp[:, d]), heads(src), dec, ALU.mult))
                        b = filled(v, ("state", g, k, d))
                        if k:
                            ins = tt(dst, b[:, 0:GW], st_tmp[:, d], ALU.add)
                        else:
                            ins = cp(dst, b[:, 0:GW])
                        free(ins, ("state", g, k, d))
                    emptied(v, ("state", g, k, 0))
                    emptied(v, ("state", g, k, 1))
                    v.sem_inc(state_ready, 1)

            def unit_segments(u):
                g, ch = divmod(u, LT)
                v.wait_ge(seg_in[u % 2], 32 * (u // 2 + 1))
                for d in range(2):
                    col = HEADS * d + HG * g
                    ins = tt(seg[u % 2][:, d], seg[u % 2][:, d], head_bc(cum[:, CT + ch, col:col + HG], P),
                             ALU.subtract)
                ins.then_inc(seg_ready, 1)

            def unit_weights(u):
                g, ch = divmod(u, LT)
                v.wait_ge(decays, u + 1)
                b = filled(v, ("cb", u))
                for d in range(2):
                    ins = tt(seg[u % 2][:, d], seg[u % 2][:, d], b[:, 0:P].unsqueeze(1).to_broadcast([P, HG, P]),
                             ALU.mult)
                free(ins, ("cb", u))
                for d in range(2):
                    b = filled(v, ("off", u, d))
                    if u >= 2:
                        filled(v, ("y", u - 2))
                    col = HEADS * d + HG * g
                    free(tt(heads(yb[u % 2][:, d]), heads(b[:, 0:GW]), head_bc(ecum[:, CT + ch, col:col + HG]),
                            ALU.mult), ("off", u, d))

            def unit_gate(u):
                g, ch = divmod(u, LT)
                y = yb[u % 2][:, 0]
                v.wait_ge(offs_summed, u + 1)
                b = filled(v, ("diag", u))
                free(tt(y, y, b[:, 0:GW], ALU.add), ("diag", u))
                emptied(v, ("diag", u))
                emptied(v, ("zT", g, XT - 1))
                tt(y, y, zs[g % 2][:, ch], ALU.mult).then_inc(gated, 1)

            def unit_norm(u):
                v.wait_ge(rstd_y, u + 1)
                c_ = 16 + u % 2
                ts(yb[u % 2][:, 0], yb[u % 2][:, 0], stat[:, c_:c_ + 1], None, ALU.mult).then_inc(y_ready, 1)

            def mix_remainder(k):
                tile = (WO_ORDER[k] - FT) % 16
                v.wait_ge(mix_hi_ready, k + 1)
                if tile < YT:
                    for u in range(LT * (tile // XT), LT * (tile // XT + 1)):
                        emptied(v, ("y", u))
                else:
                    emptied(v, ("f", tile - YT))
                tt(mix_lo[:, tile], mixT[:, tile], whole(mix_hi[:, tile]), ALU.subtract).then_inc(mix_lo_ready, 1)

            def unfold(j):
                b = filled(v, ("f", j))
                f, even, odd = mixT[:, YT + j], b[:, 0:HALF + 1], b[:, HALF + 1:SEQ]
                step(cp(f[:, 0:HALF + 1:HALF], even[:, 0:HALF + 1:HALF]))
                step(cp(f[:, 1:HALF], odd))
                step(tt(f[:, SEQ - 1:HALF:-1], even[:, 1:HALF], f[:, 1:HALF], ALU.subtract))
                free(tt(f[:, 1:HALF], even[:, 1:HALF], f[:, 1:HALF], ALU.add), ("f", j))

            def wo_remainder(n):
                v.wait_ge(wo_hi_ready, n + 1)
                tt(wo_lo[n % WO_SLOTS], wo_buf[n % WO_SLOTS], whole(wo_hi[n % 2]), ALU.subtract
                   ).then_inc(wo_lo_ready, 1)

            for r in range(GROUPS + 1):
                g = r - 1
                for i in range(6):
                    if i == 0:
                        for q in split_ahead(r, i):
                            w_remainder(q)
                    if g >= 0 and i == 0:
                        if g == 0:
                            v.wait_ge(cum_out, 16)
                        else:
                            unit_norm(4 * g - 1)
                        unit_segments(4 * g)
                        state_updates(g)
                    elif g >= 0 and i >= 3:
                        unit_norm(4 * g + i - 3)
                    if i:
                        for q in split_ahead(r, i):
                            w_remainder(q)
                    elif 0 < r < GROUPS:
                        w_remainder(W_TILES * r + 2)
                    if r < GROUPS and i < 5:
                        conv(r, i)
                    if r == GROUPS and i == 0:
                        filled(v, ("T", GROUPS - 1, 4, 1))
                        v.memset(fw, 0.0).then_inc(fw_zero, 1)
                    elif r == GROUPS and i == 1:
                        b = filled(v, "fourier_w")
                        v.wait_ge(fw_zero, 1)
                        for s in range(2):
                            for h in range(2):
                                rows = slice(F_GROUP * h, F_GROUP * (h + 1))
                                src = b[rows, 256 * s:256 * (s + 1)].rearrange("p (j c) -> p j c", j=FT)
                                ins = cp(fw[rows, :, P * s + F_GROUP * h:P * s + F_GROUP * (h + 1)], src)
                        free(ins, "fourier_w")
                    if r == GROUPS and i == 2:
                        for t in range(LT):
                            b = filled(v, ("v", t, 1))
                            free(cp(vf[:, t, 2:4], b[:].rearrange("p (j c) -> p j c", j=2)), ("v", t, 1))
                    if r == 0 and i == 1:
                        dt_chain()
                    elif r == 0 and i == 2:
                        cumulative_sums()
                    elif r == 0 and i == 3:
                        sums_as_rows()
                        mod_evac("ada_b", slice(4, 8), 4)
                    elif r == 0 and i == 5:
                        mod_evac("ada_c", slice(8, 12), 4)
                    if r == GROUPS and i == 5:
                        wo_remainder(0)
                        wo_remainder(1)
                    if g >= 0:
                        if i >= 2:
                            unit_gate(4 * g + i - 2)
                        if 1 <= i <= 4:
                            unit_weights(4 * g + i - 1)
                            if i < 4:
                                unit_segments(4 * g + i)
                    if r == GROUPS and i >= 3:
                        for k in MIX_AT[i]:
                            mix_remainder(k)
                        if i > 3:
                            unfold(i - 4)
            unfold(2)
            unfold(3)
            unit_norm(UNITS - 1)

            for k in range(MIX_EARLY, 13):
                mix_remainder(k)
            wo_remainder(2)
            wo_remainder(3)
            for k in range(13, 16):
                mix_remainder(k)
            for n in range(4, 16):
                wo_remainder(n)

            v.wait_ge(res_in, 16 * LT)
            v.wait_ge(mod_bc_in, 16 * 4)
            step(stt(rowbc["scale2"], rowbc["scale2"], 1.0, norm2_bc, ALU.add, ALU.mult))

            def residual(t, halves=(0, 1)):
                for h in halves:
                    sl = slice(512 * h, 512 * (h + 1))
                    b = filled(v, ("out", t, h))
                    if t:
                        v.wait_ge(x1_ready, 2 * t + h - 1)
                    free(tt(out_tmp[:, h], b[:], rowbc["gate1"][:, sl], ALU.mult), ("out", t, h))
                    emptied(v, ("out", t, h))
                    tt(x1[:, t, sl], x1[:, t, sl], out_tmp[:, h], ALU.add).then_inc(x1_ready, 1)

            def scale_h2(t):
                v.wait_ge(rstd_x1, t + 1)
                step(stt(h2[:, t], x1[:, t], stat[:, t:t + 1], rowbc["scale2"], ALU.mult, ALU.mult))

            def shift_h2(t):
                tt(h2[:, t], h2[:, t], rowbc["shift2"], ALU.add).then_inc(h2_ready, 1)

            def copy_nT(t):
                b = filled(v, ("nT", t, 1))
                free(cp(nT[t % 2][:, 4:8], b[:].rearrange("p (k c) -> p k c", k=4)), ("nT", t, 1))

            for k in range(16):
                wo_remainder(16 + k)
                if k in (1, 2):
                    residual(0, (k - 1,))
                elif k in (6, 7):
                    residual(1, (k - 6,))
                elif k in (4, 9):
                    scale_h2(k // 9)
                elif k in (5, 10):
                    shift_h2(k // 10)
                elif k in (11, 14):
                    copy_nT(k // 14)
            residual(2)
            residual(3)
            for t in (2, 3):
                scale_h2(t)
                shift_h2(t)
            copy_nT(3)
            b = filled(v, "logits")
            logits = b[:, 0:LT * ROUTE_W].rearrange("p (t e) -> p t e", t=LT)[:, :, 0:EXPERTS]
            step(v.tensor_reduce(rowmax, logits, AX_X, ALU.max))
            free(tt(lg, logits, rowmax.unsqueeze(2).to_broadcast([P, LT, EXPERTS]), ALU.subtract), "logits")
            v.wait_ge(exped, 1)
            step(v.tensor_reduce(rowsum, probs, AX_X, ALU.add))
            step(v.reciprocal(rowsum, rowsum))
            tt(probs, probs, rowsum.unsqueeze(2).to_broadcast([P, LT, EXPERTS]), ALU.mult).then_inc(probs_ready, 1)
            b = filled(v, "probsT")
            free(cp(pT[0:EXPERTS], b[0:EXPERTS, :]), "probsT")
            emptied(v, "probsT")
            for _ in range(CAP // 8):
                step(v.max(top8[0:EXPERTS], pT[0:EXPERTS]))
                step(v.match_replace(pT[0:EXPERTS], top8[0:EXPERTS], pT[0:EXPERTS], -1.0))
            step(ts(mask[0:EXPERTS], pT[0:EXPERTS], 0.0, None, ALU.is_lt))
            step(v.tensor_tensor_scan(cums[0:EXPERTS], ones[0:EXPERTS, 0:1].to_broadcast([EXPERTS, SEQ]),
                                      mask[0:EXPERTS], 0.0, ALU.mult, ALU.add))
            tt(slot1[0:EXPERTS], cums[0:EXPERTS], mask[0:EXPERTS], ALU.mult).then_inc(slots_ready, 1)
            b = filled(v, "slotT")
            free(cp(slotT, b[:, 0:64].rearrange("p (t e) -> p t e", t=LT)), "slotT")
            emptied(v, "slotT")
            for b in range(8):
                v.wait_ge(bank_free[b], uses[b])
                v.sem_inc(e_free[b], 1)
            v.wait_ge(gate2_in, 16)
            with v.Fori(0, EXPERTS) as e:
                one = slotT[:, :, bass.ds(e, 1)].to_broadcast([P, LT, CAP])
                tt(sel, iota1.unsqueeze(1).to_broadcast([P, LT, CAP]), one, ALU.is_equal).then_inc(sel_ready, 1)
                v.wait_ge(sel_ready, e + 1)
                for h in range(2):
                    ins = tt(sel_w[:, :, h], sel, probs[:, :, bass.ds(e, 1)].to_broadcast([P, LT, CAP]), ALU.mult)
                ins.then_inc(selw_ready, 1)
                v.wait_ge(e_full[4], e + 1)
                cp(xgT, bank[4][:].rearrange("p (k c) -> p k c", k=KT)).then_inc(e_free[4], 1)
                v.wait_ge(e_full[3], 2 * e + 1)
                for n in range(2):
                    v.wait_ge(silu_ready, 2 * e + n + 1)
                    tt(act_e[:, 512 * n:512 * (n + 1)], silu_g[:, 512 * n:512 * (n + 1)], bank[2 + n][:], ALU.mult
                       ).then_inc(act_ready, 1)
                v.wait_ge(e_full[5], 2 * e + 2)
                tt(y_e[:, 0:512], bank[4][:], gate2[:, 0:512], ALU.mult).then_inc(e_free[4], 1)
                tt(y_e[:, 512:1024], bank[5][:], gate2[:, 512:1024], ALU.mult).then_inc(e_free[5], 1)
                for i in range(8):
                    t, n = divmod(i, 2)
                    b = (6, 7, 0, 1, 2, 3, 6, 7)[i]
                    if b >= 6:
                        v.wait_ge(e_full[b], 3 * e + 2 + i // 6)
                    elif b in (1, 3):
                        v.wait_ge(e_full[b], 2 * e + 2)
                    else:
                        v.wait_ge(e_full[b], e + 1)
                    sl = slice(512 * n, 512 * (n + 1))
                    tt(x1[:, t, sl], x1[:, t, sl], bank[b][:], ALU.add).then_inc(e_free[b], 1)
            v.wait_ge(final_in, 16)
            for t in range(LT):
                v.wait_ge(rstd_x2, t + 1)
                stt(out_rows[:, t], x1[:, t], stat[:, t:t + 1], final_bc, ALU.mult, ALU.mult).then_inc(out_ready, 1)

        @block.scalar
        def _(act):
            ac = act.activation

            for t in range(TT):
                act.wait_ge(ctx_in if t < CT else lat_in, 16)
                ac(hT.rearrange("p k t -> p (k t)")[:, D * t:D * (t + 1)], x_raw[:, t], ACT.Square,
                   accum_out=stat[:, 8 + t:9 + t]).then_inc(square_done, 1)
            act.wait_ge(square_done, TT)
            emptied(act, "columns")
            ac(scT, cols_a[:, 40:56], ACT.Silu).then_inc(silu_c, 1)
            for k in range(KT):
                b = filled(act, ("xT", k, 0))
                free(ac(hT[:, k, CTX:TOK], b[:], ACT.Copy), ("xT", k, 0))

            def round_w(q):
                slot, n = raw_slot(q)
                act.wait_ge(w_in_sem[slot], 16 * n)
                if q >= 2:
                    weights_used(act, q - 2)
                ac(w_hi[q % 2], w_raw[slot], ACT.Copy).then_inc(w_hi_ready, 1)

            round_w(0)
            for k in range(KT):
                act.wait_ge(modulated, 2 * k + 1)
                ac(hi_lat[k // FT][:, k % FT], hT[:, k, CTX:TOK], ACT.Copy).then_inc(h_hi_ready, 1)
                act.wait_ge(modulated, 2 * k + 2)
                ac(hi_ctx[:, k], hT[:, k, 0:CTX], ACT.Copy).then_inc(h_hi_ready, 1)
            act.wait_ge(w_dt_in, 16)
            ac(w_dt_hi, w_dt, ACT.Copy).then_inc(dt_w_hi, 1)

            def evac_in(r, i):
                n = 5 * r + i
                if n >= 2:
                    act.wait_ge(conv_done, n - 1)
                if n < 2:
                    act.wait_ge(pads_zero, 1)
                b = filled(act, ("in", n, 0))
                free(ac(conv_in[n % 2][:, PAD + LAT0:PAD + LAT0 + SEQ], b[:], ACT.Copy), ("in", n, 0))
                if i == C_TILE:
                    return
                b = filled(act, ("in", n, 1))
                free(ac(conv_in[n % 2][:, PAD:PAD + CTX], b[:, 0:CTX], ACT.Copy), ("in", n, 1))

            def silu_tile(r, i):
                n = 5 * r + i
                act.wait_ge(conv_done, n + 1)
                dst = bc_ch[r % 2][i] if i < 2 else conv_acc[n % 2]
                first = LAT0 if i == C_TILE else 0
                ac(dst[:, first:], conv_acc[n % 2][:, first:], ACT.Silu).then_inc(tile_done, 1)

            def evac_tokens(r, s):
                o = 0 if s == 0 else P * (s - 1)
                for part, (t0, m) in enumerate(((CT, LT), (0, CT))):
                    b = filled(act, ("T", r, s, part))
                    free(ac(tok[r % 2][:, t0:t0 + m, o:o + P], b[:, 0:P * m].rearrange("p (t c) -> p t c", t=m),
                            ACT.Copy), ("T", r, s, part))

            def dt_chain():
                act.wait_ge(exp_small, 1)
                ac(dtmp[1], dtmp[1], ACT.Exp, scale=-1.0).then_inc(small_exped, 1)
                ac(abc, abc, ACT.Exp).then_inc(small_exped, 1)
                act.wait_ge(exp_small, 2)
                ac(dt, cum, ACT.Ln).then_inc(small_exped, 1)

            def exp_of_sums():
                act.wait_ge(exp_small, 3)
                ac(toend, dtmp[2], ACT.Exp).then_inc(small_exped, 1)
                ac(decay, dtmp[1], ACT.Exp).then_inc(small_exped, 1)
                ac(ecum, cum, ACT.Exp).then_inc(small_exped, 1)

            def unit_exp(u):
                act.wait_ge(masked, u + 1)
                w = seg[u % 2].rearrange("p d h l -> p (d h l)")
                ac(w, w, ACT.Exp).then_inc(decays, 1)

            def unit_square(u):
                act.wait_ge(gated, u + 1)
                act.wait_ge(offs_summed, u + 1)
                ac(yb[u % 2][:, 1], yb[u % 2][:, 0], ACT.Square, accum_out=stat[:, 18 + u % 2:19 + u % 2]
                   ).then_inc(squared, 1)

            def unit_evac(u):
                g, ch = divmod(u, LT)
                if u == 0:
                    act.wait_ge(mod_out, 16)
                b = filled(act, ("y", u))
                for j in range(XT):
                    ins = ac(yT[:, XT * g + j, P * ch:P * (ch + 1)], b[:, P * j:P * (j + 1)], ACT.Identity,
                             bias=0.0, scale=ssm_col[:, XT * g + j:XT * g + j + 1])
                free(ins, ("y", u))

            def round_mix(k):
                tile = (WO_ORDER[k] - FT) % 16
                if tile < YT:
                    for u in range(LT * (tile // XT), LT * (tile // XT + 1)):
                        emptied(act, ("y", u))
                else:
                    emptied(act, ("f", tile - YT))
                ac(mix_hi[:, tile], mixT[:, tile], ACT.Copy).then_inc(mix_hi_ready, 1)

            def round_wo(n):
                act.wait_ge(wo_in[n % WO_SLOTS], 16 * (n // WO_SLOTS + 1))
                m = n - 2
                if m >= 0 and m % 16 == 15:
                    filled(act, ("out", 2 * (m // 16) + 1, 1))
                elif m >= 0:
                    act.wait_ge(wo_used, m + 1 - m // 16)
                ac(wo_hi[n % 2], wo_buf[n % WO_SLOTS], ACT.Copy).then_inc(wo_hi_ready, 1)

            def silu_z(r, c_):
                b = filled(act, ("zT", r, c_))
                free(ac(zs[r % 2][:, :, P * c_:P * (c_ + 1)], b[:].rearrange("p (t c) -> p t c", t=LT), ACT.Silu),
                     ("zT", r, c_))

            for r in range(GROUPS + 1):
                g = r - 1
                for i in range(6):
                    for c_, q in enumerate(slot_tiles(r, i)):
                        if q + 1 in split_ahead(r, i):
                            round_w(q + 1)
                        if r < GROUPS and i == 5:
                            act.wait_ge(conv_done, 5 * r + 5)
                            b = filled(act, ("z", r, c_))
                            free(ac(z_ch[(5 * r + 5 + c_) % 2], b[:], ACT.Copy), ("z", r, c_))
                            if c_:
                                silu_z(r, c_ - 1)
                        elif r == GROUPS:
                            j = q - W_TILES * GROUPS
                            b = filled(act, ("u", j))
                            free(ac(uT[:, j], b[:], ACT.Copy), ("u", j))
                    if r < GROUPS and i < 5:
                        evac_in(r, i)
                    elif r == GROUPS and i == 2:
                        for t in range(LT):
                            b = filled(act, ("v", t, 0))
                            free(ac(vf[:, t, 0:2], b[:].rearrange("p (j c) -> p j c", j=2), ACT.Copy), ("v", t, 0))
                    if r < GROUPS and i in TOKENS_AT:
                        evac_tokens(r, TOKENS_AT[i])
                    if r < GROUPS and i == 5:
                        silu_z(r, XT - 1)
                    if g > 0 and i == 0:
                        unit_evac(4 * g - 1)
                    if g >= 0 and i >= 3:
                        unit_evac(4 * g + i - 3)
                    if g >= 0 and 1 <= i <= 4:
                        unit_exp(4 * g + i - 1)
                    if 0 < r < GROUPS and i == 0:
                        round_w(W_TILES * r + 2)
                    if r < GROUPS and i < 5:
                        silu_tile(r, i)
                    if r == 0 and i == 0:
                        b = filled(act, "dtT")
                        free(ac(dt_rows[0:DT_W, CTX:TOK], b[0:DT_W, :], ACT.Copy), "dtT")
                        b = filled(act, "dtT_ctx")
                        free(ac(dt_rows[0:DT_W, 0:CTX], b[0:DT_W, 0:CTX], ACT.Copy), "dtT_ctx")
                    elif r == 0 and i == 1:
                        dt_chain()
                    elif r == 0 and i == 2:
                        exp_of_sums()
                    if r == GROUPS and i == 5:
                        round_wo(0)
                        round_wo(1)
                    if g >= 0 and i >= 2:
                        unit_square(4 * g + i - 2)
                    if r == GROUPS and i >= 3:
                        if i == 3:
                            act.wait_ge(xdt_ready, UNITS - LT)
                            filled(act, ("diag", UNITS - LT - 1))
                            filled(act, "fourier_w")
                        for k in MIX_AT[i]:
                            round_mix(k)

            act.wait_ge(xdt_ready, UNITS)
            filled(act, ("off", UNITS - 1, 1))
            for k in range(MIX_EARLY, 13):
                round_mix(k)
            round_wo(2)
            round_wo(3)
            unit_evac(UNITS - 1)
            for k in range(13, 16):
                round_mix(k)
            for n in range(4, 16):
                round_wo(n)

            def square_x1(t):
                act.wait_ge(x1_ready, 2 * t + 2)
                ac(h2[:, t], x1[:, t], ACT.Square, accum_out=stat[:, 8 + t:9 + t]).then_inc(x1_squared, 1)

            def copy_nT(t, h):
                b = filled(act, ("nT", t, h))
                free(ac(nT[t % 2][:, 4 * h:4 * h + 4], b[:].rearrange("p (k c) -> p k c", k=4), ACT.Copy),
                     ("nT", t, h))

            for k in range(16):
                round_wo(16 + k)
                if k in (3, 8):
                    square_x1(k // 8)
                elif k in (11, 14):
                    copy_nT(k // 14, 0)
            square_x1(2)
            square_x1(3)
            copy_nT(2, 0)
            copy_nT(2, 1)
            copy_nT(3, 0)
            emptied(act, "logits")
            ac(probs, lg, ACT.Exp).then_inc(exped, 1)
            with act.Fori(0, EXPERTS) as e:
                act.wait_ge(e_full[5], 2 * e + 1)
                ac(scatter, bank[5][:], ACT.Copy).then_inc(e_free[5], 1)
                act.wait_ge(e_full[1], 2 * e + 1)
                for n in range(2):
                    ac(silu_g[:, 512 * n:512 * (n + 1)], bank[n][:], ACT.Silu).then_inc(silu_ready, 1)
                for n in range(2):
                    act.wait_ge(e_full[6 + n], 3 * e + 1)
                    ac(actT[:, 512 * n:512 * (n + 1)], bank[6 + n][:], ACT.Copy).then_inc(e_free[6 + n], 1)
            for t, (b, n) in enumerate(((6, 3 * EXPERTS), (0, EXPERTS + 1), (2, EXPERTS + 1), (6, 3 * EXPERTS + 1))):
                act.wait_ge(e_free[b], n)
                act.wait_ge(e_free[b + 1], n)
                ac(out_rows[:, t], x1[:, t], ACT.Square, accum_out=stat[:, 8 + t:9 + t]).then_inc(x2_squared, 1)

        @block.gpsimd
        def _(gp):
            step = Chain(gp, pool_step)
            tt = gp.tensor_tensor

            def state_inputs(g):
                for s in (0, 2, 3, 4):
                    emptied(gp, ("T", g, s, 0))
                    emptied(gp, ("T", g, s, 1))
                for k in range(STEPS):
                    if k >= 2:
                        filled(gp, ("state", g, k - 2, 1))
                    for d in range(2):
                        t = STEP_TILE[d][k]
                        col = HEADS * d + HG * g
                        ins = tt(heads(xw[:, k % 2, d]), heads(tok[g % 2][:, t, P:]), head_bc(toend[:, t, col:col + HG]),
                                 ALU.mult)
                    ins.then_inc(xw_ready, 1)

            def unit_inputs(u):
                g, ch = divmod(u, LT)
                if u >= 2:
                    filled(gp, ("diag", u - 2))
                xs = heads(tok[g % 2][:, CT + ch, P:])
                tt(heads(xd[u % 2]), xs, head_bc(dbc[:, HG * g:HG * (g + 1)]), ALU.mult)
                for d in range(2):
                    col = HEADS * d + HG * g
                    ins = tt(heads(xdt[u % 2][:, d]), xs, head_bc(dt[:, CT + ch, col:col + HG]), ALU.mult)
                ins.then_inc(xdt_ready, 1)

            def unit_mask(u):
                gp.wait_ge(seg_ready, u + 1)
                for d, sign in ((0, 1), (1, -1)):
                    ins = gp.affine_select(out=seg[u % 2][:, d], in_=seg[u % 2][:, d], compare_op=ALU.is_ge,
                                           fill=MASKED, base=0, pattern=[[0, HG], [sign, P]],
                                           channel_multiplier=-sign)
                ins.then_inc(masked, 1)

            def unit_sum(u):
                emptied(gp, ("off", u, 0))
                emptied(gp, ("off", u, 1))
                gp.wait_ge(xdt_ready, u + 1)
                y = yb[u % 2]
                step(tt(y[:, 0], y[:, 0], y[:, 1], ALU.add))
                tt(y[:, 0], y[:, 0], xd[u % 2], ALU.add).then_inc(offs_summed, 1)

            def rstd(dst, src, width, ready):
                step(gp.tensor_scalar(dst, src, 1.0 / width, EPS, ALU.mult, ALU.add))
                tt(dst, dst, stat[:, 28:29], ALU.pow).then_inc(ready, 1)

            def unit_rstd(u):
                gp.wait_ge(squared, u + 1)
                c_ = 16 + u % 2
                rstd(stat[:, c_:c_ + 1], stat[:, c_ + 2:c_ + 3], GW, rstd_y)

            def row_rstd(squares, ready, n):
                for t in range(n):
                    gp.wait_ge(squares, t + 1)
                    rstd(stat[:, t:t + 1], stat[:, 8 + t:9 + t], D, ready)

            step(gp.memset(stat[:, 28:29], -0.5))
            row_rstd(square_done, rstd_x, TT)
            gp.wait_ge(rows_ready, 1)
            gp.dma_start(cum_dram, cum_rows[0:48, :]).then_inc(cum_out, 16)
            emptied(gp, "ada_c")
            emptied(gp, "ada_b")
            gp.dma_start(mod_dram[4:12].rearrange("m j c -> j m c"),
                         mod_rows[0:P:32, 4 * P:12 * P].rearrange("p (m c) -> p m c", c=P)).then_inc(mod_out, 16)
            gp.wait_ge(cum_ready, 1)
            gp.wait_ge(cum_out, 16)
            for g in range(GROUPS):
                if g:
                    unit_rstd(4 * g - 1)
                state_inputs(g)
                unit_inputs(4 * g)
                unit_mask(4 * g)
                for ch in range(LT):
                    u = 4 * g + ch
                    if ch:
                        unit_rstd(u - 1)
                    unit_sum(u)
                    if ch < LT - 1:
                        unit_inputs(u + 1)
                        unit_mask(u + 1)
            unit_rstd(UNITS - 1)
            row_rstd(x1_squared, rstd_x1, LT)
            row_rstd(x2_squared, rstd_x2, LT)


_INS = ['x', 'c', 'ctx', 'c_ctx', 'w_ada', 'b_ada', 'norm1_w', 'w_in', 'conv_w', 'conv_b', 'dt_bias', 'a_log',
        'd_skip', 'ssm_norm_w', 'w_fourier', 'w_out', 'norm2_w', 'w_router', 'w_gate', 'w_up', 'w_down',
        'final_norm_w']


def kernel(**inputs):
    import numpy as _np
    import concourse.bacc as _bacc
    from concourse import mybir as _mybir
    from concourse.bass_utils import run_bass_kernel_spmd as _run

    nc = _bacc.Bacc("TRN2", target_bir_lowering=False, num_devices=1)
    consts, dft = host_constants()
    arrays, args = {}, []
    for name, a in [("consts", consts), ("dft", dft)] + [(n, _np.ascontiguousarray(inputs[n])) for n in _INS]:
        arrays[f"in_{name}_dram"] = a
        args.append(nc.dram_tensor(f"in_{name}_dram", a.shape, _mybir.dt.from_np(a.dtype), kind="ExternalInput").ap())
    args.append(nc.dram_tensor("out_0_dram", (1, SEQ, D), F32, kind="ExternalOutput").ap())
    build(nc, *args)
    r = _run(nc, [arrays], core_ids=[0])
    return r.results[0]["out_0_dram"]
```
